# Optimizing a Trainium2 kernel written in Bass

```python
import math
import jax, jax.numpy as jnp
from jax import lax
import numpy as np

D_MODEL = 1024
BATCH = 1
SEQ = 256
DEPTH = 2
DEC_BATCH = 8
DEC_SEQ = 8
PAST_LEN = 2048
PAGE_SIZE = 128

HEAD_DIM = 128
DN_HEADS = 4
MOBA_HEADS = 4
DN_WIDTH = DN_HEADS * HEAD_DIM
MOBA_WIDTH = MOBA_HEADS * HEAD_DIM
MIX_WIDTH = DN_WIDTH + MOBA_WIDTH
DN_CONV = 4
DN_CHUNK = 64
MOBA_BLOCK = 256
MOBA_TOPK = 3
MOBA_QCHUNK = 32
SC_CONV = 3
FFN_CONV = 3
D_FF = 2816
N_ATT_LAYERS = (DEPTH + 1) // 2
N_CONV_LAYERS = DEPTH // 2
OFF_DN_QKV = 0
OFF_DN_Z = 3 * DN_WIDTH
OFF_DN_BETA = OFF_DN_Z + DN_WIDTH
OFF_DN_A = OFF_DN_BETA + DN_HEADS
OFF_MB_QKV = OFF_DN_A + DN_HEADS
IN_MIX_WIDTH = OFF_MB_QKV + 3 * MOBA_WIDTH
DEEPNORM_ALPHA = (2.0 * DEPTH) ** 0.25
DEEPNORM_BETA = (8.0 * DEPTH) ** -0.25
LN_EPS = 1e-5
NORM_EPS = 1e-6
NEG_INF = -1e30

kernel_name = "hybrid_gdn_moba_shortconv_step"

def layer_norm(x, g, b):
    xf = x.astype(jnp.float32)
    mu = jnp.mean(xf, -1, keepdims=True)
    var = jnp.mean(jnp.square(xf - mu), -1, keepdims=True)
    return ((xf - mu) * lax.rsqrt(var + LN_EPS) * g.astype(jnp.float32) + b.astype(jnp.float32)).astype(x.dtype)

def rms_norm(x):
    xf = x.astype(jnp.float32)
    return xf * lax.rsqrt(jnp.mean(jnp.square(xf), -1, keepdims=True) + NORM_EPS)

def l2_norm(x):
    xf = x.astype(jnp.float32)
    return xf * lax.rsqrt(jnp.sum(jnp.square(xf), -1, keepdims=True) + NORM_EPS)

def causal_dwconv(x, w, buf):
    width = w.shape[0]
    t = x.shape[1]
    xp = jnp.concatenate([buf.astype(x.dtype), x], axis=1)
    y = xp[:, 0:t] * w[0]
    for i in range(1, width):
        y = y + xp[:, i:i + t] * w[i]
    return y, xp[:, t:]

def gated_delta_rule(q, k, v, g, beta, s0):
    bsz, t, h, _ = q.shape
    c = min(DN_CHUNK, t)
    n = -(-t // c)
    pad = n * c - t

    def chunks(a):
        a = jnp.pad(a, ((0, 0), (0, pad)) + ((0, 0),) * (a.ndim - 2))
        a = a.reshape((bsz, n, c) + a.shape[2:])
        return jnp.moveaxis(a, (1, 3), (0, 2))

    qc, kc, vc, gc, bc = (chunks(a) for a in (q, k, v, g, beta))
    incl = jnp.tril(jnp.ones((c, c), bool))
    strict = jnp.tril(jnp.ones((c, c), bool), -1)
    eye = jnp.eye(c, dtype=jnp.float32)

    def step(s, inp):
        qi, ki, vi, gi, bi = inp
        gcum = jnp.cumsum(gi, -1)
        diff = gcum[..., :, None] - gcum[..., None, :]
        decay = jnp.where(incl, jnp.exp(jnp.where(incl, diff, 0.0)), 0.0)
        kb = ki * bi[..., None]
        lower = jnp.where(strict, jnp.einsum('bhid,bhjd->bhij', kb, ki) * decay, 0.0)
        tmat = lax.linalg.triangular_solve(eye + lower, jnp.broadcast_to(eye, lower.shape),
                                           left_side=True, lower=True, unit_diagonal=True)
        u = tmat @ (vi * bi[..., None])
        w = tmat @ (kb * jnp.exp(gcum)[..., None])
        v_new = u - w @ s
        intra = jnp.einsum('bhid,bhjd->bhij', qi, ki) * decay
        out = (qi * jnp.exp(gcum)[..., None]) @ s + intra @ v_new
        g_last = gcum[..., -1:]
        s = s * jnp.exp(g_last)[..., None] + jnp.einsum('bhcd,bhce->bhde', ki * jnp.exp(g_last - gcum)[..., None], v_new)
        return s, out

    s, out = lax.scan(step, s0, (qc, kc, vc, gc, bc))
    out = jnp.moveaxis(out, (0, 2), (1, 3)).reshape(bsz, n * c, h, -1)[:, :t]
    return out, s

def moba_attend(q, k_all, v_all, pos0):
    bsz, t, h, dh = q.shape
    length = k_all.shape[1]
    nb = -(-length // MOBA_BLOCK)
    pad = nb * MOBA_BLOCK - length
    kp = jnp.pad(k_all, ((0, 0), (0, pad), (0, 0), (0, 0)))
    vp = jnp.pad(v_all, ((0, 0), (0, pad), (0, 0), (0, 0)))
    kb = jnp.moveaxis(kp.reshape(bsz, nb, MOBA_BLOCK, h, dh), 3, 1)
    vb = jnp.moveaxis(vp.reshape(bsz, nb, MOBA_BLOCK, h, dh), 3, 1)
    k_mean = jnp.mean(kb.astype(jnp.float32), axis=3)
    qh = jnp.moveaxis(q, 2, 1)
    q_pos = pos0 + jnp.arange(t)
    own = q_pos // MOBA_BLOCK
    gate = jnp.einsum('bhtd,bhnd->bhtn', qh.astype(jnp.float32), k_mean)
    gate = jnp.where(jnp.arange(nb)[None, :] < own[:, None], gate, NEG_INF)
    n_sel = min(MOBA_TOPK, nb)
    _, sel = lax.top_k(gate, n_sel)
    sel_ok = jnp.arange(n_sel)[None, :] < own[:, None]
    blocks = jnp.concatenate([sel.astype(jnp.int32),
                              jnp.broadcast_to(own.astype(jnp.int32)[None, None, :, None], (bsz, h, t, 1))], -1)
    ok = jnp.concatenate([sel_ok, jnp.ones((t, 1), bool)], -1)
    r = n_sel + 1
    qc = math.gcd(t, MOBA_QCHUNK)
    nq = t // qc
    qs = jnp.moveaxis(qh.reshape(bsz, h, nq, qc, dh), 2, 0)
    bs = jnp.moveaxis(blocks.reshape(bsz, h, nq, qc, r), 2, 0)
    ps = q_pos.reshape(nq, qc)
    oks = ok.reshape(nq, qc, r)
    kflat = kb.reshape(bsz, h, nb, MOBA_BLOCK * dh)
    vflat = vb.reshape(bsz, h, nb, MOBA_BLOCK * dh)
    slopes = jnp.asarray(2.0 ** (-8.0 * np.arange(1, h + 1) / h), jnp.float32)
    scale = dh ** -0.5

    def attend(args):
        qi, bi, pi, oki = args
        idx = bi.reshape(bsz, h, qc * r, 1)
        kg = jnp.take_along_axis(kflat, idx, axis=2).reshape(bsz, h, qc, r, MOBA_BLOCK, dh)
        vg = jnp.take_along_axis(vflat, idx, axis=2).reshape(bsz, h, qc, r, MOBA_BLOCK, dh)
        s_pos = bi[..., None] * MOBA_BLOCK + jnp.arange(MOBA_BLOCK)
        dist = pi[:, None, None] - s_pos
        allowed = oki[:, :, None] & (dist >= 0)
        logits = (jnp.einsum('bhqd,bhqrsd->bhqrs', qi.astype(jnp.float32), kg.astype(jnp.float32)) * scale
                  - slopes[:, None, None, None] * dist.astype(jnp.float32))
        logits = jnp.where(allowed, logits, NEG_INF)
        p = jax.nn.softmax(logits.reshape(bsz, h, qc, r * MOBA_BLOCK), axis=-1).reshape(logits.shape)
        return jnp.einsum('bhqrs,bhqrsd->bhqd', p, vg.astype(jnp.float32)).astype(q.dtype)

    out = lax.map(attend, (qs, bs, ps, oks))
    out = jnp.moveaxis(out, 0, 2).reshape(bsz, h, t, dh)
    return jnp.moveaxis(out, 1, 2).reshape(bsz, t, h * dh)

def mix_even(x, pos0, past_kv, s0, conv0, w_in, conv_w, a_log, dt_bias, norm_w, w_out):
    bsz, t, _ = x.shape
    hcat = x @ w_in
    dn_qkv = hcat[..., OFF_DN_QKV:OFF_DN_Z]
    dn_z = hcat[..., OFF_DN_Z:OFF_DN_BETA]
    dn_b = hcat[..., OFF_DN_BETA:OFF_DN_A]
    dn_a = hcat[..., OFF_DN_A:OFF_MB_QKV]
    mb_qkv = hcat[..., OFF_MB_QKV:].reshape(bsz, t, 3, MOBA_HEADS, HEAD_DIM)
    qkv, conv_new = causal_dwconv(dn_qkv, conv_w, conv0)
    qkv = jax.nn.silu(qkv).reshape(bsz, t, 3, DN_HEADS, HEAD_DIM)
    q = l2_norm(qkv[:, :, 0]) * HEAD_DIM ** -0.5
    k = l2_norm(qkv[:, :, 1])
    v = qkv[:, :, 2].astype(jnp.float32)
    beta = jax.nn.sigmoid(dn_b.astype(jnp.float32))
    g = -jnp.exp(a_log.astype(jnp.float32)) * jax.nn.softplus(dn_a.astype(jnp.float32) + dt_bias.astype(jnp.float32))
    o_dn, s = gated_delta_rule(q, k, v, g, beta, s0.astype(jnp.float32))
    o_dn = rms_norm(o_dn) * norm_w.astype(jnp.float32) * jax.nn.silu(dn_z.reshape(bsz, t, DN_HEADS, HEAD_DIM).astype(jnp.float32))
    o_dn = o_dn.reshape(bsz, t, DN_WIDTH).astype(x.dtype)
    mq, mk, mv = mb_qkv[:, :, 0], mb_qkv[:, :, 1], mb_qkv[:, :, 2]
    if past_kv is None:
        k_all, v_all = mk, mv
    else:
        k_all = jnp.concatenate([past_kv[0].astype(mk.dtype), mk], axis=1)
        v_all = jnp.concatenate([past_kv[1].astype(mv.dtype), mv], axis=1)
    o_mb = moba_attend(mq, k_all, v_all, pos0)
    y = jnp.concatenate([o_dn, o_mb], axis=-1) @ w_out
    return y, s.astype(x.dtype), conv_new, mk, mv

def shortconv_mix(x, w_in, conv_w, buf, w_out):
    gate_b, gate_c, xh = jnp.split(x @ w_in, 3, axis=-1)
    u, buf_new = causal_dwconv(gate_c * xh, conv_w, buf)
    return (gate_b * u) @ w_out, buf_new

def conv_ffn(x, w_up, conv_w, buf, w_down):
    u, gt = jnp.split(x @ w_up, 2, axis=-1)
    uc, buf_new = causal_dwconv(u, conv_w, buf)
    return (jax.nn.gelu(uc, approximate=False) * gt) @ w_down, buf_new

def trunk(x, pos0, past_kv, dn_s0, dn_c0, sc_c0, ffn_c0, w_in_mix, dn_conv_w, dn_a_log, dn_dt_bias, dn_norm_w,
          w_out_mix, w_in_sc, sc_conv_w, w_out_sc, ln_mix_g, ln_mix_b, w_up, ffn_conv_w, w_down, ln_ffn_g, ln_ffn_b):
    ks, vs, dns, dncs, sccs, ffcs = [], [], [], [], [], []
    for layer in range(DEPTH):
        i = layer // 2
        if layer % 2 == 0:
            y, s, dnc, k_new, v_new = mix_even(x, pos0, past_kv(i), dn_s0[i], dn_c0[i], w_in_mix[i], dn_conv_w[i],
                                               dn_a_log[i], dn_dt_bias[i], dn_norm_w[i], w_out_mix[i])
            ks.append(k_new)
            vs.append(v_new)
            dns.append(s)
            dncs.append(dnc)
        else:
            y, scc = shortconv_mix(x, w_in_sc[i], sc_conv_w[i], sc_c0[i], w_out_sc[i])
            sccs.append(scc)
        x = layer_norm(DEEPNORM_ALPHA * x + y, ln_mix_g[layer], ln_mix_b[layer])
        y, ffc = conv_ffn(x, w_up[layer], ffn_conv_w[layer], ffn_c0[layer], w_down[layer])
        ffcs.append(ffc)
        x = layer_norm(DEEPNORM_ALPHA * x + y, ln_ffn_g[layer], ln_ffn_b[layer])
    return x, jnp.stack(ks), jnp.stack(vs), jnp.stack(dns), jnp.stack(dncs), jnp.stack(sccs), jnp.stack(ffcs)

def setup_inputs(seed: int = 0) -> dict:
    key = jax.random.key(seed)
    keys = iter(jax.random.split(key, 32))

    def nrm(shape, scale=1.0):
        return jax.random.normal(next(keys), shape, jnp.float32) * scale

    n_pages = PAST_LEN // PAGE_SIZE
    n_used = DEC_BATCH * n_pages
    n_pool = n_used + max(1, n_used // 4)
    kv_shape = (N_ATT_LAYERS, n_pool, PAGE_SIZE, MOBA_HEADS, HEAD_DIM)
    page_table = jax.random.permutation(next(keys), n_pool)[:n_used].reshape(DEC_BATCH, n_pages).astype(jnp.int32)
    dt = jnp.exp(jax.random.uniform(next(keys), (N_ATT_LAYERS, DN_HEADS), jnp.float32, math.log(1e-3), math.log(1e-1)))
    return {
        "x_prompt": nrm((BATCH, SEQ, D_MODEL)),
        "x_sample": nrm((DEC_BATCH, DEC_SEQ, D_MODEL)),
        "cache_k": nrm(kv_shape),
        "cache_v": nrm(kv_shape),
        "state_dn": nrm((N_ATT_LAYERS, DEC_BATCH, DN_HEADS, HEAD_DIM, HEAD_DIM), 0.1),
        "state_dn_conv": nrm((N_ATT_LAYERS, DEC_BATCH, DN_CONV - 1, 3 * DN_WIDTH)),
        "state_sc_conv": nrm((N_CONV_LAYERS, DEC_BATCH, SC_CONV - 1, D_MODEL)),
        "state_ffn_conv": nrm((DEPTH, DEC_BATCH, FFN_CONV - 1, D_FF)),
        "page_table": page_table,
        "w_in_mix": nrm((N_ATT_LAYERS, D_MODEL, IN_MIX_WIDTH), D_MODEL ** -0.5),
        "dn_conv_w": nrm((N_ATT_LAYERS, DN_CONV, 3 * DN_WIDTH), DN_CONV ** -0.5),
        "dn_a_log": jnp.log(jax.random.uniform(next(keys), (N_ATT_LAYERS, DN_HEADS), jnp.float32, 1.0, 16.0)),
        "dn_dt_bias": dt + jnp.log(-jnp.expm1(-dt)),
        "dn_norm_w": 1.0 + nrm((N_ATT_LAYERS, HEAD_DIM), 0.02),
        "w_out_mix": nrm((N_ATT_LAYERS, MIX_WIDTH, D_MODEL), DEEPNORM_BETA * MIX_WIDTH ** -0.5),
        "w_in_sc": nrm((N_CONV_LAYERS, D_MODEL, 3 * D_MODEL), D_MODEL ** -0.5),
        "sc_conv_w": nrm((N_CONV_LAYERS, SC_CONV, D_MODEL), SC_CONV ** -0.5),
        "w_out_sc": nrm((N_CONV_LAYERS, D_MODEL, D_MODEL), DEEPNORM_BETA * D_MODEL ** -0.5),
        "ln_mix_g": 1.0 + nrm((DEPTH, D_MODEL), 0.02),
        "ln_mix_b": nrm((DEPTH, D_MODEL), 0.02),
        "w_up": nrm((DEPTH, D_MODEL, 2 * D_FF), D_MODEL ** -0.5),
        "ffn_conv_w": nrm((DEPTH, FFN_CONV, D_FF), FFN_CONV ** -0.5),
        "w_down": nrm((DEPTH, D_FF, D_MODEL), DEEPNORM_BETA * D_FF ** -0.5),
        "ln_ffn_g": 1.0 + nrm((DEPTH, D_MODEL), 0.02),
        "ln_ffn_b": nrm((DEPTH, D_MODEL), 0.02),
    }

def reference(x_prompt, x_sample, cache_k, cache_v, state_dn, state_dn_conv, state_sc_conv, state_ffn_conv, page_table,
              w_in_mix, dn_conv_w, dn_a_log, dn_dt_bias, dn_norm_w, w_out_mix, w_in_sc, sc_conv_w, w_out_sc,
              ln_mix_g, ln_mix_b, w_up, ffn_conv_w, w_down, ln_ffn_g, ln_ffn_b):
    bp = x_prompt.shape[0]
    dt = x_prompt.dtype
    dn0 = jnp.zeros((N_ATT_LAYERS, bp, DN_HEADS, HEAD_DIM, HEAD_DIM), dt)
    dnc0 = jnp.zeros((N_ATT_LAYERS, bp, DN_CONV - 1, 3 * DN_WIDTH), dt)
    scc0 = jnp.zeros((N_CONV_LAYERS, bp, SC_CONV - 1, D_MODEL), dt)
    ffc0 = jnp.zeros((DEPTH, bp, FFN_CONV - 1, D_FF), dt)
    y_prompt, k_p, v_p, dn_p, dnc_p, scc_p, ffc_p = trunk(
        x_prompt, 0, lambda i: None, dn0, dnc0, scc0, ffc0, w_in_mix, dn_conv_w, dn_a_log, dn_dt_bias, dn_norm_w,
        w_out_mix, w_in_sc, sc_conv_w, w_out_sc, ln_mix_g, ln_mix_b, w_up, ffn_conv_w, w_down, ln_ffn_g, ln_ffn_b)
    db, n_pages = page_table.shape
    past_len = n_pages * PAGE_SIZE

    def past_kv(i):
        kp = cache_k[i, page_table].reshape(db, past_len, MOBA_HEADS, HEAD_DIM)
        vp = cache_v[i, page_table].reshape(db, past_len, MOBA_HEADS, HEAD_DIM)
        return kp, vp

    y_sample, k_s, v_s, dn_s, dnc_s, scc_s, ffc_s = trunk(
        x_sample, past_len, past_kv, state_dn, state_dn_conv, state_sc_conv, state_ffn_conv, w_in_mix, dn_conv_w,
        dn_a_log, dn_dt_bias, dn_norm_w, w_out_mix, w_in_sc, sc_conv_w, w_out_sc, ln_mix_g, ln_mix_b, w_up,
        ffn_conv_w, w_down, ln_ffn_g, ln_ffn_b)
    return (y_prompt, y_sample, k_p, v_p, k_s, v_s, dn_p, dn_s, dnc_p, dnc_s, scc_p, scc_s, ffc_p, ffc_s)


_drawn_inputs = setup_inputs


def setup_inputs(seed=0):
    import zlib

    import numpy as np

    out = dict(_drawn_inputs(seed))
    spreads = {}
    factors = {'dn_norm_w': 8.0, 'cache_v': 2.867}
    for name, (base, spread) in spreads.items():
        noise = np.random.default_rng([zlib.crc32(name.encode()), seed]).standard_normal(out[name].shape)
        drawn = base * np.exp(spread * noise) if base else spread * noise
        out[name] = __import__('jax').numpy.asarray(drawn.astype(out[name].dtype))
    for name, factor in factors.items():
        out[name] = (out[name] * factor).astype(out[name].dtype)
    return out
```

```python
from contextlib import ExitStack

import concourse.bass as bass
from concourse import mybir

F32 = mybir.dt.float32
F32R = mybir.dt.float32r
I32 = mybir.dt.int32
ALU = mybir.AluOpType
ACT = mybir.ActivationFunctionType
AX = mybir.AxisListType

P = 128
D = 1024
KD = D // P
SEQ, NB, NT = 256, 8, 8
SMP = NB * NT
TOK = SEQ + SMP
H, HD = 4, 128
PAST, PAGE, POOL = 2048, 128, 160
NPG = PAST // PAGE
BLK = 256
NBLK = PAST // BLK
TOPK = 3
DFF = 2816
KF = DFF // P
DNW = 3 * H * HD
ALPHA = 4.0 ** 0.25
SCALE = HD ** -0.5
LN_EPS, NORM_EPS = 1e-5, 1e-6
NEG = -1e30
SLOPES = [2.0 ** (-8.0 * (h + 1) / H) for h in range(H)]
TILES = [(0, 128), (128, 128), (256, 64)]

WD = 356
WF = 348
LD, LF = 344, 336

SLOT_MIX, SLOT_OUT, SLOT_FFN, SLOT_DOWN, SLOT_SC = 7, 2, KF // 2, 6, 6
S_MIX = 0
S_OUT = S_MIX + SLOT_MIX
S_UP = [S_OUT + SLOT_OUT]
S_DOWN = [S_UP[0] + SLOT_FFN]
S_SC = S_DOWN[0] + SLOT_DOWN
S_SCO = S_SC + SLOT_SC
S_UP.append(S_SCO + SLOT_OUT)
S_DOWN.append(S_UP[1] + SLOT_FFN)
S_END = S_DOWN[1] + SLOT_DOWN
CREDIT = 4

PA_DN, PA_SC, PA_LMG, PA_LMB, PA_NW, PA_N = 0, 48, 72, 88, 104, 105
PB_F, PB_LFG, PB_LFB, PB_N = 0, 66, 82, 98
PC_N = 66

SEMS = """
params_in xtok_in hist_in wba_in pt_in raw_in k_in0 k_in1 k_in2 k_in3 s0_in0 stores
hi_done lo_done chunk_done rel_act conv_step
kT_mm kT_a kT_v s_mm s_raw s_bias s_kept mT_mm m_col ov_mm
gelu_done h_done hh_done hid_ready sc_prod
pe_step act_step dve_step pool_step
""".split()


class Steps:

    def __init__(self, sem, names):
        self.sem, self.names, self.made = sem, names, []
        self.value = {n: i + 1 for i, n in enumerate(names)}

    def up(self, ins, name):
        self.made.append(name)
        assert self.names[len(self.made) - 1] == name, (name, len(self.made))
        ins.then_inc(self.sem, 1)

    def wait(self, eng, name):
        eng.wait_ge(self.sem, self.value[name])


STEPS = {
    "pe": """
xT0 xT1 xT2 xT3 xT4 xT5 xT6 xT7 parT histT ba dntail0 dntail1 dntail2 ss0 ss1 ss2 ss3 ss4 ss5 ss6 ss7 cum0 kk0 tok0
cum1 kk1 tok1 cum2 kk2 tok2 invw0 invw1 invw2 invw3 invw4 invw5 invu3 invu4 invu5 invw6 invw7 invw8 invu6 invu7 invu8
invw9 invw10 invu9 invu10 invw11 invw12 invu11 invu12 invw13 invw14 invu13 invu14 invw15 invw16 invu15 invu16 vn0 o0
st0 ks1 vn1 o1 st1 ksT ks2 vn2 o2 stS0 stS1 stS2 stS3 oss0 oss1 oss2 oss3 kvT0 kvT1 kvT2 kvT3 kvT4 kvT5 ps0 ps1 pT0
pT1 pT2 po0 po1 own gates statT c0 c1 c2 c3 mb den f0_hist stat0 f0_tail0 f0_tail1 f0_tail2 f0_tail3 f0_tail4 f0_tail5
stat1 sc_hist sc_tail0 sc_tail1 stat2 f1_hist f1_tail0 f1_tail1 f1_tail2 f1_tail3 f1_tail4 f1_tail5 stat3 yT0 yT1 yT2
yT3 yT4 yT5
""".split(),
    "act": """
par0 par1 par2 xh0 xh1 xh2 xh3 xh4 xh5 xh6 xh7 hist silu dntail0 dntail1 dntail2 gexp gln l2sq0 l2sq1 l2sq2 ssln0
l2sq3 ssln1 l2sq4 ssln2 l2sq5 ssln3 l2sq6 ssln4 l2sq7 ssln5 ssln6 ssln7 rn egc0 egcb0 decay0 egc1 egcb1 decay1 egc2
egcb2 decay2 wsb3 wsb4 wsb5 wsb6 wsb7 wsb8 wsb9 wsb10 wsb11 wsb12 wsb13 wsb14 wsb15 wsb16 vnsb0 oT0 vnsb1 oT1 ksTsb
vnsb2 osq0 osq1 osq2 osq3 oln0 oln1 oln2 oln3 orn mixh_done kvtok0 kvtok1 kvtok2 kvtok3 kvtok4 kvtok5 pexp0 pexp1
pexp2 pexp3 pexp4 pexp5 pexp6 pexp7 pTsb0 pTsb1 pTsb2 poh0 poh1 pexpS0 pexpS1 pexpS2 pexpS3 ownexp attn_endh sq0_0
sq0_1 sq0_2 sq0_3 sq0_4 sq0_5 sq0_6 sq0_7 msq0 lnv0 rstd0 ln0_0 lnh0_0 ln0_1 lnh0_1 ln0_2 lnh0_2 ln0_3 lnh0_3 ln0_4
lnh0_4 ln0_5 lnh0_5 ln0_6 lnh0_6 ln0_7 lnh0_7 f0_hist f0_tail0 f0_tail1 f0_tail2 f0_tail3 f0_tail4 f0_tail5 sq1_0
sq1_1 sq1_2 sq1_3 sq1_4 sq1_5 sq1_6 sq1_7 msq1 lnv1 rstd1 ln1_0 lnh1_0 ln1_1 lnh1_1 ln1_2 lnh1_2 ln1_3 lnh1_3 ln1_4
lnh1_4 ln1_5 lnh1_5 ln1_6 lnh1_6 ln1_7 lnh1_7 sc_hist sch0 sch1 sch2 sch3 sch4 sch5 sch6 sch7 sc_tail0 sc_tail1 sq2_0
sq2_1 sq2_2 sq2_3 sq2_4 sq2_5 sq2_6 sq2_7 msq2 lnv2 rstd2 ln2_0 lnh2_0 ln2_1 lnh2_1 ln2_2 lnh2_2 ln2_3 lnh2_3 ln2_4
lnh2_4 ln2_5 lnh2_5 ln2_6 lnh2_6 ln2_7 lnh2_7 f1_hist f1_tail0 f1_tail1 f1_tail2 f1_tail3 f1_tail4 f1_tail5 sq3_0
sq3_1 sq3_2 sq3_3 sq3_4 sq3_5 sq3_6 sq3_7 msq3 lnv3 rstd3 ln3_0 ln3_1 ln3_2 ln3_3 ln3_4 ln3_5 ln3_6 ln3_7 y0 y1 y2 y3
y4 y5
""".split(),
    "dve": """
gz xres0 xres1 xres2 xres3 xres4 xres5 xres6 xres7 xl0 xl1 xl2 xl3 xl4 xl5 xl6 xl7 ba gxa gx gone beta gsp g qknorm
qkn ug0 gcl0 cumsb0 dmax0 dmat0 mask0 La0 intra0 L0 tok0 qg0 ug1 gcl1 cumsb1 dmax1 dmat1 mask1 La1 intra1 L1 tok1 qg1
ug2 gcl2 cumsb2 dmax2 dmat2 mask2 La2 intra2 L2 tok2 qg2 inv0 inv1 inv2 inv3 inv4 inv5 inv6 inv7 inv8 inv9 inv10 inv11
inv12 inv13 inv14 inv15 inv16 state0 rhsa1 rhs1 statea state1 rhsa2 rhs2 oT2 vnm0 s0g0 stS0 vnm1 s0g1 stS1 vnm2 s0g2
stS2 vnm3 s0g3 stS3 on1 mixo mixl_done plog0 plog1 pmaxa0 pmax0 pmaxa1 pmax1 prec0 pnorm0 prec1 pnorm1 pol0 pol1 owl
mo pick8 mos gsb statsb gate mblk rk1 rk2 rk3 rank pen mpen mt mtot shift rc rm z0 z1 z2 z3 ownz dsum0 dsum1 dsum2
dsum3 drec ovn attn_end r0_0 r0_1 r0_2 r0_3 r0_4 r0_5 r0_6 r0_7 vara0 var0 bm0 t1_0_0 t2_0_0 t1_0_1 t2_0_1 x0_0 t1_0_2
t2_0_2 x0_1 t1_0_3 t2_0_3 x0_2 t1_0_4 t2_0_4 x0_3 t1_0_5 t2_0_5 x0_4 t1_0_6 t2_0_6 x0_5 t1_0_7 t2_0_7 x0_6 x0_7 r1_0
r1_1 r1_2 r1_3 r1_4 r1_5 r1_6 r1_7 vara1 var1 bm1 t1_1_0 t2_1_0 t1_1_1 t2_1_1 x1_0 t1_1_2 t2_1_2 x1_1 t1_1_3 t2_1_3
x1_2 t1_1_4 t2_1_4 x1_3 t1_1_5 t2_1_5 x1_4 t1_1_6 t2_1_6 x1_5 t1_1_7 t2_1_7 x1_6 x1_7 scp0 schl0 scp1 schl1 scp2 schl2
scp3 schl3 scp4 schl4 scp5 schl5 scp6 schl6 scp7 schl7 sc_gated r2_0 r2_1 r2_2 r2_3 r2_4 r2_5 r2_6 r2_7 vara2 var2 bm2
t1_2_0 t2_2_0 t1_2_1 t2_2_1 x2_0 t1_2_2 t2_2_2 x2_1 t1_2_3 t2_2_3 x2_2 t1_2_4 t2_2_4 x2_3 t1_2_5 t2_2_5 x2_4 t1_2_6
t2_2_6 x2_5 t1_2_7 t2_2_7 x2_6 x2_7 r3_0 r3_1 r3_2 r3_3 r3_4 r3_5 r3_6 r3_7 vara3 var3 bm3 t1_3_0 t2_3_0 t1_3_1 t2_3_1
t1_3_2 t2_3_2 t1_3_3 t2_3_3 t1_3_4 t2_3_4 t1_3_5 t2_3_5 t1_3_6 t2_3_6 t1_3_7 t2_3_7
""".split(),
    "pool": """
const0 const1 ident_done const2 const3 cin_zero const4 const5 const6 const7 const8 const9 const10 const11 const12
const13 const14 const15 const16 const17 const18 const19 const20 const21 const22 const23 const24 const25 const26
const27 const28 const29 const30 const31 const32 const33 const34 const35 const36 const37 const38 const39 const40
const41 const42 const43 const44 const45 const46 const47 const48 const49 const50 const51 const52 const53 const54
const55 const56 const57 const58 const59 const60 const61 const62 const63 const64 const65 const66 const67 const68
const69 const70 const71 const72 consts dnlast lm0 lm1 lm2 lm3 lm4 lm5 lm6 lm7 lm8 lm9 lm10 lm11 lm12 lm13 lm14 lm15
lm16 f0_zero accs0_1 accq0_0 accq0_1 accs0_2 accq0_2 accs0_3 accq0_3 accs0_4 accq0_4 accs0_5 accq0_5 accs0_6 accq0_6
f0_last sc_zero accs1_1 accq1_0 accq1_1 accs1_2 accq1_2 accs1_3 accq1_3 accs1_4 accq1_4 accs1_5 accq1_5 accs1_6
accq1_6 sc_last f1_zero accs2_1 accq2_0 accq2_1 accs2_2 accq2_2 accs2_3 accq2_3 accs2_4 accq2_4 accs2_5 accq2_5
accs2_6 accq2_6 f1_last accs3_1 accq3_0 accq3_1 accs3_2 accq3_2 accs3_3 accq3_3 accs3_4 accq3_4 accs3_5 accq3_5
accs3_6 accq3_6
""".split(),
}


def trunk_program(nc, a, o):
    ctx = ExitStack()
    with ctx:
        def sb(name, shape, dt=F32, stack=ctx):
            return stack.enter_context(nc.sbuf_tensor(name, shape, dt))

        s = {n: ctx.enter_context(nc.semaphore(n)) for n in SEMS}
        bank = [ctx.enter_context(nc.psum_tensor(f"bank{i}", [P, 512], F32)) for i in range(8)]

        raw = sb("raw", [P, 2 * KD * 512])
        hi = sb("hi", [P, 2, KD, 256], F32R)
        lo = sb("lo", [P, 2, KD, 256], F32R)
        xh = sb("xh", [P, KD, TOK], F32R)
        xl = sb("xl", [P, KD, TOK], F32R)
        xres = sb("xres", [P, KD, TOK])
        par = sb("par", [P, 3, P])
        ident = sb("ident", [P, P])
        ones = sb("ones", [P, P])
        onesD = sb("onesD", [P, P])
        eps6 = sb("eps6", [P, 2])
        scrap = sb("scrap", [P, 3, 8])

        sA = ExitStack()
        mb = sb("mb", [P, 12 * TOK], stack=sA)
        upper = sb("upper", [P, P], stack=sA)
        lower = sb("lower", [P, P], stack=sA)
        bdiff = sb("bdiff", [P, 7, P], stack=sA)
        same8 = sb("same8", [SMP, SMP], stack=sA)
        upper8 = sb("upper8", [SMP, SMP], stack=sA)
        lower8 = sb("lower8", [SMP, SMP], stack=sA)
        pick8 = sb("pick8", [SMP, NT], stack=sA)
        ltri = sb("ltri", [32, NBLK, NBLK], stack=sA)
        pastb = sb("pastb", [P, 512], stack=sA)
        promptb = sb("promptb", [P, H, 256], stack=sA)
        ownq = sb("ownq", [SMP, H, SMP], stack=sA)
        ownk = sb("ownk", [SMP, H, SMP], stack=sA)
        gates = sb("gates", [P, 14, 12], stack=sA)
        dtal = sb("dtal", [P, 2, H], stack=sA)
        s1 = ExitStack()
        zsb = sb("zsb", [P, H, TOK], stack=s1)
        qkv = sb("qkv", [P, 12 * WF], stack=s1)
        s11 = ExitStack()
        cin = sb("cin", [P, 12 * WD], stack=s11)
        xtok = sb("xtok", [P, 3, D], stack=s11)
        prows = sb("prows", [P, 3, P], stack=s11)
        dnrows = sb("dnrows", [64, DNW], stack=s11)
        wba = sb("wba", [P, KD, 8], stack=s11)
        iot = sb("iot", [P, 512], I32, stack=s11)
        iof = sb("iof", [P, 512], stack=s11)
        bs = sb("bs", [P, 8, P], stack=s11)
        s11.close()
        s2 = ExitStack()
        tP = sb("tP", [P, 2, 512], stack=s2)
        ttP = sb("ttP", [P, 2, 512], stack=s2)
        lP = sb("lP", [P, 2, 512], stack=s2)
        inP = sb("inP", [P, 2, 512], stack=s2)
        tS = sb("tS", [SMP, 256], stack=s2)
        ttS = sb("ttS", [SMP, 256], stack=s2)
        lS = sb("lS", [SMP, 256], stack=s2)
        inS = sb("inS", [SMP, 256], stack=s2)
        s0 = sb("s0", [P, 32, P], stack=s2)
        ktok = sb("ktok", [P, 3, 512], stack=s2)
        vtok = sb("vtok", [P, 3, 512], stack=s2)
        qg = sb("qg", [P, H, TOK], stack=s2)
        spr = sb("spr", [P, 512], stack=s2)
        rtmp = sb("rtmp", [P, 512], stack=s2)
        vnew = sb("vnew", [P, 512], stack=s2)
        eglS = sb("eglS", [P, 32], stack=s2)
        s2.close()
        s1.close()
        s3 = ExitStack()
        kring = sb("kring", [P, 4, 4, 512], stack=s3)
        sx = sb("sx", [P, NB * 512], stack=s3)
        kwork = sb("kwork", [P, 2048], stack=s3)
        kvtok = sb("kvtok", [P, 2, 3, 512], stack=s3)
        pst = sb("pst", [P, 3, 8], stack=s3)
        mcol = sb("mcol", [P, 2, 32], stack=s3)
        owl = sb("owl", [SMP, 2, 256], stack=s3)
        mo = sb("mo", [SMP, 4], stack=s3)
        mos = sb("mos", [SMP, NB, H], stack=s3)
        st32 = sb("st32", [32, 10, 64], stack=s3)
        rkA = sb("rkA", [32, 512], stack=s3)
        rkB = sb("rkB", [32, 512], stack=s3)
        rm = sb("rm", [32, 256], stack=s3)
        dsum = sb("dsum", [P, 256], stack=s3)
        drec = sb("drec", [P, 256], stack=s3)
        ovn = sb("ovn", [P, 256], stack=s3)
        ptab = sb("ptab", [1, NB * NPG], I32, stack=s3)
        s3.close()
        sA.close()

        hh = sb("hh", [P, KF, TOK], F32R)
        hl = sb("hl", [P, KF, TOK], F32R)
        cb = sb("cb", [P, KF * WF])
        rows = sb("rows", [64, DFF])
        acc = sb("acc", [P, 2 * WF])
        hraw = sb("hraw", [P, 2, TOK])
        sq = sb("sq", [P, 2, TOK])
        lnt = sb("lnt", [P, 5, TOK])

        step = {e: Steps(s[f"{e}_step"], STEPS[e]) for e in ("pe", "act", "dve", "pool")}
        PE, AC, DV, PO = step["pe"], step["act"], step["dve"], step["pool"]

        spares = [0, 0, 0]

        def spare(e):
            spares[e] += 1
            return scrap[:, e, spares[e] - 1:spares[e]]

        def t4(x, n=P):
            return x.rearrange("p (h c) -> p h c", h=H)

        def tri(t):
            return (upper[:], lower[:]) if t < 2 else (upper8[:], lower8[:])

        def mid(x, n):
            return x.rearrange("p (a c) -> p a c", a=1).to_broadcast([x.shape[0], n, x.shape[1]])

        def last(x, n):
            return x.rearrange("p (c a) -> p c a", a=1).to_broadcast([x.shape[0], x.shape[1], n])

        def gate(i, t, n=P):
            return gates[0:n, i, 4 * t:4 * t + 4]

        B_, X_, NX, L1, EB, BETA, G_, GC, EGC, NBE, KD_, GL, EGL = range(13)
        T_ = [tP[:, 0, :], tP[:, 1, :], tS[:]]
        TT = [ttP[:, 0, :], ttP[:, 1, :], ttS[:]]
        L_ = [lP[:, 0, :], lP[:, 1, :], lS[:]]
        IN = [inP[:, 0, :], inP[:, 1, :], inS[:]]
        member = same8[:, 0:SMP:NT]
        sc0 = s0[:, :, :].rearrange("p a c -> p (a c)")
        lmb = [sc0[:, 512 * i:512 * i + 512] for i in range(2)]
        wsb = [sc0[:, 1024:1536], sc0[:, 1536:2048], sc0[0:SMP, 2048:2304]]
        dsc = [sc0[:, 2304:2816], sc0[:, 2816:3328]]
        kq = qkv[:, 8 * WF:8 * WF + 512]
        vnm = tP[0:SMP, :, :].rearrange("p a c -> p (a c)")
        qk3 = qkv[:, :].rearrange("p (c w) -> p c w", w=WF)
        oT = qk3[:, 0:4, 0:TOK]
        INV = [(l, t) for l in range(7) for t in range(3) if t < 2 or l < 3]

        smp = sc0[:, 3328:4096].rearrange("p (c w) -> p c w", w=SMP)

        def head(c, t):
            return qk3[:, c, 128 * t:128 * t + 128] if t < 2 else smp[:, c, :]

        def weight(i):
            return raw[:, bass.ds(i % 2 * (KD * 512), KD * 512)].rearrange("p (k c) -> p k c", c=512)

        def vec(pack, row):
            return par[:, pack, row:row + 1]

        par2 = par[:, :, :].rearrange("p a c -> p (a c)")

        def l2s(c):
            return (rtmp, spr)[c % 2][:, 0:LD]

        l2n = sc0[:, 0:8 * LD].rearrange("p (c w) -> p c w", w=LD)
        pl0 = sx[:, 0:512].rearrange("p (h c) -> p h c", h=H)
        pl1 = sx[:, 512:1536].rearrange("p (h c) -> p h c", h=H)
        pT = sx[:, 1536:3072]
        kT, sraw, sbias = [kwork[:, 0:512], kwork[:, 512:1024]], kwork[:, 1024:1536], kwork[:, 1536:2048]
        rc = kwork[0:32, :]
        last2 = lnt[:, 0:2, :].rearrange("p a c -> p (a c)")
        mbh = mb[:, :].rearrange("p (c w) -> p c w", w=TOK)
        CONV = [48, 48 + 3 * KF + 3 * KD]
        REL = [32, 32 + KF + KD]
        REL_SC, CONV_SC = 32 + KF, 48 + 3 * KF

        def hraw_y(t):
            return cb[0:TILES[t][1], D * t:D * t + D]

        block = ctx.enter_context(nc.Block())

        @block.sync
        def _(sp_):
            w_mix = a["w_in_mix"][0].rearrange("(k p) c -> p k c", p=P)
            w_out = a["w_out_mix"][0].rearrange("(k p) c -> p k c", p=P)
            w_sc = a["w_in_sc"][0].rearrange("(k p) c -> p k c", p=P)
            w_so = a["w_out_sc"][0].rearrange("(k p) c -> p k c", p=P)

            def slot_free(n):
                sp_.wait_ge(s["lo_done"], 2 * (n - 1))
                sp_.wait_ge(s["raw_in"], 32 * n)

            def load_whole(n, src, nk=KD):
                sp_.dma_start(weight(n)[:, 0:nk, :], src).then_inc(s["raw_in"], 32)

            sp_.dma_start(xtok[:, 0:2, :], a["x_prompt"][0].rearrange("(t p) d -> p t d", p=P)).then_inc(s["xtok_in"], 16)
            sp_.dma_start(xtok[0:SMP, 2, :], a["x_sample"].rearrange("b t d -> (b t) d")).then_inc(s["xtok_in"], 16)
            for n in range(SLOT_MIX):
                if n == 1:
                    sp_.wait_ge(s["raw_in"], 32)
                if n > 1:
                    slot_free(n)
                c0 = 512 * n if n < 4 else 2056 + 512 * (n - 4)
                load_whole(n, w_mix[:, :, c0:c0 + 512])
            with sp_.Fori(0, SLOT_OUT) as i:
                slot_free(i + S_OUT)
                load_whole(i + S_OUT, w_out[:, :, bass.ds(i * 512, 512)])

            AC.wait(sp_, "mixh_done")
            DV.wait(sp_, "mixl_done")
            sp_.wait_ge(s["stores"], 16 * 7)
            sp_.dma_start(ptab[:, :], a["page_table"].rearrange("(a b) n -> a (b n)", a=1)).then_inc(s["pt_in"], 16)
            sp_.wait_ge(s["pt_in"], 16)

            def load_pages(cache, b, g):
                for j in range(4):
                    page = sp_.value_load(ptab[0:1, bass.ds(b * NPG + (4 * g + j), 1)], min_val=0, max_val=POOL - 1)
                    src = cache[bass.ds(page, 1)].rearrange("o p h d -> (o p) (h d)")
                    sp_.dma_start(kring[:, g, j, :], src).then_inc(s[f"k_in{g}"], 16)

            for g in range(4):
                load_pages(a["cache_k"][0], 0, g)
            with sp_.Fori(1, NB) as b:
                for g in range(4):
                    sp_.wait_ge(s["kT_mm"], b * 16 + (4 * g + 4 - 16))
                    load_pages(a["cache_k"][0], b, g)
            for g in range(4):
                sp_.wait_ge(s["kT_mm"], NB * 16 + (4 * g + 4 - 16))
                sp_.wait_ge(s[f"k_in{g}"], NB * 64)
                load_pages(a["cache_v"][0], 0, g)
            with sp_.Fori(1, NB) as b:
                for g in range(4):
                    sp_.wait_ge(s["ov_mm"], b * 4 + (g + 1 - 4))
                    load_pages(a["cache_v"][0], b, g)

            def feed_forward(layer):
                w_up = a["w_up"][layer].rearrange("(k p) c -> p k c", p=P)
                w_dn = a["w_down"][layer].rearrange("(k p) c -> p k c", p=P)
                with sp_.Fori(0, SLOT_FFN) as i:
                    slot_free(i + S_UP[layer])
                    w = weight(i + S_UP[layer])
                    sp_.dma_start(w[:, :, 0:256], w_up[:, :, bass.ds(i * 256, 256)]).then_inc(s["raw_in"], 16)
                    sp_.dma_start(w[:, :, 256:512], w_up[:, :, bass.ds(i * 256 + DFF, 256)]).then_inc(s["raw_in"], 16)
                with sp_.Fori(0, 2) as i:
                    for k in range(3):
                        n = 3 * i + (S_DOWN[layer] + k)
                        nk = min(KD, KF - KD * k)
                        slot_free(n)
                        load_whole(n, w_dn[:, KD * k:KD * k + nk, bass.ds(i * 512, 512)], nk)

            feed_forward(0)
            with sp_.Fori(0, 4) as i:
                slot_free(i + S_SC)
                w = weight(i + S_SC)
                sp_.dma_start(w[:, :, 0:256], w_sc[:, :, bass.ds(i * 256 + D, 256)]).then_inc(s["raw_in"], 16)
                sp_.dma_start(w[:, :, 256:512], w_sc[:, :, bass.ds(i * 256 + 2 * D, 256)]).then_inc(s["raw_in"], 16)
            with sp_.Fori(0, 2) as i:
                slot_free(i + (S_SC + 4))
                load_whole(i + (S_SC + 4), w_sc[:, :, bass.ds(i * 512, 512)])
            with sp_.Fori(0, SLOT_OUT) as i:
                slot_free(i + S_SCO)
                load_whole(i + S_SCO, w_so[:, :, bass.ds(i * 512, 512)])
            feed_forward(1)

        @block.gpsimd
        def _(pool):
            PAR = [(a["dn_conv_w"].rearrange("l k (c p) -> (l k c) p", p=P), 0, PA_DN, 48),
                   (a["sc_conv_w"].rearrange("l k (c p) -> (l k c) p", p=P), 0, PA_SC, 24),
                   (a["ln_mix_g"].rearrange("l (c p) -> (l c) p", p=P), 0, PA_LMG, 16),
                   (a["ln_mix_b"].rearrange("l (c p) -> (l c) p", p=P), 0, PA_LMB, 16),
                   (a["dn_norm_w"], 0, PA_NW, 1),
                   (a["ffn_conv_w"][0].rearrange("k (c p) -> (k c) p", p=P), 1, PB_F, 66),
                   (a["ln_ffn_g"].rearrange("l (c p) -> (l c) p", p=P), 1, PB_LFG, 16),
                   (a["ln_ffn_b"].rearrange("l (c p) -> (l c) p", p=P), 1, PB_LFB, 16),
                   (a["ffn_conv_w"][1].rearrange("k (c p) -> (k c) p", p=P), 2, 0, 66)]
            for src, pack, row, n in PAR:
                pool.dma_start(prows[row:row + n, pack, :], src).then_inc(s["params_in"], 16)
            pool.dma_start(dnrows[0:24, :], a["state_dn_conv"][0].rearrange("b k c -> (b k) c")).then_inc(s["hist_in"], 16)
            with nc.allow_non_contiguous_dma(reason="eight gate columns of a wide row"):
                pool.dma_start(wba[:, :, :], a["w_in_mix"][0].rearrange("(k p) c -> p k c", p=P)[:, :, 2048:2056])\
                    .then_inc(s["wba_in"], 16)
            pool.dma_start(dtal[:, 0, :], a["dn_dt_bias"][0:1, :].to_broadcast([P, H])).then_inc(s["wba_in"], 16)
            pool.dma_start(dtal[:, 1, :], a["dn_a_log"][0:1, :].to_broadcast([P, H])).then_inc(s["wba_in"], 16)

            made = [0]

            def link(ins):
                PO.up(ins, f"const{made[0]}")
                PO.wait(pool, f"const{made[0]}")
                made[0] += 1

            def select(x, pattern, base, cm, fill, op=ALU.is_ge):
                link(pool.affine_select(out=x, in_=x, compare_op=op, fill=fill, base=base, pattern=pattern,
                                        channel_multiplier=cm))

            link(pool.memset(ident[:], 0.0))
            select(ident[:], [[-1, P]], 0, 1, 1.0, ALU.not_equal)
            PO.up(pool.memset(ones[:], 1.0), "ident_done")
            link(pool.memset(onesD[:], 1.0 / D))
            link(pool.memset(eps6[:], NORM_EPS))
            cin3 = cin[:, :].rearrange("p (c w) -> p c w", w=WD)
            PO.up(pool.memset(cin3[:, :, 0:3], 0.0), "cin_zero")
            link(pool.memset(upper[:], 1.0))
            select(upper[:], [[1, P]], 0, -1, 0.0)
            link(pool.memset(lower[:], 1.0))
            select(lower[:], [[-1, P]], -1, 1, 0.0)
            link(pool.memset(bs[:, 7, :], 1.0))
            link(pool.tensor_copy(bs[:, 0, :], ident[:]))
            for l in range(1, 7):
                z, n = 1 << l, P >> l
                link(pool.memset(bs[:, l, :], 1.0))
                x = bs[:, l, :].rearrange("p (n z) -> p n z", z=z)
                select(x, [[-z, n], [0, z]], 0, 1, 0.0)
                select(x, [[z, n], [0, z]], z - 1, -1, 0.0)
            link(pool.tensor_sub(bdiff[:, :, :], bs[:, 1:8, :], bs[:, 0:7, :]))
            link(pool.tensor_copy(same8[:], bs[0:SMP, 3, 0:SMP]))
            link(pool.tensor_mul(upper8[:], upper[0:SMP, 0:SMP], same8[:]))
            link(pool.tensor_mul(lower8[:], lower[0:SMP, 0:SMP], same8[:]))
            link(pool.memset(ltri[:], 1.0))
            select(ltri[:], [[1, NBLK], [-1, NBLK]], -1, 0, 0.0)
            link(pool.iota(iot[:, 0:128].rearrange("p (g t) -> p g t", t=NT), pattern=[[PAGE, NPG], [-1, NT]], base=-PAST,
                           channel_multiplier=1))
            link(pool.iota(iot[:, 128:384], pattern=[[1, 256]], base=-128, channel_multiplier=-1))
            link(pool.iota(iot[:, 384:448], pattern=[[1, SMP]], base=0, channel_multiplier=-1))
            link(pool.tensor_copy(iof[:, 0:448], iot[:, 0:448]))
            for h in range(H):
                link(pool.tensor_scalar(pastb[:, 128 * h:128 * h + 128], iof[:, 0:128], SLOPES[h], None, ALU.mult))
                link(pool.tensor_scalar(promptb[:, h, :], iof[:, 128:384], SLOPES[h], None, ALU.mult))
                link(pool.tensor_scalar(ownq[:, h, :], iof[0:SMP, 384:448], SLOPES[h], None, ALU.mult))
                link(pool.tensor_scalar(ownk[:, h, :], iof[0:SMP, 384:448], -SLOPES[h], None, ALU.mult))
            select(promptb[:, :, :], [[0, H], [-1, 256]], 128, 1, NEG)
            select(ownq[:, :, :], [[0, H], [-1, SMP]], 0, 1, NEG)
            select(ownk[:, :, :], [[0, H], [1, SMP]], 0, -1, NEG)
            for x in (ownq, ownk):
                for h in range(H):
                    w = x[:, h, :].rearrange("p (b t) -> p b t", t=NT)
                    select(w, [[-NT, NB], [0, NT]], 0, 1, NEG)
                    select(w, [[NT, NB], [0, NT]], NT - 1, -1, NEG)
            PO.up(pool.tensor_copy(iof[0:1, 0:1], iof[0:1, 1:2]), "consts")

            pool.wait_ge(s["rel_act"], 12 + CREDIT)
            PO.wait(pool, "consts")
            PO.up(pool.tensor_copy(iof[:, 0:324].rearrange("p (c b s) -> p c b s", c=12, s=3),
                                   cin3[:, :, SEQ:SEQ + 99].rearrange("p c (b s) -> p c b s", s=11)[:, :, :, 0:3]), "dnlast")
            AC.wait(pool, "dntail2")
            pool.dma_start(o["dnc_p"][0, 0], dnrows[32:35, :]).then_inc(s["stores"], 16)
            pool.dma_start(o["dnc_s"][0].rearrange("b k c -> (b k) c"), dnrows[35:59, :]).then_inc(s["stores"], 16)

            for n, (l, t) in enumerate(INV):
                sz = TILES[t][1]
                if n == 0:
                    DV.wait(pool, "tok2")
                DV.wait(pool, f"L{t}")
                if n >= 2:
                    PE.wait(pool, f"invw{n - 2}")
                    if INV[n - 2][0] == 0:
                        DV.wait(pool, f"inv{n - 2}")
                x = t4(lmb[n % 2][0:sz, 0:H * sz])
                PO.up(pool.tensor_tensor(x, t4(L_[t]), mid(bdiff[0:sz, l, 0:sz], H), ALU.mult), f"lm{n}")

            DV.wait(pool, "qg2")
            PE.wait(pool, f"invu{len(INV) - 1}")
            PE.wait(pool, f"invw{len(INV) - 1}")
            for h in range(H):
                pool.dma_start(s0[:, NB * h:NB * h + NB, :], a["state_dn"][0, :, h].rearrange("b d v -> d b v"))\
                    .then_inc(s["s0_in0"], 16)
            DV.wait(pool, "state1")
            pool.dma_start(o["dn_p"][0, 0].rearrange("h d v -> d h v"), t4(spr[:, :])).then_inc(s["stores"], 16)
            for h in range(H):
                DV.wait(pool, f"stS{h}")
                pool.dma_start(o["dn_s"][0, :, h].rearrange("b d v -> d b v"), s0[:, NB * h:NB * h + NB, :])\
                    .then_inc(s["stores"], 16)
            for kv, (op, os_) in enumerate((("k_p", "k_s"), ("v_p", "v_s"))):
                AC.wait(pool, f"kvtok{3 * kv + 2}")
                pool.dma_start(o[op][0, 0].rearrange("(t p) h d -> p t (h d)", p=P), kvtok[:, kv, 0:2, :]).then_inc(s["stores"], 16)
                pool.dma_start(o[os_][0].rearrange("b t h d -> (b t) (h d)"), kvtok[0:SMP, kv, 2, :]).then_inc(s["stores"], 16)

            pool.memset(spare(2), 0.0).then_inc(s["s_kept"], 1)
            with pool.Fori(0, NB) as b:
                pool.wait_ge(s["s_bias"], b + 1)
                pool.tensor_copy(sx[:, bass.ds(b * 512, 512)], kwork[:, 1536:2048]).then_inc(s["s_kept"], 1)

            def accumulate(n):
                for m in range(1, KD - 1):
                    DV.wait(pool, f"r{n}_{m}")
                    if m > 1:
                        PO.wait(pool, f"accs{n}_{m - 1}")
                    PO.up(pool.tensor_tensor(lnt[:, 0, :], xres[:, 0, :] if m == 1 else lnt[:, 0, :], xres[:, m, :],
                                             ALU.add), f"accs{n}_{m}")
                    if m == 1:
                        AC.wait(pool, f"sq{n}_0")
                        PO.up(pool.tensor_copy(lnt[:, 1, :], sq[:, 0, :]), f"accq{n}_0")
                    AC.wait(pool, f"sq{n}_{m}")
                    PO.wait(pool, f"accq{n}_{m - 1}")
                    PO.up(pool.tensor_tensor(lnt[:, 1, :], lnt[:, 1, :], sq[:, m % 2, :], ALU.add), f"accq{n}_{m}")

            cb3 = cb[:, :].rearrange("p (c w) -> p c w", w=WF)

            def history(name, src, n):
                pool.dma_start(rows[32:48, 0:P * n], src.rearrange("b k c -> (b k) c")).then_inc(s["hist_in"], 16)
                PO.up(pool.memset(cb3[:, 0:n, 0:2], 0.0), f"{name}_zero")

            def tails(name, n, op, os_):
                if name == "sc":
                    pool.wait_ge(s["sc_prod"], KD + 2)
                else:
                    pool.wait_ge(s["rel_act"], REL[int(name[1])] + KF)
                PO.up(pool.tensor_copy(last2[:, 0:18 * n].rearrange("p (c b s) -> p c b s", c=n, s=2),
                                       cb3[:, 0:n, SEQ:SEQ + 90].rearrange("p c (b s) -> p c b s", s=10)[:, :, :, 0:2]),
                      f"{name}_last")
                AC.wait(pool, f"{name}_tail{(n - 1) // 4}")
                pool.dma_start(op, rows[0:2, 0:P * n]).then_inc(s["stores"], 16)
                pool.dma_start(os_.rearrange("b k c -> (b k) c"), rows[2:18, 0:P * n]).then_inc(s["stores"], 16)

            DV.wait(pool, "attn_end")
            AC.wait(pool, "attn_endh")
            pool.wait_ge(s["stores"], 16 * 11)
            history("f0", a["state_ffn_conv"][0], KF)
            accumulate(0)
            tails("f0", KF, o["ffc_p"][0, 0], o["ffc_s"][0])
            PE.wait(pool, "f0_hist")
            history("sc", a["state_sc_conv"][0], KD)
            accumulate(1)
            pool.wait_ge(s["stores"], 16 * 13)
            tails("sc", KD, o["scc_p"][0, 0], o["scc_s"][0])
            PE.wait(pool, "sc_hist")
            DV.wait(pool, "sc_gated")
            history("f1", a["state_ffn_conv"][1], KF)
            accumulate(2)
            pool.wait_ge(s["stores"], 16 * 15)
            tails("f1", KF, o["ffc_p"][1, 0], o["ffc_s"][1])
            accumulate(3)
            for t in range(3):
                for half in range(2):
                    AC.wait(pool, f"y{2 * t + half}")
                cols = hraw_y(t)
                if t < 2:
                    pool.dma_start(o["y_p"][0, P * t:P * t + P, :], cols).then_inc(s["stores"], 16)
                else:
                    pool.dma_start(o["y_s"].rearrange("b t d -> (b t) d"), cols).then_inc(s["stores"], 16)
            pool.wait_ge(s["stores"], 16 * (17 + 3))

        @block.scalar
        def _(act):
            def copy(out, in_):
                return act.activation(out, in_, ACT.Copy)

            def split_hi(n, p):
                act.wait_ge(s["raw_in"], 32 * n + 32)
                act.wait_ge(s["chunk_done"], 4 * n + (2 * p - 2 + CREDIT))
                copy(hi[:, p], weight(n)[:, :, 256 * p:256 * p + 256]).then_inc(s["hi_done"], 1)

            def chunk(n, j):
                act.wait_ge(s["chunk_done"], 4 * n + (j + 1 + CREDIT))

            for _ in range(CREDIT):
                act.memzero(spare(0)).then_inc(s["rel_act"], 1)
            for i, n in enumerate((PA_N, PB_N, PC_N)):
                PE.wait(act, "parT")
                AC.up(copy(par[:, i, 0:n], bank[4][:, 128 * i:128 * i + n]), f"par{i}")
            for k in range(KD):
                DV.wait(act, f"xres{k}")
                AC.up(copy(xh[:, k, :], xres[:, k, :]), f"xh{k}")
            PE.wait(act, "histT")
            PO.wait(act, "cin_zero")
            cin3 = cin[:, :].rearrange("p (c w) -> p c w", w=WD)
            AC.up(copy(cin3[:, :, 259:347].rearrange("p c (b s) -> p c b s", s=11)[:, :, :, 0:3],
                       bank[5][:, 0:288].rearrange("p (c b k) -> p c b k", c=12, b=NB)), "hist")

            split_hi(0, 0)

            def mix_slot(n, evacuate):
                split_hi(n, 1)
                for j in (0, 1):
                    chunk(n, j)
                    evacuate(j)
                split_hi(n + 1, 0)
                for j in (2, 3):
                    chunk(n, j)
                    evacuate(j)

            with act.Fori(0, 3) as i:
                def to_rows(j):
                    copy(cin[:, bass.ds((4 * i + j) * WD + 3, SEQ)], bank[j][:, 0:SEQ])
                    copy(cin[:, bass.ds((4 * i + j) * WD + 259, 88)].rearrange("p (b s) -> p b s", s=11)[:, :, 3:11],
                         bank[j][:, SEQ:TOK].rearrange("p (b t) -> p b t", t=NT)).then_inc(s["rel_act"], 1)
                mix_slot(i, to_rows)
            mix_slot(3, lambda j: act.activation(zsb[:, j, :], bank[j][:, 0:TOK], ACT.Silu).then_inc(s["rel_act"], 1))
            act.wait_ge(s["conv_step"], 48)
            for c in range(12):
                ins = act.activation(qkv[:, c * WF:c * WF + LD], qkv[:, c * WF:c * WF + LD], ACT.Silu)
            AC.up(ins, "silu")
            with act.Fori(0, 3) as i:
                mix_slot(i + 4, lambda j: copy(mb[:, bass.ds((4 * i + j) * TOK, TOK)], bank[j][:, 0:TOK])
                         .then_inc(s["rel_act"], 1))
            for g in range(3):
                PE.wait(act, f"dntail{g}")
                AC.up(copy(dnrows[32:59, 512 * g:512 * g + 512], bank[4 + g][0:27, :]), f"dntail{g}")

            DV.wait(act, "gx")
            act.activation(gates[:, L1, :], gates[:, NX, :], ACT.Exp)
            act.activation(gates[:, EB, :], gates[:, B_, :], ACT.Exp, scale=-1.0)
            AC.up(act.activation(dtal[:, 1, :], dtal[:, 1, :], ACT.Exp), "gexp")
            DV.wait(act, "gone")
            AC.up(act.activation(gates[:, L1, :], gates[:, L1, :], ACT.Ln), "gln")

            act.wait_ge(s["stores"], 32)
            AC.wait(act, "silu")
            PO.wait(act, "consts")
            for c in range(10):
                if c >= 2:
                    PE.wait(act, f"ss{c - 2}")
                if c < 8:
                    AC.up(act.activation(l2s(c), qkv[:, c * WF:c * WF + LD], ACT.Square), f"l2sq{c}")
                if c >= 2:
                    AC.up(act.activation(l2n[:, c - 2, :], bank[(c - 2) % 4][:, 0:LD], ACT.Ln, bias=eps6[:, 0:1]),
                          f"ssln{c - 2}")
            AC.wait(act, "ssln7")
            AC.up(act.activation(l2n[:, :, :], l2n[:, :, :], ACT.Exp, scale=-0.5), "rn")

            for t, (_, n) in enumerate(TILES):
                bk = 4 * (t % 2)
                gcb, small = bank[bk + 2], bank[bk + 3]
                PE.wait(act, f"cum{t}")
                DV.wait(act, f"cumsb{t}")
                AC.up(act.activation(gate(EGC, t, n), gate(GC, t, n), ACT.Exp), f"egc{t}")
                act.activation(gate(KD_, t, n), gate(KD_, t, n), ACT.Exp)
                if t < 2:
                    act.activation(gate(EGL, t), gate(GL, t), ACT.Exp)
                else:
                    act.activation(eglS[:, :], small[:, 8:40], ACT.Exp)
                if t:
                    DV.wait(act, f"qg{t - 1}")
                DV.wait(act, f"dmat{t}")
                AC.up(act.activation(t4(vnew[:, 0:H * n]), gcb[:, 0:H * n].rearrange("p (h c) -> p h c", h=H), ACT.Exp),
                      f"egcb{t}")
                act.activation(dsc[0][0:n, 0:H * n], dsc[0][0:n, 0:H * n], ACT.Exp)
                AC.up(act.activation(dsc[1][0:n, 0:H * n], dsc[1][0:n, 0:H * n], ACT.Exp, scale=-1.0), f"decay{t}")

            for n, (l, t) in enumerate(INV):
                sz = TILES[t][1]
                if l == 0:
                    continue
                PE.wait(act, f"invw{n}")
                AC.up(copy(wsb[t][0:sz, 0:H * sz], bank[(0, 3, 6)[t]][0:sz, 0:H * sz]), f"wsb{n}")

            for t in range(2):
                PE.wait(act, f"vn{t}")
                AC.up(copy(vnew[:, :], bank[0][:, :]), f"vnsb{t}")
                PE.wait(act, f"o{t}")
                AC.up(copy(oT[:, :, 128 * t:128 * t + 128], t4(bank[1][:, :])), f"oT{t}")
            PE.wait(act, "ksT")
            for u in range(2):
                ins = copy(kq[:, 256 * u:256 * u + 256].rearrange("p (a t) -> p a t", t=NT),
                           bank[4][:, :].rearrange("p (a u t) -> p a u t", u=2, t=NT)[:, :, u, :])
            AC.up(ins, "ksTsb")
            PE.wait(act, "vn2")
            AC.up(copy(vnew[0:SMP, :], bank[7][0:SMP, :]), "vnsb2")

            for h in range(H):
                DV.wait(act, "oT2")
                AC.wait(act, "oT1")
                AC.up(act.activation(qg[:, h, :], oT[:, h, :], ACT.Square), f"osq{h}")
            for h in range(H):
                PE.wait(act, f"oss{h}")
                AC.up(act.activation(qg[:, h, :], bank[h][:, 0:TOK], ACT.Ln, scale=1.0 / HD, bias=eps6[:, 0:1]), f"oln{h}")
            AC.wait(act, "oln3")
            AC.up(act.activation(qg[:, :, :], qg[:, :, :], ACT.Exp, scale=-0.5), "orn")
            DV.wait(act, "mixo")
            AC.up(copy(xh[:, 0:4, :], oT), "mixh_done")

            act.wait_ge(s["stores"], 16 * 7)
            for i in range(6):
                n = TILES[i % 3][1]
                PE.wait(act, f"kvT{i}")
                if i == 0:
                    DV.wait(act, "mixl_done")
                AC.up(copy(kvtok[0:n, i // 3, i % 3, :], bank[i][0:n, :]), f"kvtok{i}")

            for i in range(8):
                t, h = divmod(i, 4)
                DV.wait(act, f"pmax{t}")
                x = pl0[:, h, :] if t == 0 else pl1[:, h, :]
                AC.up(act.activation(x, x, ACT.Exp, bias=pst[:, 0, i:i + 1], accum_out=pst[:, 1, i:i + 1]), f"pexp{i}")
            for g in range(3):
                PE.wait(act, f"pT{g}")
                AC.up(copy(pT[:, 512 * g:512 * g + 512], bank[3 + g][:, :]), f"pTsb{g}")
            for t in range(2):
                PE.wait(act, f"po{t}")
                AC.up(copy(xh[:, 4:8, 128 * t:128 * t + 128], t4(bank[6 + t][:, :])), f"poh{t}")

            act.memzero(spare(0)).then_inc(s["kT_a"], 1)
            act.memzero(spare(0)).then_inc(s["s_raw"], 1)
            with act.Fori(0, NB) as b:
                for u in range(1, 16, 2):
                    act.wait_ge(s["kT_mm"], 16 * b + (u + 1))
                    copy(kwork[:, 512:1024], bank[1][:, :]).then_inc(s["kT_a"], 1)
                act.wait_ge(s["s_mm"], b + 1)
                copy(kwork[:, 1024:1536], bank[2][:, :]).then_inc(s["s_raw"], 1)

            for j in range(4):
                DV.wait(act, f"z{j}")
                x = sx[:, 1024 * j:1024 * j + 1024]
                AC.up(act.activation(x, x, ACT.Exp), f"pexpS{j}")
            DV.wait(act, "ownz")
            AC.up(act.activation(owl[:, 0, :], owl[:, 0, :], ACT.Exp), "ownexp")
            DV.wait(act, "ovn")
            AC.up(copy(xh[:, 4:8, SEQ:TOK], ovn[:, :].rearrange("p (h c) -> p h c", h=H)), "attn_endh")

            def square(n, m):
                DV.wait(act, f"r{n}_{m}")
                if m >= 2:
                    PO.wait(act, f"accq{n}_{m - 2}")
                AC.up(act.activation(sq[:, m % 2, :], xres[:, m, :], ACT.Square), f"sq{n}_{m}")

            def norm(n, gpack, grow, bpack, brow):
                PE.wait(act, f"stat{n}")
                AC.up(act.activation(lnt[:, 2, :], bank[4][:, 0:TOK], ACT.Square), f"msq{n}")
                DV.wait(act, f"var{n}")
                AC.up(act.activation(lnt[:, 3, :], lnt[:, 3, :], ACT.Ln), f"lnv{n}")
                AC.wait(act, f"lnv{n}")
                AC.up(act.activation(lnt[:, 3, :], lnt[:, 3, :], ACT.Exp, scale=-0.5), f"rstd{n}")
                for m in range(KD):
                    DV.wait(act, f"t2_{n}_{m}")
                    AC.up(act.activation(xres[:, m, :], hraw[:, m % 2, :], ACT.Identity, scale=vec(gpack, grow + m),
                                         bias=vec(bpack, brow + m)), f"ln{n}_{m}")
                    if n < 3:
                        AC.wait(act, f"ln{n}_{m}")
                        AC.up(copy(xh[:, m, :], xres[:, m, :]), f"lnh{n}_{m}")

            cb3 = cb[:, :].rearrange("p (c w) -> p c w", w=WF)

            def history(name, n):
                PE.wait(act, f"{name}_hist")
                PO.wait(act, f"{name}_zero")
                AC.up(copy(cb3[:, 0:n, 258:338].rearrange("p c (b s) -> p c b s", s=10)[:, :, :, 0:2],
                           bank[6][:, 0:16 * n].rearrange("p (c b k) -> p c b k", c=n, b=NB)), f"{name}_hist")

            def tails(name, n):
                for g in range((n + 3) // 4):
                    w = min(512, P * n - 512 * g)
                    PE.wait(act, f"{name}_tail{g}")
                    AC.up(copy(rows[0:18, 512 * g:512 * g + w], bank[4 + g % 2 * 3][0:18, 0:w]), f"{name}_tail{g}")

            def feed_forward(layer):
                base = S_UP[layer]
                with act.Fori(0, SLOT_FFN) as i:
                    split_hi(i + base, 1)
                    for j in (0, 1):
                        chunk(i + base, j)
                        copy(cb[:, bass.ds((2 * i + j) * WF + 2, SEQ)], bank[j][:, 0:SEQ])
                        copy(cb[:, bass.ds((2 * i + j) * WF + 258, 80)].rearrange("p (b s) -> p b s", s=10)[:, :, 2:10],
                             bank[j][:, SEQ:TOK].rearrange("p (b t) -> p b t", t=NT)).then_inc(s["rel_act"], 1)
                    split_hi(i + (base + 1), 0)
                    for j in (0, 1):
                        act.wait_ge(s["conv_step"], 6 * i + (CONV[layer] + 5 + j))
                        act.activation(acc[:, WF * j:WF * j + LF], acc[:, WF * j:WF * j + LF], ACT.Gelu)\
                            .then_inc(s["gelu_done"], 1)
                    for j in (0, 1):
                        act.wait_ge(s["h_done"], 2 * i + (KF * layer + j + 3))
                        copy(hh[:, bass.ds(2 * i + j, 1), :], hraw[:, j:j + 1, :]).then_inc(s["hh_done"], 1)

            def down(layer, n):
                for i in range(2):
                    for k in range(3):
                        slot = S_DOWN[layer] + 3 * i + k
                        split_hi(slot, 1)
                        if k == 2:
                            square(n, 4 * i)
                            square(n, 4 * i + 1)
                        if slot + 1 < S_END:
                            split_hi(slot + 1, 0)
                        if k == 2:
                            square(n, 4 * i + 2)
                            square(n, 4 * i + 3)

            def out_proj(base, n):
                for i in range(SLOT_OUT):
                    split_hi(base + i, 1)
                    square(n, 4 * i)
                    square(n, 4 * i + 1)
                    split_hi(base + i + 1, 0)
                    square(n, 4 * i + 2)
                    square(n, 4 * i + 3)

            out_proj(S_OUT, 0)
            norm(0, 0, PA_LMG, 0, PA_LMB)
            history("f0", KF)
            feed_forward(0)
            tails("f0", KF)
            down(0, 1)
            norm(1, 1, PB_LFG, 1, PB_LFB)
            history("sc", KD)
            with act.Fori(0, 4) as i:
                n = i + S_SC
                split_hi(n, 1)
                for j in (0, 1):
                    chunk(n, j)
                    act.wait_ge(s["sc_prod"], 2 * i + (j + 1))
                    copy(hraw[:, j, :], bank[j][:, 0:TOK]).then_inc(s["rel_act"], 1)
                split_hi(i + (S_SC + 1), 0)
            for n in range(S_SC + 4, S_SC + 6):
                split_hi(n, 1)
                split_hi(n + 1, 0)
                for j in range(4):
                    DV.wait(act, f"scp{4 * (n - S_SC - 4) + j}")
                    AC.up(copy(hh[:, 4 * (n - S_SC - 4) + j, :], hraw[:, j % 2, :]), f"sch{4 * (n - S_SC - 4) + j}")
            tails("sc", KD)
            out_proj(S_SCO, 2)
            norm(2, 0, PA_LMG + KD, 0, PA_LMB + KD)
            history("f1", KF)
            feed_forward(1)
            tails("f1", KF)
            down(1, 3)
            norm(3, 1, PB_LFG + KD, 1, PB_LFB + KD)
            for i in range(6):
                n = TILES[i // 2][1]
                PE.wait(act, f"yT{i}")
                AC.up(copy(hraw_y(i // 2)[:, 512 * (i % 2):512 * (i % 2) + 512], bank[i][0:n, :]), f"y{i}")

        @block.vector
        def _(dve):
            def split_lo(n, p):
                dve.wait_ge(s["hi_done"], 2 * n + (p + 1))
                dve.tensor_tensor(lo[:, p], weight(n)[:, :, 256 * p:256 * p + 256], hi[:, p], ALU.subtract)\
                   .then_inc(s["lo_done"], 1)

            def chunk(n, j):
                dve.wait_ge(s["chunk_done"], 4 * n + (j + 1 + CREDIT))

            def tt(out, a_, b_, op):
                return dve.tensor_tensor(out, a_, b_, op)

            dve.memset(spare(1), 0.0).then_inc(s["h_done"], 1)
            dve.memset(spare(1), 0.0).then_inc(s["h_done"], 1)
            dve.memset(spare(1), 0.0).then_inc(s["sc_prod"], 1)
            dve.memset(spare(1), 0.0).then_inc(s["sc_prod"], 1)
            DV.up(dve.memset(gates[:, :, :], 0.0), "gz")
            for k in range(KD):
                PE.wait(dve, f"xT{k}")
                DV.up(dve.tensor_copy(xres[:, k, :], bank[k % 4][:, 0:TOK]), f"xres{k}")
            for k in range(KD):
                AC.wait(dve, f"xh{k}")
                DV.up(tt(xl[:, k, :], xres[:, k, :], xh[:, k, :], ALU.subtract), f"xl{k}")
            PE.wait(dve, "ba")
            DV.wait(dve, "gz")
            for i, at in ((B_, 0), (X_, 4)):
                dve.tensor_copy(gates[:, i, 0:8].rearrange("p (t h) -> p t h", h=H),
                                bank[6][:, 0:16].rearrange("p (t h) -> p t h", h=8)[:, :, at:at + 4])
                ins = dve.tensor_copy(gates[0:SMP, i, 8:12], bank[6][0:SMP, 16 + at:20 + at])
            DV.up(ins, "ba")

            split_lo(0, 0)
            AC.wait(dve, "par2")
            AC.wait(dve, "hist")
            with dve.Fori(0, 3) as i:
                for q in range(2):
                    if q == 0:
                        split_lo(i, 1)
                    else:
                        split_lo(i + 1, 0)
                    for r in range(4):
                        for jj in range(2):
                            c = 4 * i + (2 * q + jj)
                            if r == 0:
                                dve.wait_ge(s["rel_act"], 4 * i + (2 * q + jj + 5))
                            else:
                                dve.wait_ge(s["conv_step"], 16 * i + (8 * q + 2 * (r - 1) + jj + 1))
                            x = cin[:, bass.ds(c * WD + r, LD)]
                            y = qkv[:, bass.ds(c * WF, LD)]
                            w = par2[:, bass.ds(c + (PA_DN + 12 * r), 1)]
                            if r == 0:
                                ins = dve.tensor_scalar(y, x, w, None, ALU.mult)
                            else:
                                ins = dve.scalar_tensor_tensor(out=y, in0=x, scalar=w, in1=y, op0=ALU.mult, op1=ALU.add)
                            ins.then_inc(s["conv_step"], 1)
            with dve.Fori(3, SLOT_MIX) as i:
                split_lo(i, 1)
                split_lo(i + 1, 0)

            dve.wait_ge(s["wba_in"], 48)
            DV.wait(dve, "ba")
            dt3 = dtal[:, 0:1, :].to_broadcast([P, 3, H])
            g3 = [gates[:, i, :].rearrange("p (t h) -> p t h", h=H) for i in range(13)]
            DV.up(tt(g3[X_], g3[X_], dt3, ALU.add), "gxa")
            DV.wait(dve, "gxa")
            DV.up(dve.scalar_tensor_tensor(out=gates[:, NX, :], in0=gates[:, X_, :], scalar=-1.0, in1=gates[:, X_, :],
                                           op0=ALU.mult, op1=ALU.min), "gx")
            AC.wait(dve, "gexp")
            dve.tensor_scalar(gates[:, L1, :], gates[:, L1, :], 1.0, None, ALU.add)
            DV.up(dve.tensor_scalar(gates[:, EB, :], gates[:, EB, :], 1.0, None, ALU.add), "gone")
            DV.wait(dve, "gone")
            DV.up(dve.reciprocal(gates[:, BETA, :], gates[:, EB, :]), "beta")
            AC.wait(dve, "gln")
            DV.up(dve.scalar_tensor_tensor(out=gates[:, X_, :], in0=gates[:, X_, :], scalar=0.0, in1=gates[:, L1, :],
                                           op0=ALU.max, op1=ALU.add), "gsp")
            DV.wait(dve, "gsp")
            DV.up(dve.scalar_tensor_tensor(out=g3[G_], in0=g3[X_], scalar=-1.0, in1=dtal[:, 1:2, :].to_broadcast([P, 3, H]),
                                           op0=ALU.mult, op1=ALU.mult), "g")

            AC.wait(dve, "rn")
            for c in range(8):
                x = qkv[:, c * WF:c * WF + LD]
                ins = dve.scalar_tensor_tensor(out=x, in0=x, scalar=SCALE if c < 4 else 1.0, in1=l2n[:, c, :],
                                               op0=ALU.mult, op1=ALU.mult)
            DV.up(ins, "qknorm")
            DV.wait(dve, "qknorm")
            DV.up(dve.tensor_copy(smp.rearrange("p c (b s) -> p c b s", s=NT),
                                  qk3[:, :, 259:347].rearrange("p c (b s) -> p c b s", s=11)[:, :, :, 0:NT]), "qkn")

            DV.wait(dve, "g")
            for t, (_, n) in enumerate(TILES):
                bk = 4 * (t % 2)
                kkb, qkb, gcb, small = bank[bk], bank[bk + 1], bank[bk + 2], bank[bk + 3]
                up_, lo_ = tri(t)
                if t:
                    PE.wait(dve, f"cum{t - 1}")
                else:
                    PO.wait(dve, "consts")
                if t == 2:
                    tt(rtmp[0:SMP, 0:32].rearrange("p (h b) -> p h b", h=H), last(gate(G_, t, n), NB), mid(member, H), ALU.mult)
                DV.up(tt(t4(spr[0:n, 0:H * n]), mid(up_, H), last(gate(G_, t, n), n), ALU.mult), f"ug{t}")
                PE.wait(dve, f"cum{t}")
                dve.tensor_copy(gate(GC, t, n), small[0:n, 0:4])
                DV.up(dve.tensor_copy(gate(GL, t, n), small[0:n, 4:8]), f"gcl{t}")
                DV.wait(dve, f"gcl{t}")
                tt(t4(dsc[0][0:n, 0:H * n]), t4(gcb[0:n, 0:H * n]), last(gate(GC, t, n), n), ALU.subtract)
                DV.up(tt(gate(KD_, t, n), gate(GL, t, n), gate(GC, t, n), ALU.subtract), f"cumsb{t}")
                DV.wait(dve, f"cumsb{t}")
                DV.up(dve.tensor_scalar(dsc[1][0:n, 0:H * n], dsc[0][0:n, 0:H * n], 0.0, None, ALU.max), f"dmax{t}")
                DV.up(dve.tensor_scalar(dsc[0][0:n, 0:H * n], dsc[0][0:n, 0:H * n], 0.0, None, ALU.min), f"dmat{t}")
                AC.wait(dve, f"egc{t}")
                dve.scalar_tensor_tensor(out=gate(NBE, t, n), in0=gate(BETA, t, n), scalar=-1.0, in1=gate(EGC, t, n),
                                         op0=ALU.mult, op1=ALU.mult)
                AC.wait(dve, f"decay{t}")
                tt(t4(dsc[0][0:n, 0:H * n]), t4(dsc[0][0:n, 0:H * n]), mid(up_, H), ALU.mult)
                DV.up(tt(t4(dsc[1][0:n, 0:H * n]), t4(dsc[1][0:n, 0:H * n]), mid(lo_, H), ALU.mult), f"mask{t}")
                DV.wait(dve, f"mask{t}")
                PE.wait(dve, f"kk{t}")
                DV.up(tt(L_[t], kkb[0:n, 0:H * n], dsc[1][0:n, 0:H * n], ALU.mult), f"La{t}")
                DV.up(tt(IN[t], qkb[0:n, 0:H * n], dsc[0][0:n, 0:H * n], ALU.mult), f"intra{t}")
                DV.wait(dve, f"La{t}")
                DV.up(tt(t4(L_[t]), t4(L_[t]), last(gate(BETA, t, n), n), ALU.mult), f"L{t}")
                PE.wait(dve, f"tok{t}")
                tt(t4(ktok[0:n, t, :]), t4(kkb[0:n, :]), last(gate(KD_, t, n), HD), ALU.mult)
                DV.up(tt(t4(vtok[0:n, t, :]), t4(qkb[0:n, :]), last(gate(BETA, t, n), HD), ALU.mult), f"tok{t}")
                AC.wait(dve, f"egcb{t}")
                if t < 2:
                    DV.up(tt(qg[:, :, 128 * t:128 * t + 128], qk3[:, 0:4, 128 * t:128 * t + 128], t4(vnew[:, :]), ALU.mult), f"qg{t}")
                else:
                    kq5 = kq.rearrange("p (h b u t) -> p h b u t", h=H, b=NB, u=2)
                    for h in range(H):
                        dve.tensor_copy(kq5[:, h, :, 0, :], head(4 + h, 2).rearrange("p (b t) -> p b t", t=NT))
                        ins = tt(kq5[:, h, :, 1, :], head(h, 2).rearrange("p (b t) -> p b t", t=NT), vnew[:, 64 * h:64 * h + 64].rearrange("p (b t) -> p b t", t=NT),
                                 ALU.mult)
                    DV.up(ins, "qg2")

            for n, (l, t) in enumerate(INV):
                sz = TILES[t][1]
                w, u, v = ((0, 1, 2), (3, 4, 5), (6, 7, 7))[t]
                if l == 0:
                    PE.wait(dve, f"invw{n}")
                    PO.wait(dve, f"lm{n}")
                    tt(t4(TT[t]), mid(ident[0:sz, 0:sz], H), t4(bank[w][0:sz, 0:H * sz]), ALU.subtract)
                    DV.up(tt(t4(T_[t]), mid(ident[0:sz, 0:sz], H), t4(lmb[n % 2][0:sz, 0:H * sz]), ALU.subtract), f"inv{n}")
                else:
                    PE.wait(dve, f"invu{n}")
                    off = 256 if t == 2 else 0
                    tt(T_[t], T_[t], bank[u][0:sz, 0:H * sz], ALU.subtract)
                    DV.up(tt(TT[t], TT[t], bank[v][0:sz, off:off + H * sz], ALU.subtract), f"inv{n}")

            PE.wait(dve, "st0")
            DV.up(dve.tensor_copy(spr[:, :], bank[2][:, :]), "state0")
            PE.wait(dve, "ks1")
            DV.up(tt(t4(rtmp[:, :]), t4(bank[3][:, :]), last(gate(NBE, 1), HD), ALU.mult), "rhsa1")
            DV.wait(dve, "rhsa1")
            DV.up(tt(rtmp[:, :], rtmp[:, :], vtok[:, 1, :], ALU.add), "rhs1")
            PE.wait(dve, "st1")
            DV.up(tt(t4(spr[:, :]), t4(spr[:, :]), last(gate(EGL, 1), HD), ALU.mult), "statea")
            DV.wait(dve, "statea")
            DV.up(tt(spr[:, :], spr[:, :], bank[2][:, :], ALU.add), "state1")
            PE.wait(dve, "ks2")
            DV.up(tt(t4(rtmp[0:SMP, :]), t4(bank[6][0:SMP, :]), last(gate(NBE, 2, SMP), HD), ALU.mult), "rhsa2")
            DV.wait(dve, "rhsa2")
            DV.up(tt(rtmp[0:SMP, :], rtmp[0:SMP, :], vtok[0:SMP, 2, :], ALU.add), "rhs2")
            PE.wait(dve, "o2")
            qs = kq[:, 256:512].rearrange("p (h b t) -> p h b t", h=H, t=NT)
            DV.up(tt(oT[:, :, SEQ:TOK].rearrange("p h (b t) -> p h b t", t=NT),
                     bank[5][:, 0:256].rearrange("p (h b t) -> p h b t", h=H, t=NT), qs, ALU.add), "oT2")
            AC.wait(dve, "vnsb2")
            for h in range(H):
                if h:
                    PE.wait(dve, f"stS{h - 1}")
                DV.up(tt(vnm.rearrange("p (b v) -> p b v", v=HD), mid(vnew[0:SMP, 128 * h:128 * h + 128], NB),
                         last(member, HD), ALU.mult), f"vnm{h}")
                x = s0[:, NB * h:NB * h + NB, :]
                DV.up(tt(x, x, last(eglS[:, NB * h:NB * h + NB], HD), ALU.mult), f"s0g{h}")
                DV.wait(dve, f"s0g{h}")
                PE.wait(dve, f"stS{h}")
                y = x.rearrange("p b v -> p (b v)")
                bk = 0 if h % 2 else 2
                tt(y[:, 0:512], y[:, 0:512], bank[bk][:, :], ALU.add)
                DV.up(tt(y[:, 512:1024], y[:, 512:1024], bank[bk + 1][:, :], ALU.add), f"stS{h}")

            AC.wait(dve, "orn")
            DV.up(tt(oT, oT, qg[:, :, :], ALU.mult), "on1")
            DV.wait(dve, "on1")
            DV.up(dve.scalar_tensor_tensor(out=oT, in0=oT, scalar=vec(0, PA_NW), in1=zsb[:, :, :], op0=ALU.mult,
                                           op1=ALU.mult), "mixo")
            AC.wait(dve, "mixh_done")
            DV.up(tt(xl[:, 0:4, :], oT, xh[:, 0:4, :], ALU.subtract), "mixl_done")

            dve.wait_ge(s["stores"], 16 * 7)
            PE.wait(dve, "ps0")
            DV.up(dve.scalar_tensor_tensor(out=pl0, in0=t4(bank[0][:, :]), scalar=SCALE, in1=promptb[:, :, 128:256],
                                           op0=ALU.mult, op1=ALU.add), "plog0")
            PE.wait(dve, "ps1")
            for q in range(2):
                ins = dve.scalar_tensor_tensor(out=pl1[:, 2 * q:2 * q + 2, :],
                                               in0=bank[1 + q][:, :].rearrange("p (h c) -> p h c", h=2), scalar=SCALE,
                                               in1=promptb[:, 2 * q:2 * q + 2, :], op0=ALU.mult, op1=ALU.add)
            DV.up(ins, "plog1")
            for t, x in enumerate((pl0, pl1)):
                DV.wait(dve, f"plog{t}")
                DV.up(dve.tensor_reduce(pst[:, 2, 4 * t:4 * t + 4], x, AX.X, ALU.max), f"pmaxa{t}")
                DV.wait(dve, f"pmaxa{t}")
                DV.up(dve.tensor_scalar(pst[:, 0, 4 * t:4 * t + 4], pst[:, 2, 4 * t:4 * t + 4], -1.0, None, ALU.mult), f"pmax{t}")
            for t, x in enumerate((pl0, pl1)):
                AC.wait(dve, f"pexp{4 * t + 3}")
                DV.up(dve.reciprocal(pst[:, 2, 4 * t:4 * t + 4], pst[:, 1, 4 * t:4 * t + 4]), f"prec{t}")
                DV.wait(dve, f"prec{t}")
                DV.up(tt(x, x, last(pst[:, 2, 4 * t:4 * t + 4], 128 + 128 * t), ALU.mult), f"pnorm{t}")
            for t in range(2):
                AC.wait(dve, f"poh{t}")
                DV.up(tt(xl[:, 4:8, 128 * t:128 * t + 128], t4(bank[6 + t][:, :]), xh[:, 4:8, 128 * t:128 * t + 128],
                         ALU.subtract), f"pol{t}")

            dve.memset(spare(1), 0.0).then_inc(s["kT_v"], 1)
            with dve.Fori(0, NB) as b:
                for u in range(0, 16, 2):
                    dve.wait_ge(s["kT_mm"], 16 * b + (u + 1))
                    dve.tensor_copy(kT[0], bank[0][:, :]).then_inc(s["kT_v"], 1)
                dve.wait_ge(s["s_raw"], b + 2)
                dve.wait_ge(s["s_kept"], b + 1)
                dve.scalar_tensor_tensor(out=sbias, in0=sraw, scalar=SCALE, in1=pastb[:, :], op0=ALU.mult, op1=ALU.add)\
                   .then_inc(s["s_bias"], 1)
                dve.wait_ge(s["mT_mm"], b + 1)
                dve.tensor_reduce(mcol[:, 0, bass.ds(4 * b, 4)], t4(bank[5][:, :]), AX.X, ALU.max).then_inc(s["m_col"], 1)

            PE.wait(dve, "own")
            for i, m in enumerate((ownk, ownq)):
                ins = dve.scalar_tensor_tensor(out=owl[:, i, :], in0=bank[7][0:SMP, 256 * i:256 * i + 256], scalar=SCALE,
                                               in1=m[:, :, :].rearrange("p h c -> p (h c)"), op0=ALU.mult, op1=ALU.add)
            DV.up(ins, "owl")
            DV.wait(dve, "owl")
            DV.up(dve.tensor_reduce(mo[:, :], owl[:, 1, :].rearrange("p (h c) -> p h c", h=H), AX.X, ALU.max), "mo")
            DV.wait(dve, "mo")
            PO.wait(dve, "const1")
            DV.up(dve.tensor_reduce(pick8[:, :], ident[0:SMP, 0:SMP].rearrange("p (b t) -> p t b", t=NT), AX.X, ALU.add),
                  "pick8")
            DV.up(tt(mos[:, :, :], mid(mo[:, :], NB), last(member, H), ALU.mult), "mos")
            PE.wait(dve, "gates")
            DV.up(dve.tensor_copy(mcol[:, 1, :], bank[4][:, 0:32]), "gsb")
            row = [st32[:, i, :] for i in range(10)]
            PE.wait(dve, "statT")
            dve.tensor_copy(row[8][:, 16:24], bank[7][0:32, 0:8])
            DV.up(dve.tensor_copy(st32[:, 0:4, :].rearrange("p a c -> p (a c)"), bank[6][0:32, 0:256]), "statsb")
            DV.wait(dve, "statsb")

            def halves(i):
                v = st32[:, i:i + 2, :].rearrange("p a c -> p (a c)").rearrange("p (n u q) -> p u q n", u=2, q=NT)
                return v[:, 0], v[:, 1]

            def qn(x):
                return x.rearrange("p (q n) -> p q n", n=NBLK)

            g0, g1 = halves(0)
            m0, m1 = halves(2)
            DV.up(tt(qn(row[4]), g0, g1, ALU.add), "gate")
            DV.up(tt(qn(row[6]), m0, m1, ALU.max), "mblk")
            DV.wait(dve, "gate")
            for q in range(NT):
                gm = mid(row[4][:, 8 * q:8 * q + 8], NBLK)
                gn = last(row[4][:, 8 * q:8 * q + 8], NBLK)
                A = rkA[:, 64 * q:64 * q + 64].rearrange("p (n m) -> p n m", m=NBLK)
                B = rkB[:, 64 * q:64 * q + 64].rearrange("p (n m) -> p n m", m=NBLK)
                tt(A, gm, gn, ALU.is_gt)
                ins = tt(B, gm, gn, ALU.is_equal)
            DV.up(ins, "rk1")
            DV.wait(dve, "rk1")
            lt = ltri[:, :, :].rearrange("p n m -> p (n m)")
            DV.up(tt(rkB[:, :].rearrange("p (q c) -> p q c", q=NT), rkB[:, :].rearrange("p (q c) -> p q c", q=NT), mid(lt, NT),
                     ALU.mult), "rk2")
            DV.wait(dve, "rk2")
            DV.up(tt(rkA[:, :], rkA[:, :], rkB[:, :], ALU.add), "rk3")
            DV.wait(dve, "rk3")
            DV.up(dve.tensor_reduce(row[9], rkA[:, :].rearrange("p (c m) -> p c m", m=NBLK), AX.X, ALU.add), "rank")
            DV.wait(dve, "rank")
            DV.up(dve.tensor_scalar(row[5], row[9], TOPK - 0.5, NEG, ALU.is_gt, ALU.mult), "pen")
            DV.wait(dve, "pen")
            DV.up(tt(row[6], row[6], row[5], ALU.add), "mpen")
            DV.wait(dve, "mpen")
            DV.up(dve.tensor_reduce(row[8][:, 0:8], qn(row[6]), AX.X, ALU.max), "mt")
            DV.wait(dve, "mt")
            DV.up(tt(row[8][:, 8:16], row[8][:, 0:8], row[8][:, 16:24], ALU.max), "mtot")
            DV.wait(dve, "mtot")
            DV.up(tt(row[7].rearrange("p (n q) -> p q n", q=NT), qn(row[5]), last(row[8][:, 8:16], NBLK), ALU.subtract), "shift")
            DV.wait(dve, "shift")
            id32 = ident[0:32, 0:32]
            dve.wait_ge(s["s_kept"], NB + 1)
            DV.up(tt(rc.rearrange("p (a c) -> p a c", a=32), mid(row[7], 32), last(id32, 64), ALU.mult), "rc")
            DV.up(tt(rm[:, :].rearrange("p (a c) -> p a c", a=32), mid(row[8][:, 8:16], 32), last(id32, NT), ALU.mult), "rm")
            for j in range(4):
                PE.wait(dve, f"c{j}")
                x = sx[:, 1024 * j:1024 * j + 1024].rearrange("p (a u q) -> p a u q", u=2, q=NT)
                sh = bank[j][:, :].rearrange("p (a q) -> p a q", q=NT)
                tt(x[:, :, 0, :], x[:, :, 0, :], sh, ALU.add)
                DV.up(tt(x[:, :, 1, :], x[:, :, 1, :], sh, ALU.add), f"z{j}")
            PE.wait(dve, "mb")
            DV.up(tt(owl[:, 0, :].rearrange("p (h b t) -> p h b t", h=H, t=NT),
                     owl[:, 0, :].rearrange("p (h b t) -> p h b t", h=H, t=NT),
                     bank[4][0:SMP, 0:256].rearrange("p (b h t) -> p h b t", h=H, t=NT), ALU.subtract), "ownz")
            for j in range(4):
                AC.wait(dve, f"pexpS{j}")
                x = sx[:, 1024 * j:1024 * j + 1024].rearrange("p (a g q) -> p a q g", g=NPG, q=NT)
                DV.up(dve.tensor_reduce(dsum[:, 64 * j:64 * j + 64].rearrange("p (a q) -> p a q", q=NT), x, AX.X, ALU.add),
                      f"dsum{j}")
            PE.wait(dve, "den")
            DV.up(dve.reciprocal(drec[:, :], bank[5][:, 0:256]), "drec")
            DV.wait(dve, "drec")
            dve.wait_ge(s["ov_mm"], 4 * NB)
            DV.up(tt(ovn[:, :].rearrange("p (h b t) -> p h b t", h=H, t=NT),
                     bank[6][:, 0:256].rearrange("p (h b t) -> p h b t", h=H, t=NT),
                     drec[:, :].rearrange("p (b h t) -> p h b t", h=H, t=NT), ALU.mult), "ovn")
            AC.wait(dve, "attn_endh")
            DV.up(tt(xl[:, 4:8, SEQ:TOK], ovn[:, :].rearrange("p (h c) -> p h c", h=H), xh[:, 4:8, SEQ:TOK], ALU.subtract),
                  "attn_end")

            def residual(n, m, slot):
                chunk(slot, m % 4)
                DV.up(dve.scalar_tensor_tensor(out=xres[:, m, :], in0=xres[:, m, :], scalar=ALPHA, in1=bank[m % 4][:, 0:TOK],
                                               op0=ALU.mult, op1=ALU.add), f"r{n}_{m}")

            def norm(n):
                AC.wait(dve, f"msq{n}")
                DV.up(tt(lnt[:, 3, :], bank[5][:, 0:TOK], lnt[:, 2, :], ALU.subtract), f"vara{n}")
                DV.wait(dve, f"vara{n}")
                DV.up(dve.tensor_scalar(lnt[:, 3, :], lnt[:, 3, :], 0.0, LN_EPS, ALU.max, ALU.add), f"var{n}")
                AC.wait(dve, f"rstd{n}")
                DV.up(tt(lnt[:, 4, :], bank[4][:, 0:TOK], lnt[:, 3, :], ALU.mult), f"bm{n}")
                DV.wait(dve, f"bm{n}")
                for m in range(KD + 1):
                    if m < KD:
                        if m >= 2:
                            AC.wait(dve, f"ln{n}_{m - 2}")
                        DV.up(tt(hraw[:, m % 2, :], xres[:, m, :], lnt[:, 3, :], ALU.mult), f"t1_{n}_{m}")
                        DV.wait(dve, f"t1_{n}_{m}")
                        DV.up(tt(hraw[:, m % 2, :], hraw[:, m % 2, :], lnt[:, 4, :], ALU.subtract), f"t2_{n}_{m}")
                    if m and n < 3:
                        AC.wait(dve, f"lnh{n}_{m - 1}")
                        DV.up(tt(xl[:, m - 1, :], xres[:, m - 1, :], xh[:, m - 1, :], ALU.subtract), f"x{n}_{m - 1}")

            def out_proj(base, n):
                for i in range(SLOT_OUT):
                    split_lo(base + i, 1)
                    residual(n, 4 * i, base + i)
                    residual(n, 4 * i + 1, base + i)
                    split_lo(base + i + 1, 0)
                    residual(n, 4 * i + 2, base + i)
                    residual(n, 4 * i + 3, base + i)

            def down(layer, n):
                for i in range(2):
                    for k in range(3):
                        slot = S_DOWN[layer] + 3 * i + k
                        split_lo(slot, 1)
                        if k == 2:
                            residual(n, 4 * i, slot)
                            residual(n, 4 * i + 1, slot)
                        if slot + 1 < S_END:
                            split_lo(slot + 1, 0)
                        if k == 2:
                            residual(n, 4 * i + 2, slot)
                            residual(n, 4 * i + 3, slot)

            def convolve(c, w0, nch, y, i, jj, r, base):
                if r:
                    dve.wait_ge(s["conv_step"], 6 * i + (base + 2 * (r - 1) + jj + 1))
                x = cb[:, bass.ds(c * WF + r, LF)]
                w = par2[:, bass.ds(c + (w0 + nch * r), 1)]
                if r == 0:
                    ins = dve.tensor_scalar(y, x, w, None, ALU.mult)
                else:
                    ins = dve.scalar_tensor_tensor(out=y, in0=x, scalar=w, in1=y, op0=ALU.mult, op1=ALU.add)
                ins.then_inc(s["conv_step"], 1)

            def padded(x):
                return x.rearrange("p (b s) -> p b s", s=10)[:, :, 0:NT]

            def feed_forward(layer):
                base = S_UP[layer]
                w0 = P + PB_F if layer == 0 else 2 * P
                with dve.Fori(0, SLOT_FFN) as i:
                    split_lo(i + base, 1)
                    for r in range(3):
                        for j in (0, 1):
                            if r == 0:
                                dve.wait_ge(s["rel_act"], 2 * i + (REL[layer] + j + 1))
                            convolve(2 * i + j, w0, KF, acc[:, WF * j:WF * j + LF], i, j, r, CONV[layer])
                    split_lo(i + (base + 1), 0)
                    for j in (0, 1):
                        dve.wait_ge(s["gelu_done"], 2 * i + (KF * layer + j + 1))
                        chunk(i + base, 2 + j)
                        tt(hraw[:, j, 0:SEQ], acc[:, WF * j:WF * j + SEQ], bank[2 + j][:, 0:SEQ], ALU.mult)
                        tt(hraw[:, j, SEQ:TOK].rearrange("p (b t) -> p b t", t=NT), padded(acc[:, WF * j + 258:WF * j + 338]),
                           bank[2 + j][:, SEQ:TOK].rearrange("p (b t) -> p b t", t=NT), ALU.mult).then_inc(s["h_done"], 1)
                    for j in (0, 1):
                        dve.wait_ge(s["hh_done"], 2 * i + (KF * layer + j + 1))
                        tt(hl[:, bass.ds(2 * i + j, 1), :], hraw[:, j:j + 1, :], hh[:, bass.ds(2 * i + j, 1), :], ALU.subtract)\
                            .then_inc(s["hid_ready"], 1)

            out_proj(S_OUT, 0)
            norm(0)
            AC.wait(dve, "f0_hist")
            feed_forward(0)
            down(0, 1)
            norm(1)
            AC.wait(dve, "sc_hist")
            with dve.Fori(0, 4) as i:
                split_lo(i + S_SC, 1)
                split_lo(i + (S_SC + 1), 0)
                for j in (0, 1):
                    dve.wait_ge(s["rel_act"], 2 * i + (REL_SC + j + 1))
                    chunk(i + S_SC, 2 + j)
                    tt(cb[:, bass.ds((2 * i + j) * WF + 2, SEQ)], hraw[:, j, 0:SEQ], bank[2 + j][:, 0:SEQ], ALU.mult)
                    tt(cb[:, bass.ds((2 * i + j) * WF + 258, 80)].rearrange("p (b s) -> p b s", s=10)[:, :, 2:10],
                       hraw[:, j, SEQ:TOK].rearrange("p (b t) -> p b t", t=NT),
                       bank[2 + j][:, SEQ:TOK].rearrange("p (b t) -> p b t", t=NT), ALU.mult).then_inc(s["sc_prod"], 1)
                for r in range(3):
                    for j in (0, 1):
                        if r == 0:
                            dve.wait_ge(s["sc_prod"], 2 * i + (j + 3))
                        convolve(2 * i + j, PA_SC, KD, cb[:, bass.ds((2 * i + j) * WF + KD * WF, LF)], i, j, r, CONV_SC)
            dve.wait_ge(s["conv_step"], CONV_SC + 24)
            for i in range(2):
                n = S_SC + 4 + i
                split_lo(n, 1)
                for j in range(4):
                    m = 4 * i + j
                    if j == 2:
                        split_lo(n + 1, 0)
                    chunk(n, j)
                    if m >= 2:
                        AC.wait(dve, f"sch{m - 2}")
                    y = cb[:, (KD + m) * WF:(KD + m) * WF + WF]
                    tt(hraw[:, m % 2, 0:SEQ], y[:, 0:SEQ], bank[j][:, 0:SEQ], ALU.mult)
                    DV.up(tt(hraw[:, m % 2, SEQ:TOK].rearrange("p (b t) -> p b t", t=NT), padded(y[:, 258:338]),
                             bank[j][:, SEQ:TOK].rearrange("p (b t) -> p b t", t=NT), ALU.mult), f"scp{m}")
                    AC.wait(dve, f"sch{m}")
                    DV.up(tt(hl[:, m, :], hraw[:, m % 2, :], hh[:, m, :], ALU.subtract), f"schl{m}")
            DV.up(dve.memset(spare(1), 0.0), "sc_gated")
            out_proj(S_SCO, 2)
            norm(2)
            AC.wait(dve, "f1_hist")
            feed_forward(1)
            down(1, 3)
            norm(3)

        @block.tensor
        def _(pe):
            def mm(out, lhsT, rhs, start=True, stop=True, **kw):
                return pe.matmul(out, lhsT, rhs, start=start, stop=stop, **kw)

            PO.wait(pe, "ident_done")
            PO.wait(pe, "const1")
            pe.wait_ge(s["xtok_in"], 32)
            for k in range(KD):
                if k >= 4:
                    DV.wait(pe, f"xres{k - 4}")
                for t, (at, n) in enumerate(TILES):
                    ins = pe.transpose(bank[k % 4][:, at:at + n], xtok[0:n, t, P * k:P * k + P], ident[0:n, 0:n])
                    if t == 0 and k < CREDIT:
                        ins.then_inc(s["chunk_done"], 1)
                PE.up(ins, f"xT{k}")
            pe.wait_ge(s["params_in"], 16 * 9)
            for i, n in enumerate((PA_N, PB_N, PC_N)):
                ins = pe.transpose(bank[4][:, 128 * i:128 * i + n], prows[0:n, i, :], ident[0:n, 0:n])
            PE.up(ins, "parT")
            pe.wait_ge(s["hist_in"], 16)
            for c in range(12):
                ins = pe.transpose(bank[5][:, 24 * c:24 * c + 24], dnrows[0:24, P * c:P * c + P], ident[0:24, 0:24])
            PE.up(ins, "histT")
            pe.wait_ge(s["wba_in"], 48)
            DV.wait(pe, "xres7")
            for t, (at, n) in enumerate(TILES):
                for k in range(KD):
                    ins = mm(bank[6][0:n, 8 * t:8 * t + 8], xres[:, k, at:at + n], wba[:, k, :], k == 0, k == KD - 1)
            PE.up(ins, "ba")

            def project(n, xa, xb, nk, free, ready, k0=0, start=True, stop=True):
                for p in range(2):
                    pe.wait_ge(s["lo_done"], 2 * n + (p + 1))
                    for c in range(2):
                        j = 2 * p + c
                        if start:
                            free(j)
                        for k in range(nk):
                            if j == 0:
                                ready(k0 + k)
                            out = bank[j][:, 0:TOK]
                            w, v = hi[:, p, k, P * c:P * c + P], lo[:, p, k, P * c:P * c + P]
                            mm(out, w, xa[:, k0 + k, :], start and k == 0, False)
                            mm(out, w, xb[:, k0 + k, :], False, False)
                            ins = mm(out, v, xa[:, k0 + k, :], False, stop and k == nk - 1)
                        ins.then_inc(s["chunk_done"], 1)

            with pe.Fori(0, SLOT_MIX) as i:
                project(i, xh, xl, KD, lambda j: pe.wait_ge(s["rel_act"], 4 * i + (j + 1)), lambda k: DV.wait(pe, f"xl{k}"))
            AC.wait(pe, "par2")
            AC.wait(pe, "hist")
            DV.wait(pe, "ba")
            PO.wait(pe, "dnlast")
            for g in range(3):
                for c in range(4):
                    ins = pe.transpose(bank[4 + g][0:27, P * c:P * c + P], iof[:, 27 * (4 * g + c):27 * (4 * g + c) + 27],
                                       ident[:, :])
                PE.up(ins, f"dntail{g}")

            for c in range(8):
                AC.wait(pe, f"l2sq{c}")
                if c >= 4:
                    AC.wait(pe, f"ssln{c - 4}")
                elif c == 0:
                    pe.wait_ge(s["rel_act"], 32)
                PE.up(mm(bank[c % 4][:, 0:LD], ones[:, :], l2s(c)), f"ss{c}")

            for t, (at, n) in enumerate(TILES):
                bk = 4 * (t % 2)
                kkb, qkb, gcb, small = bank[bk], bank[bk + 1], bank[bk + 2], bank[bk + 3]
                up_ = tri(t)[0]
                DV.wait(pe, f"ug{t}")
                if t == 0:
                    AC.wait(pe, "ssln7")
                if t == 1:
                    AC.wait(pe, "dntail2")
                if t == 2:
                    DV.wait(pe, "tok0")
                    AC.wait(pe, "decay0")
                mm(gcb[:, 0:H * n], ones[0:n, :], spr[0:n, 0:H * n])
                mm(small[0:n, 0:4], up_, gate(G_, t, n))
                if t < 2:
                    ins = mm(small[:, 4:8], ones[0:n, :], gate(G_, t, n))
                else:
                    mm(small[0:n, 4:8], same8[:, :], gate(G_, t, n))
                    ins = mm(small[:, 8:40], ones[0:n, :], rtmp[0:n, 0:32])
                PE.up(ins, f"cum{t}")
                DV.wait(pe, "qkn")
                for h in range(H):
                    mm(kkb[0:n, n * h:n * h + n], head(4 + h, t), head(4 + h, t))
                for h in range(H):
                    ins = mm(qkb[0:n, n * h:n * h + n], head(4 + h, t), head(h, t))
                PE.up(ins, f"kk{t}")
                DV.wait(pe, f"L{t}")
                DV.wait(pe, f"intra{t}")
                for h in range(H):
                    pe.transpose(kkb[0:n, P * h:P * h + P], head(4 + h, t), ident[:, :])
                for h in range(H):
                    ins = pe.transpose(qkb[0:n, P * h:P * h + P], head(8 + h, t), ident[:, :])
                PE.up(ins, f"tok{t}")

            BK = ((0, 1, 2), (3, 4, 5), (6, 7, 7))
            for l in range(7):
                todo = [(n, t) for n, (l_, t) in enumerate(INV) if l_ == l]
                for n, t in todo:
                    sz = TILES[t][1]
                    PO.wait(pe, f"lm{n}")
                    if l == 0:
                        DV.wait(pe, "tok2")
                        AC.wait(pe, "decay2")
                    else:
                        DV.wait(pe, f"inv{INV.index((l - 1, t))}")
                    for h in range(H):
                        ins = mm(bank[BK[t][0]][0:sz, sz * h:sz * h + sz], lmb[n % 2][0:sz, sz * h:sz * h + sz],
                                 ident[0:sz, 0:sz] if l == 0 else TT[t][:, sz * h:sz * h + sz])
                    PE.up(ins, f"invw{n}")
                if l:
                    for n, t in todo:
                        sz = TILES[t][1]
                        off = 256 if t == 2 else 0
                        AC.wait(pe, f"wsb{n}")
                        for h in range(H):
                            q = slice(sz * h, sz * h + sz)
                            mm(bank[BK[t][1]][0:sz, q], wsb[t][0:sz, q], T_[t][:, q])
                            ins = mm(bank[BK[t][2]][0:sz, off + sz * h:off + sz * h + sz], T_[t][:, q], wsb[t][0:sz, q])
                        PE.up(ins, f"invu{n}")

            for t in range(2):
                DV.wait(pe, f"inv{INV.index((6, t))}")
                rhs = vtok[:, 0, :] if t == 0 else rtmp[:, :]
                if t:
                    DV.wait(pe, "state0")
                    for h in range(H):
                        q = slice(P * h, P * h + P)
                        ins = mm(bank[3][:, q], head(4 + h, 1), spr[:, q])
                    PE.up(ins, "ks1")
                    DV.wait(pe, "rhs1")
                    AC.wait(pe, "oT0")
                for h in range(H):
                    q = slice(P * h, P * h + P)
                    ins = mm(bank[0][:, q], TT[t][:, q], rhs[:, q])
                PE.up(ins, f"vn{t}")
                AC.wait(pe, f"vnsb{t}")
                for h in range(H):
                    q = slice(P * h, P * h + P)
                    ins = mm(bank[1][:, q], vnew[:, q], IN[t][:, q], True, t == 0)
                    if t:
                        ins = mm(bank[1][:, q], spr[:, q], qg[:, h, P:2 * P], False, True)
                PE.up(ins, f"o{t}")
                for h in range(H):
                    q = slice(P * h, P * h + P)
                    ins = mm(bank[2][:, q], ktok[:, t, q], vnew[:, q])
                PE.up(ins, f"st{t}")
            pe.wait_ge(s["s0_in0"], 64)
            DV.wait(pe, "qg2")
            for i in range(32):
                ins = mm(bank[4][:, 16 * i:16 * i + 16], s0[:, i, :], kq[:, 16 * i:16 * i + 16])
            PE.up(ins, "ksT")
            AC.wait(pe, "ksTsb")
            for h in range(H):
                ins = pe.transpose(bank[6][0:SMP, P * h:P * h + P], kq[:, SMP * h:SMP * h + SMP], ident[:, :])
            PE.up(ins, "ks2")
            DV.wait(pe, "rhs2")
            for h in range(H):
                ins = mm(bank[7][0:SMP, P * h:P * h + P], TT[2][:, SMP * h:SMP * h + SMP], rtmp[0:SMP, P * h:P * h + P])
            PE.up(ins, "vn2")
            AC.wait(pe, "vnsb2")
            for h in range(H):
                ins = mm(bank[5][:, SMP * h:SMP * h + SMP], vnew[0:SMP, P * h:P * h + P], IN[2][:, SMP * h:SMP * h + SMP])
            PE.up(ins, "o2")
            for h in range(H):
                DV.wait(pe, f"vnm{h}")
                if h == 0:
                    DV.wait(pe, "state1")
                if h == 1:
                    AC.wait(pe, "oT1")
                if h >= 2:
                    DV.wait(pe, f"stS{h - 2}")
                bk = 0 if h % 2 else 2
                mm(bank[bk][:, :], ktok[0:SMP, 2, P * h:P * h + P], vnm[:, 0:512])
                PE.up(mm(bank[bk + 1][:, :], ktok[0:SMP, 2, P * h:P * h + P], vnm[:, 512:1024]), f"stS{h}")
            for h in range(H):
                AC.wait(pe, f"osq{h}")
                DV.wait(pe, "stS3")
                PE.up(mm(bank[h][:, 0:TOK], ones[:, :], qg[:, h, :]), f"oss{h}")

            for i in range(6):
                at, n = TILES[i % 3]
                if i < 4:
                    AC.wait(pe, f"oln{i}")
                for h in range(H):
                    ins = pe.transpose(bank[i][0:n, P * h:P * h + P], mbh[:, 4 + 4 * (i // 3) + h, at:at + n], ident[:, :])
                PE.up(ins, f"kvT{i}")
            AC.wait(pe, "kvtok0")
            for h in range(H):
                ins = mm(bank[0][:, P * h:P * h + P], mbh[:, h, 0:P], mbh[:, 4 + h, 0:P])
            PE.up(ins, "ps0")
            AC.wait(pe, "kvtok2")
            for h in range(H):
                ins = mm(bank[1 + h // 2][:, 256 * (h % 2):256 * (h % 2) + 256], mbh[:, h, P:2 * P], mbh[:, 4 + h, 0:2 * P])
            PE.up(ins, "ps1")
            AC.wait(pe, "kvtok5")
            for g, (x, c0, t) in enumerate(((pl0, 0, 0), (pl1, 0, 1), (pl1, P, 1))):
                DV.wait(pe, f"pnorm{t}")
                for h in range(H):
                    ins = pe.transpose(bank[3 + g][:, P * h:P * h + P], x[:, h, c0:c0 + P], ident[:, :])
                PE.up(ins, f"pT{g}")
            for t in range(2):
                AC.wait(pe, f"pTsb{2 * t}")
                for h in range(H):
                    for c in range(t + 1):
                        ins = mm(bank[6 + t][:, P * h:P * h + P], kvtok[:, 1, c, P * h:P * h + P],
                                 pT[:, 512 * (t + c) + P * h:512 * (t + c) + P * h + P], c == 0, c == t)
                PE.up(ins, f"po{t}")

            DV.wait(pe, "pol1")
            for i in range(2):
                for h in range(H):
                    k_, q_ = mbh[:, 4 + h, SEQ:TOK], mbh[:, h, SEQ:TOK]
                    ins = mm(bank[7][0:SMP, 256 * i + SMP * h:256 * i + SMP * h + SMP], *((k_, q_), (q_, k_))[i])
            PE.up(ins, "own")
            with pe.Fori(0, NB) as b:
                def unit_transpose(u):
                    g, h = divmod(u, H)
                    pe.wait_ge(s[f"k_in{g}"], 64 * b + 64)
                    pe.wait_ge(s["kT_v"] if u % 2 == 0 else s["kT_a"], 8 * b + (u // 2 + 1))
                    for j in range(4):
                        ins = pe.transpose(bank[u % 2][:, P * j:P * j + P], kring[:, g, j, P * h:P * h + P], ident[:, :])
                    ins.then_inc(s["kT_mm"], 1)

                unit_transpose(0)
                for u in range(16):
                    if u < 15:
                        unit_transpose(u + 1)
                    g, h = divmod(u, H)
                    pe.wait_ge(s["kT_v"] if u % 2 == 0 else s["kT_a"], 8 * b + (u // 2 + 2))
                    if u == 0:
                        pe.wait_ge(s["s_raw"], b + 1)
                    for j in range(4):
                        at = P * h + NT * (4 * g + j)
                        ins = mm(bank[2][:, at:at + NT], kT[u % 2][:, P * j:P * j + P],
                                 mb[:, bass.ds(b * NT + (TOK * h + SEQ), NT)])
                ins.then_inc(s["s_mm"], 1)
                pe.wait_ge(s["s_raw"], b + 2)
                for h in range(H):
                    ins = mm(bank[4][:, bass.ds(4 * b + h, 1)], sraw[:, P * h:P * h + P], ones[:, 0:1])
                pe.wait_ge(s["s_bias"], b + 1)
                for h in range(H):
                    ins = pe.transpose(bank[5][:, P * h:P * h + P], sbias[:, P * h:P * h + P], ident[:, :])
                ins.then_inc(s["mT_mm"], 1)
            PE.up(mm(bank[3][:, 0:1], ones[:, :], ones[:, 0:1]), "gates")
            DV.wait(pe, "gsb")
            pe.wait_ge(s["m_col"], NB)
            pe.transpose(bank[6][0:32, 0:P], mcol[:, 1, :], ident[:, :])
            pe.transpose(bank[6][0:32, P:2 * P], mcol[:, 0, :], ident[:, :])
            DV.wait(pe, "mos")
            PO.wait(pe, "consts")
            DV.wait(pe, "pick8")
            PE.up(mm(bank[7][0:32, 0:8], mos[:, :, :].rearrange("p b h -> p (b h)"), pick8[:, :]), "statT")
            DV.wait(pe, "rc")
            for j in range(4):
                PE.up(mm(bank[j][:, :], ones[0:32, :], rc[:, 512 * j:512 * j + 512]), f"c{j}")
            DV.wait(pe, "rm")
            PE.up(mm(bank[4][:, 0:256], ones[0:32, :], rm[:, :]), "mb")
            AC.wait(pe, "ownexp")
            for h in range(H):
                mm(bank[6][:, SMP * h:SMP * h + SMP], kvtok[0:SMP, 1, 2, P * h:P * h + P], owl[:, 0, SMP * h:SMP * h + SMP],
                   h == 0, False, skip_group_check=True)
            DV.wait(pe, "dsum3")
            mm(bank[5][:, 0:256], ones[:, :], dsum[:, :], True, False)
            PE.up(mm(bank[5][:, 0:256], ones[0:SMP, :], owl[:, 0, :].rearrange("p (h b t) -> p b h t", h=H, t=NT), False, True),
                  "den")
            with pe.Fori(0, NB) as b:
                for g in range(4):
                    pe.wait_ge(s[f"k_in{g}"], 64 * b + (64 * NB + 64))
                    for j in range(4):
                        for h in range(H):
                            ins = mm(bank[6][:, bass.ds(8 * b + SMP * h, 8)], kring[:, g, j, P * h:P * h + P],
                                     sx[:, bass.ds(512 * b + (P * h + NT * (4 * g + j)), NT)], False, False,
                                     skip_group_check=True)
                    ins.then_inc(s["ov_mm"], 1)

            def stats(n):
                PO.wait(pe, f"accs{n}_6")
                mm(bank[4][:, 0:TOK], onesD[:, :], lnt[:, 0, :], True, False)
                DV.wait(pe, f"r{n}_7")
                mm(bank[4][:, 0:TOK], onesD[:, :], xres[:, 7, :], False, True)
                PO.wait(pe, f"accq{n}_6")
                mm(bank[5][:, 0:TOK], onesD[:, :], lnt[:, 1, :], True, False)
                AC.wait(pe, f"sq{n}_7")
                PE.up(mm(bank[5][:, 0:TOK], onesD[:, :], sq[:, 1, :], False, True), f"stat{n}")

            hist_loads = [1]

            def history(name, n):
                hist_loads[0] += 1
                pe.wait_ge(s["hist_in"], 16 * hist_loads[0])
                for c in range(n):
                    ins = pe.transpose(bank[6][:, 16 * c:16 * c + 16], rows[32:48, P * c:P * c + P], ident[32:48, 32:48])
                PE.up(ins, f"{name}_hist")

            def tails(name, n):
                PO.wait(pe, f"{name}_last")
                for g in range((n + 3) // 4):
                    if g >= 2:
                        AC.wait(pe, f"{name}_tail{g - 2}")
                    for c in range(4 * g, min(n, 4 * g + 4)):
                        ins = pe.transpose(bank[4 + g % 2 * 3][0:18, P * (c % 4):P * (c % 4) + P],
                                           last2[:, 18 * c:18 * c + 18], ident[:, :])
                    PE.up(ins, f"{name}_tail{g}")

            def nothing(_):
                pass

            def feed_forward(layer, n):
                base = S_UP[layer]
                with pe.Fori(0, SLOT_FFN) as i:
                    def free(j):
                        if j < 2:
                            pe.wait_ge(s["rel_act"], 2 * i + (REL[layer] - 2 + j + 1))
                        else:
                            pe.wait_ge(s["h_done"], 2 * i + (KF * layer + j - 2 + 1))
                    project(i + base, xh, xl, KD, free, lambda k: DV.wait(pe, f"x{n - 1}_{k}"))
                pe.wait_ge(s["h_done"], KF * (layer + 1) + 2)
                tails(f"f{layer}", KF)
                for i in range(2):
                    for k in range(3):
                        nk = min(KD, KF - KD * k)

                        def free(j):
                            if i:
                                DV.wait(pe, f"r{n}_{j}")
                        project(S_DOWN[layer] + 3 * i + k, hh, hl, nk, free,
                                lambda q: pe.wait_ge(s["hid_ready"], KF * layer + q + 1), KD * k, k == 0, k == 2)
                stats(n)

            def out_proj(base, xa, xb, ready, n, free0):
                for i in range(SLOT_OUT):
                    project(base + i, xa, xb, KD, free0 if i == 0 else lambda j: DV.wait(pe, f"r{n}_{j}"), ready)
                stats(n)

            DV.wait(pe, "attn_end")
            history("f0", KF)
            out_proj(S_OUT, xh, xl, nothing, 0, nothing)
            feed_forward(0, 1)
            history("sc", KD)
            with pe.Fori(0, 4) as i:
                def free(j):
                    if j < 2:
                        pe.wait_ge(s["rel_act"], 2 * i + (REL_SC - 2 + j + 1))
                    else:
                        pe.wait_ge(s["sc_prod"], 2 * i + (j - 2 + 1))
                project(i + S_SC, xh, xl, KD, free, lambda k: DV.wait(pe, f"x1_{k}"))
            for i in range(2):
                def free(j):
                    if i:
                        DV.wait(pe, f"scp{j}")
                    elif j < 2:
                        pe.wait_ge(s["rel_act"], REL_SC + KD)
                    else:
                        pe.wait_ge(s["sc_prod"], KD + 2)
                project(S_SC + 4 + i, xh, xl, KD, free, nothing)
            tails("sc", KD)
            out_proj(S_SCO, hh, hl, lambda k: DV.wait(pe, f"schl{k}"), 2, lambda j: DV.wait(pe, f"scp{4 + j}"))
            history("f1", KF)
            feed_forward(1, 3)
            for i in range(6):
                at, n = TILES[i // 2]
                for c in range(4):
                    m = 4 * (i % 2) + c
                    AC.wait(pe, f"ln3_{m}")
                    ins = pe.transpose(bank[i][0:n, P * c:P * c + P], xres[:, m, at:at + n], ident[:, :])
                PE.up(ins, f"yT{i}")



_INS = ["x_prompt", "x_sample", "cache_k", "cache_v", "state_dn", "state_dn_conv", "state_sc_conv", "state_ffn_conv",
        "page_table", "w_in_mix", "dn_conv_w", "dn_a_log", "dn_dt_bias", "dn_norm_w", "w_out_mix", "w_in_sc", "sc_conv_w",
        "w_out_sc", "ln_mix_g", "ln_mix_b", "w_up", "ffn_conv_w", "w_down", "ln_ffn_g", "ln_ffn_b"]
_OUTS = [("y_p", (1, SEQ, D)), ("y_s", (NB, NT, D)), ("k_p", (1, 1, SEQ, H, HD)), ("v_p", (1, 1, SEQ, H, HD)),
         ("k_s", (1, NB, NT, H, HD)), ("v_s", (1, NB, NT, H, HD)), ("dn_p", (1, 1, H, HD, HD)),
         ("dn_s", (1, NB, H, HD, HD)), ("dnc_p", (1, 1, 3, DNW)), ("dnc_s", (1, NB, 3, DNW)), ("scc_p", (1, 1, 2, D)),
         ("scc_s", (1, NB, 2, D)), ("ffc_p", (2, 1, 2, DFF)), ("ffc_s", (2, NB, 2, DFF))]


def kernel(**inputs):
    import numpy as np
    import concourse.bacc as bacc
    from concourse.bass_utils import run_bass_kernel_spmd as run

    nc = bacc.Bacc("TRN2", target_bir_lowering=False, num_devices=1)
    arrays = {n: np.ascontiguousarray(inputs[n]) for n in _INS}
    a = {n: nc.dram_tensor(n, x.shape, mybir.dt.from_np(x.dtype), kind="ExternalInput").ap() for n, x in arrays.items()}
    o = {n: nc.dram_tensor(n, shape, F32, kind="ExternalOutput").ap() for n, shape in _OUTS}
    trunk_program(nc, a, o)
    r = run(nc, [arrays], core_ids=[0])
    return tuple(r.results[0][n] for n, _ in _OUTS)
```

```python
from contextlib import ExitStack

import concourse.bass as bass
from concourse import mybir

F32 = mybir.dt.float32
F32R = mybir.dt.float32r
I32 = mybir.dt.int32
ALU = mybir.AluOpType
ACT = mybir.ActivationFunctionType
AX = mybir.AxisListType

P = 128
D = 1024
KD = D // P
SEQ, NB, NT = 256, 8, 8
SMP = NB * NT
TOK = SEQ + SMP
H, HD = 4, 128
PAST, PAGE, POOL = 2048, 128, 160
NPG = PAST // PAGE
BLK = 256
NBLK = PAST // BLK
TOPK = 3
DFF = 2816
KF = DFF // P
DNW = 3 * H * HD
ALPHA = 4.0 ** 0.25
SCALE = HD ** -0.5
LN_EPS, NORM_EPS = 1e-5, 1e-6
NEG = -1e30
SLOPES = [2.0 ** (-8.0 * (h + 1) / H) for h in range(H)]
TILES = [(0, 128), (128, 128), (256, 64)]

WD = 356
WF = 348
LD, LF = 344, 336

SLOT_MIX, SLOT_OUT, SLOT_FFN, SLOT_DOWN, SLOT_SC = 7, 2, KF // 2, 6, 6
S_MIX = 0
S_OUT = S_MIX + SLOT_MIX
S_UP = [S_OUT + SLOT_OUT]
S_DOWN = [S_UP[0] + SLOT_FFN]
S_SC = S_DOWN[0] + SLOT_DOWN
S_SCO = S_SC + SLOT_SC
S_UP.append(S_SCO + SLOT_OUT)
S_DOWN.append(S_UP[1] + SLOT_FFN)
S_END = S_DOWN[1] + SLOT_DOWN
CREDIT = 4

PA_DN, PA_SC, PA_LMG, PA_LMB, PA_NW, PA_N = 0, 48, 72, 88, 104, 105
PB_F, PB_LFG, PB_LFB, PB_N = 0, 66, 82, 98
PC_N = 66

SEMS = """
params_in xtok_in hist_in wba_in pt_in raw_in k_in0 k_in1 v_in0 v_in1 s0_in0 stores
hi_done lo_done chunk_done rel_act conv_step
kT_mm kT_hi kT_lo q_fp q_hi q_lo s_mm s_bias s_row s_max row shifted p_exp p_norm pT_mm pT_hi pT_lo
v_hi v_lo v_mm o_row
gelu_done h_done hh_done hid_ready sc_prod
pe_step act_step dve_step pool_step
""".split()


class Steps:

    def __init__(self, sem, names):
        self.sem, self.names, self.made = sem, names, []
        self.value = {n: i + 1 for i, n in enumerate(names)}

    def up(self, ins, name):
        self.made.append(name)
        assert self.names[len(self.made) - 1] == name, (name, len(self.made))
        ins.then_inc(self.sem, 1)

    def wait(self, eng, name):
        eng.wait_ge(self.sem, self.value[name])


STEPS = {
    "pe": """
xT0 xT1 xT2 xT3 xT4 xT5 xT6 xT7 parT histT ba dntail0 dntail1 dntail2 ss0 ss1 ss2 ss3 ss4 ss5 ss6 ss7 cum0 kk0 tok0
cum1 kk1 tok1 cum2 kk2 tok2 invw0 invw1 invw2 invw3 invw4 invw5 invu3 invu4 invu5 invw6 invw7 invw8 invu6 invu7 invu8
invw9 invw10 invu9 invu10 invw11 invw12 invu11 invu12 invw13 invw14 invu13 invu14 invw15 invw16 invu15 invu16 vn0 o0
st0 ks1 vn1 o1 st1 ksT ks2 vn2 o2 stS0 stS1 stS2 stS3 oss0 oss1 oss2 oss3 kvT0 kvT1 kvT2 kvT3 kvT4 kvT5 ps0 ps1 pT0
pT1 pT2 po0 po1 attn_mm f0_hist stat0 f0_tail0 f0_tail1 f0_tail2 f0_tail3 f0_tail4 f0_tail5 stat1 sc_hist sc_tail0
sc_tail1 stat2 f1_hist f1_tail0 f1_tail1 f1_tail2 f1_tail3 f1_tail4 f1_tail5 stat3 yT0 yT1 yT2 yT3 yT4 yT5
""".split(),
    "act": """
par0 par1 par2 xh0 xh1 xh2 xh3 xh4 xh5 xh6 xh7 hist silu dntail0 dntail1 dntail2 gexp gln l2sq0 l2sq1 l2sq2 ssln0
l2sq3 ssln1 l2sq4 ssln2 l2sq5 ssln3 l2sq6 ssln4 l2sq7 ssln5 ssln6 ssln7 rn egc0 egcb0 decay0 egc1 egcb1 decay1 egc2
egcb2 decay2 wsb3 wsb4 wsb5 wsb6 wsb7 wsb8 wsb9 wsb10 wsb11 wsb12 wsb13 wsb14 wsb15 wsb16 vnsb0 oT0 vnsb1 oT1 ksTsb
vnsb2 osq0 osq1 osq2 osq3 oln0 oln1 oln2 oln3 orn mixh_done kvtok0 kvtok1 kvtok2 kvtok3 kvtok4 kvtok5 pexp0 pexp1
pexp2 pexp3 pexp4 pexp5 pexp6 pexp7 pTsb0 pTsb1 pTsb2 poh0 poh1 voh attn_endh sq0_0 sq0_1 sq0_2 sq0_3 sq0_4 sq0_5
sq0_6 sq0_7 msq0 lnv0 rstd0 ln0_0 lnh0_0 ln0_1 lnh0_1 ln0_2 lnh0_2 ln0_3 lnh0_3 ln0_4 lnh0_4 ln0_5 lnh0_5 ln0_6 lnh0_6
ln0_7 lnh0_7 f0_hist f0_tail0 f0_tail1 f0_tail2 f0_tail3 f0_tail4 f0_tail5 sq1_0 sq1_1 sq1_2 sq1_3 sq1_4 sq1_5 sq1_6
sq1_7 msq1 lnv1 rstd1 ln1_0 lnh1_0 ln1_1 lnh1_1 ln1_2 lnh1_2 ln1_3 lnh1_3 ln1_4 lnh1_4 ln1_5 lnh1_5 ln1_6 lnh1_6 ln1_7
lnh1_7 sc_hist sch0 sch1 sch2 sch3 sch4 sch5 sch6 sch7 sc_tail0 sc_tail1 sq2_0 sq2_1 sq2_2 sq2_3 sq2_4 sq2_5 sq2_6
sq2_7 msq2 lnv2 rstd2 ln2_0 lnh2_0 ln2_1 lnh2_1 ln2_2 lnh2_2 ln2_3 lnh2_3 ln2_4 lnh2_4 ln2_5 lnh2_5 ln2_6 lnh2_6 ln2_7
lnh2_7 f1_hist f1_tail0 f1_tail1 f1_tail2 f1_tail3 f1_tail4 f1_tail5 sq3_0 sq3_1 sq3_2 sq3_3 sq3_4 sq3_5 sq3_6 sq3_7
msq3 lnv3 rstd3 ln3_0 ln3_1 ln3_2 ln3_3 ln3_4 ln3_5 ln3_6 ln3_7 y0 y1 y2 y3 y4 y5
""".split(),
    "dve": """
gz pages xres0 xres1 xres2 xres3 xres4 xres5 xres6 xres7 xl0 xl1 xl2 xl3 xl4 xl5 xl6 xl7 ba gxa gx gone beta gsp g
qknorm qkn ug0 gcl0 cumsb0 dmax0 dmat0 mask0 La0 intra0 L0 tok0 qg0 ug1 gcl1 cumsb1 dmax1 dmat1 mask1 La1 intra1 L1
tok1 qg1 ug2 gcl2 cumsb2 dmax2 dmat2 mask2 La2 intra2 L2 tok2 qg2 inv0 inv1 inv2 inv3 inv4 inv5 inv6 inv7 inv8 inv9
inv10 inv11 inv12 inv13 inv14 inv15 inv16 state0 rhsa1 rhs1 statea state1 rhsa2 rhs2 oT2 vnm0 s0g0 stS0 vnm1 s0g1 stS1
vnm2 s0g2 stS2 vnm3 s0g3 stS3 on1 mixo mixl_done plog0 plog1 pmaxa0 pmax0 pmaxa1 pmax1 prec0 pnorm0 prec1 pnorm1 pol0
pol1 vol rowc0 rowc attn_end r0_0 r0_1 r0_2 r0_3 r0_4 r0_5 r0_6 r0_7 vara0 var0 bm0 t1_0_0 t2_0_0 t1_0_1 t2_0_1 x0_0
t1_0_2 t2_0_2 x0_1 t1_0_3 t2_0_3 x0_2 t1_0_4 t2_0_4 x0_3 t1_0_5 t2_0_5 x0_4 t1_0_6 t2_0_6 x0_5 t1_0_7 t2_0_7 x0_6 x0_7
r1_0 r1_1 r1_2 r1_3 r1_4 r1_5 r1_6 r1_7 vara1 var1 bm1 t1_1_0 t2_1_0 t1_1_1 t2_1_1 x1_0 t1_1_2 t2_1_2 x1_1 t1_1_3
t2_1_3 x1_2 t1_1_4 t2_1_4 x1_3 t1_1_5 t2_1_5 x1_4 t1_1_6 t2_1_6 x1_5 t1_1_7 t2_1_7 x1_6 x1_7 scp0 schl0 scp1 schl1
scp2 schl2 scp3 schl3 scp4 schl4 scp5 schl5 scp6 schl6 scp7 schl7 sc_gated r2_0 r2_1 r2_2 r2_3 r2_4 r2_5 r2_6 r2_7
vara2 var2 bm2 t1_2_0 t2_2_0 t1_2_1 t2_2_1 x2_0 t1_2_2 t2_2_2 x2_1 t1_2_3 t2_2_3 x2_2 t1_2_4 t2_2_4 x2_3 t1_2_5 t2_2_5
x2_4 t1_2_6 t2_2_6 x2_5 t1_2_7 t2_2_7 x2_6 x2_7 r3_0 r3_1 r3_2 r3_3 r3_4 r3_5 r3_6 r3_7 vara3 var3 bm3 t1_3_0 t2_3_0
t1_3_1 t2_3_1 t1_3_2 t2_3_2 t1_3_3 t2_3_3 t1_3_4 t2_3_4 t1_3_5 t2_3_5 t1_3_6 t2_3_6 t1_3_7 t2_3_7
""".split(),
    "pool": """
const0 const1 ident_done const2 const3 cin_zero const4 const5 const6 const7 const8 const9 const10 const11 const12
const13 const14 const15 const16 const17 const18 const19 const20 const21 const22 const23 const24 const25 const26
const27 const28 const29 const30 const31 const32 const33 const34 const35 const36 const37 const38 const39 const40
const41 const42 const43 const44 const45 const46 const47 const48 const49 const50 const51 const52 const53 const54
const55 const56 const57 const58 consts dnlast lm0 lm1 lm2 lm3 lm4 lm5 lm6 lm7 lm8 lm9 lm10 lm11 lm12 lm13 lm14 lm15
lm16 f0_zero accs0_1 accq0_0 accq0_1 accs0_2 accq0_2 accs0_3 accq0_3 accs0_4 accq0_4 accs0_5 accq0_5 accs0_6 accq0_6
f0_last sc_zero accs1_1 accq1_0 accq1_1 accs1_2 accq1_2 accs1_3 accq1_3 accs1_4 accq1_4 accs1_5 accq1_5 accs1_6
accq1_6 sc_last f1_zero accs2_1 accq2_0 accq2_1 accs2_2 accq2_2 accs2_3 accq2_3 accs2_4 accq2_4 accs2_5 accq2_5
accs2_6 accq2_6 f1_last accs3_1 accq3_0 accq3_1 accs3_2 accq3_2 accs3_3 accq3_3 accs3_4 accq3_4 accs3_5 accq3_5
accs3_6 accq3_6
""".split(),
}


def trunk_program(nc, a, o):
    ctx = ExitStack()
    with ctx:
        def sb(name, shape, dt=F32, stack=ctx):
            return stack.enter_context(nc.sbuf_tensor(name, shape, dt))

        s = {n: ctx.enter_context(nc.semaphore(n)) for n in SEMS}
        bank = [ctx.enter_context(nc.psum_tensor(f"bank{i}", [P, 512], F32)) for i in range(8)]

        raw = sb("raw", [P, 2 * KD * 512])
        hi = sb("hi", [P, 2, KD, 256], F32R)
        lo = sb("lo", [P, 2, KD, 256], F32R)
        xh = sb("xh", [P, KD, TOK], F32R)
        xl = sb("xl", [P, KD, TOK], F32R)
        xres = sb("xres", [P, KD, TOK])
        par = sb("par", [P, 3, P])
        ident = sb("ident", [P, P])
        ptab = sb("ptab", [1, NB * NPG], I32)
        pair = sb("pair", [1, NB * NPG // 2], I32)
        ones = sb("ones", [P, P])
        onesD = sb("onesD", [P, P])
        eps6 = sb("eps6", [P, 2])
        scrap = sb("scrap", [P, 3, 8])

        sA = ExitStack()
        mb = sb("mb", [P, 12 * TOK], stack=sA)
        upper = sb("upper", [P, P], stack=sA)
        lower = sb("lower", [P, P], stack=sA)
        bdiff = sb("bdiff", [P, 7, P], stack=sA)
        same8 = sb("same8", [SMP, SMP], stack=sA)
        upper8 = sb("upper8", [SMP, SMP], stack=sA)
        lower8 = sb("lower8", [SMP, SMP], stack=sA)
        ltri = sb("ltri", [32, NBLK, NBLK], stack=sA)
        promptb = sb("promptb", [P, H, 256], stack=sA)
        c128 = sb("c128", [32, 128], stack=sA)
        back = sb("back", [32, NPG + 1], stack=sA)
        slope = sb("slope", [32, 1], stack=sA)
        ownb = sb("ownb", [32, 120], stack=sA)
        gates = sb("gates", [P, 14, 12], stack=sA)
        dtal = sb("dtal", [P, 2, H], stack=sA)
        s1 = ExitStack()
        zsb = sb("zsb", [P, H, TOK], stack=s1)
        qkv = sb("qkv", [P, 12 * WF], stack=s1)
        s11 = ExitStack()
        cin = sb("cin", [P, 12 * WD], stack=s11)
        xtok = sb("xtok", [P, 3, D], stack=s11)
        prows = sb("prows", [P, 3, P], stack=s11)
        dnrows = sb("dnrows", [64, DNW], stack=s11)
        wba = sb("wba", [P, KD, 8], stack=s11)
        iot = sb("iot", [P, 512], I32, stack=s11)
        iof = sb("iof", [P, 512], stack=s11)
        bs = sb("bs", [P, 8, P], stack=s11)
        s11.close()
        s2 = ExitStack()
        tP = sb("tP", [P, 2, 512], stack=s2)
        ttP = sb("ttP", [P, 2, 512], stack=s2)
        lP = sb("lP", [P, 2, 512], stack=s2)
        inP = sb("inP", [P, 2, 512], stack=s2)
        tS = sb("tS", [SMP, 256], stack=s2)
        ttS = sb("ttS", [SMP, 256], stack=s2)
        lS = sb("lS", [SMP, 256], stack=s2)
        inS = sb("inS", [SMP, 256], stack=s2)
        s0 = sb("s0", [P, 32, P], stack=s2)
        ktok = sb("ktok", [P, 3, 512], stack=s2)
        vtok = sb("vtok", [P, 3, 512], stack=s2)
        qg = sb("qg", [P, H, TOK], stack=s2)
        spr = sb("spr", [P, 512], stack=s2)
        rtmp = sb("rtmp", [P, 512], stack=s2)
        vnew = sb("vnew", [P, 512], stack=s2)
        eglS = sb("eglS", [P, 32], stack=s2)
        s2.close()
        s1.close()
        s3 = ExitStack()
        kring = sb("kring", [P, 2, 4, 512], stack=s3)
        vring = sb("vring", [P, 2, 4, 512], stack=s3)
        kTh = sb("kTh", [P, 2, 512], F32R, stack=s3)
        kTl = sb("kTl", [P, 2, 512], F32R, stack=s3)
        sbias = sb("sbias", [P, PAST + SMP], stack=s3)
        prob = sb("prob", [P, PAST + SMP], stack=s3)
        pTs = sb("pTs", [P, NPG + 1, 2, 32], F32R, stack=s3)
        kvtok = sb("kvtok", [P, 2, 3, 512], stack=s3)
        voh = sb("voh", [SMP, 512], F32R, stack=s3)
        vol = sb("vol", [SMP, 512], F32R, stack=s3)
        pst = sb("pst", [P, 3, 8], stack=s3)
        qpf = sb("qpf", [P, H, 32], stack=s3)
        qph = sb("qph", [P, H, 32], F32R, stack=s3)
        qpl = sb("qpl", [P, H, 32], F32R, stack=s3)
        twice = sb("twice", [SMP, 32], stack=s3)
        gsum = sb("gsum", [32, NBLK], stack=s3)
        bmax = sb("bmax", [32, NBLK + 1], stack=s3)
        pen = sb("pen", [32, NBLK + 1], stack=s3)
        shift = sb("shift", [32, NBLK + 1], stack=s3)
        dn = sb("dn", [32, NBLK + 1], stack=s3)
        rk = sb("rk", [32, 2, NBLK * NBLK], stack=s3)
        r1 = sb("r1", [32, 4], stack=s3)
        rank = sb("rank", [32, NBLK], stack=s3)
        s3.close()
        sA.close()

        hh = sb("hh", [P, KF, TOK], F32R)
        hl = sb("hl", [P, KF, TOK], F32R)
        cb = sb("cb", [P, KF * WF])
        rows = sb("rows", [64, DFF])
        acc = sb("acc", [P, 2 * WF])
        hraw = sb("hraw", [P, 2, TOK])
        sq = sb("sq", [P, 2, TOK])
        lnt = sb("lnt", [P, 5, TOK])

        step = {e: Steps(s[f"{e}_step"], STEPS[e]) for e in ("pe", "act", "dve", "pool")}
        PE, AC, DV, PO = step["pe"], step["act"], step["dve"], step["pool"]

        spares = [0, 0, 0]

        def spare(e):
            spares[e] += 1
            return scrap[:, e, spares[e] - 1:spares[e]]

        def t4(x, n=P):
            return x.rearrange("p (h c) -> p h c", h=H)

        def tri(t):
            return (upper[:], lower[:]) if t < 2 else (upper8[:], lower8[:])

        def mid(x, n):
            return x.rearrange("p (a c) -> p a c", a=1).to_broadcast([x.shape[0], n, x.shape[1]])

        def last(x, n):
            return x.rearrange("p (c a) -> p c a", a=1).to_broadcast([x.shape[0], x.shape[1], n])

        def gate(i, t, n=P):
            return gates[0:n, i, 4 * t:4 * t + 4]

        B_, X_, NX, L1, EB, BETA, G_, GC, EGC, NBE, KD_, GL, EGL = range(13)
        T_ = [tP[:, 0, :], tP[:, 1, :], tS[:]]
        TT = [ttP[:, 0, :], ttP[:, 1, :], ttS[:]]
        L_ = [lP[:, 0, :], lP[:, 1, :], lS[:]]
        IN = [inP[:, 0, :], inP[:, 1, :], inS[:]]
        member = same8[:, 0:SMP:NT]
        sc0 = s0[:, :, :].rearrange("p a c -> p (a c)")
        lmb = [sc0[:, 512 * i:512 * i + 512] for i in range(2)]
        wsb = [sc0[:, 1024:1536], sc0[:, 1536:2048], sc0[0:SMP, 2048:2304]]
        dsc = [sc0[:, 2304:2816], sc0[:, 2816:3328]]
        kq = qkv[:, 8 * WF:8 * WF + 512]
        vnm = tP[0:SMP, :, :].rearrange("p a c -> p (a c)")
        qk3 = qkv[:, :].rearrange("p (c w) -> p c w", w=WF)
        oT = qk3[:, 0:4, 0:TOK]
        INV = [(l, t) for l in range(7) for t in range(3) if t < 2 or l < 3]

        smp = sc0[:, 3328:4096].rearrange("p (c w) -> p c w", w=SMP)

        def head(c, t):
            return qk3[:, c, 128 * t:128 * t + 128] if t < 2 else smp[:, c, :]

        def weight(i):
            return raw[:, bass.ds(i % 2 * (KD * 512), KD * 512)].rearrange("p (k c) -> p k c", c=512)

        def vec(pack, row):
            return par[:, pack, row:row + 1]

        par2 = par[:, :, :].rearrange("p a c -> p (a c)")

        def l2s(c):
            return (rtmp, spr)[c % 2][:, 0:LD]

        l2n = sc0[:, 0:8 * LD].rearrange("p (c w) -> p c w", w=LD)
        pl0 = sbias[:, 0:512].rearrange("p (h c) -> p h c", h=H)
        pl1 = sbias[:, 512:1536].rearrange("p (h c) -> p h c", h=H)
        pT = prob[:, 0:1536]
        vh = hi[:, 1].rearrange("p k c -> p (k c)").rearrange("p (w j c) -> p w j c", w=2, c=512)
        vl = lo[:, 1].rearrange("p k c -> p (k c)").rearrange("p (w j c) -> p w j c", w=2, c=512)
        keyb = raw[0:32, 0:PAST]
        orow = raw[0:SMP, PAST:PAST + 512]
        UNITS, VUNITS = 16, 8

        def after(eng, sem, value):
            if not isinstance(value, int) or value > 0:
                eng.wait_ge(s[sem], value)

        last2 = lnt[:, 0:2, :].rearrange("p a c -> p (a c)")
        mbh = mb[:, :].rearrange("p (c w) -> p c w", w=TOK)
        CONV = [48, 48 + 3 * KF + 3 * KD]
        REL = [32, 32 + KF + KD]
        REL_SC, CONV_SC = 32 + KF, 48 + 3 * KF

        def hraw_y(t):
            return cb[0:TILES[t][1], D * t:D * t + D]

        block = ctx.enter_context(nc.Block())

        @block.sync
        def _(sp_):
            w_mix = a["w_in_mix"][0].rearrange("(k p) c -> p k c", p=P)
            w_out = a["w_out_mix"][0].rearrange("(k p) c -> p k c", p=P)
            w_sc = a["w_in_sc"][0].rearrange("(k p) c -> p k c", p=P)
            w_so = a["w_out_sc"][0].rearrange("(k p) c -> p k c", p=P)

            def slot_free(n):
                sp_.wait_ge(s["lo_done"], 2 * (n - 1))
                sp_.wait_ge(s["raw_in"], 32 * n)

            def load_whole(n, src, nk=KD):
                sp_.dma_start(weight(n)[:, 0:nk, :], src).then_inc(s["raw_in"], 32)

            sp_.dma_start(ptab[:, :], a["page_table"].rearrange("(a b) n -> a (b n)", a=1)).then_inc(s["pt_in"], 16)
            sp_.dma_start(xtok[:, 0:2, :], a["x_prompt"][0].rearrange("(t p) d -> p t d", p=P)).then_inc(s["xtok_in"], 16)
            sp_.dma_start(xtok[0:SMP, 2, :], a["x_sample"].rearrange("b t d -> (b t) d")).then_inc(s["xtok_in"], 16)
            for n in range(SLOT_MIX):
                if n == 1:
                    sp_.wait_ge(s["raw_in"], 32)
                if n > 1:
                    slot_free(n)
                c0 = 512 * n if n < 4 else 2056 + 512 * (n - 4)
                load_whole(n, w_mix[:, :, c0:c0 + 512])
            slot_free(S_OUT)
            load_whole(S_OUT, w_out[:, :, 0:512])

            AC.wait(sp_, "mixh_done")
            DV.wait(sp_, "mixl_done")
            DV.wait(sp_, "pages")
            sp_.wait_ge(s["stores"], 16 * 7)

            def load_pages(ring, cache, landed, b, g):
                words = [sp_.value_load(pair[0:1, bass.ds(b * (NPG // 2) + (2 * g + j), 1)], min_val=0,
                                        max_val=POOL * POOL - 1) for j in range(2)]
                return [(ring[:, g % 2, 2 * j + u, :], cache[bass.ds(x, 1)].rearrange("o p h d -> (o p) (h d)"), landed)
                        for j, w in enumerate(words) for u, x in enumerate((w % POOL, w // POOL))]

            def start(loads):
                for dst, src, landed in loads:
                    sp_.dma_start(dst, src).then_inc(s[landed], 16)

            def load_k(b, g):
                loads = load_pages(kring, a["cache_k"][0], f"k_in{g % 2}", b, g)
                after(sp_, "kT_mm", b * UNITS + 4 * (g - 1))
                start(loads)

            def load_v(b, g):
                loads = load_pages(vring, a["cache_v"][0], f"v_in{g % 2}", b, g)
                after(sp_, "v_lo", b * VUNITS + (2 * g - 2))
                start(loads)

            def pages(b, c, d, n):
                for g in range(2):
                    if d is not None:
                        load_v(d, 2 + g)
                    if b is not None:
                        load_k(b, 2 + g)
                for g in range(2):
                    if c is not None:
                        load_v(c, g)
                    if n is not None:
                        load_k(n, g)

            pages(None, None, None, 0)
            pages(0, None, None, 1)
            pages(1, 0, None, 2)
            with sp_.Fori(2, NB - 1) as b:
                pages(b, b - 1, b - 2, b + 1)
            pages(NB - 1, NB - 2, NB - 3, None)
            pages(None, NB - 1, NB - 2, None)
            pages(None, None, NB - 1, None)
            PE.wait(sp_, "attn_mm")
            slot_free(S_OUT + 1)
            load_whole(S_OUT + 1, w_out[:, :, 512:1024])

            def feed_forward(layer):
                w_up = a["w_up"][layer].rearrange("(k p) c -> p k c", p=P)
                w_dn = a["w_down"][layer].rearrange("(k p) c -> p k c", p=P)
                with sp_.Fori(0, SLOT_FFN) as i:
                    slot_free(i + S_UP[layer])
                    w = weight(i + S_UP[layer])
                    sp_.dma_start(w[:, :, 0:256], w_up[:, :, bass.ds(i * 256, 256)]).then_inc(s["raw_in"], 16)
                    sp_.dma_start(w[:, :, 256:512], w_up[:, :, bass.ds(i * 256 + DFF, 256)]).then_inc(s["raw_in"], 16)
                with sp_.Fori(0, 2) as i:
                    for k in range(3):
                        n = 3 * i + (S_DOWN[layer] + k)
                        nk = min(KD, KF - KD * k)
                        slot_free(n)
                        load_whole(n, w_dn[:, KD * k:KD * k + nk, bass.ds(i * 512, 512)], nk)

            feed_forward(0)
            with sp_.Fori(0, 4) as i:
                slot_free(i + S_SC)
                w = weight(i + S_SC)
                sp_.dma_start(w[:, :, 0:256], w_sc[:, :, bass.ds(i * 256 + D, 256)]).then_inc(s["raw_in"], 16)
                sp_.dma_start(w[:, :, 256:512], w_sc[:, :, bass.ds(i * 256 + 2 * D, 256)]).then_inc(s["raw_in"], 16)
            with sp_.Fori(0, 2) as i:
                slot_free(i + (S_SC + 4))
                load_whole(i + (S_SC + 4), w_sc[:, :, bass.ds(i * 512, 512)])
            with sp_.Fori(0, SLOT_OUT) as i:
                slot_free(i + S_SCO)
                load_whole(i + S_SCO, w_so[:, :, bass.ds(i * 512, 512)])
            feed_forward(1)

        @block.gpsimd
        def _(pool):
            PAR = [(a["dn_conv_w"].rearrange("l k (c p) -> (l k c) p", p=P), 0, PA_DN, 48),
                   (a["sc_conv_w"].rearrange("l k (c p) -> (l k c) p", p=P), 0, PA_SC, 24),
                   (a["ln_mix_g"].rearrange("l (c p) -> (l c) p", p=P), 0, PA_LMG, 16),
                   (a["ln_mix_b"].rearrange("l (c p) -> (l c) p", p=P), 0, PA_LMB, 16),
                   (a["dn_norm_w"], 0, PA_NW, 1),
                   (a["ffn_conv_w"][0].rearrange("k (c p) -> (k c) p", p=P), 1, PB_F, 66),
                   (a["ln_ffn_g"].rearrange("l (c p) -> (l c) p", p=P), 1, PB_LFG, 16),
                   (a["ln_ffn_b"].rearrange("l (c p) -> (l c) p", p=P), 1, PB_LFB, 16),
                   (a["ffn_conv_w"][1].rearrange("k (c p) -> (k c) p", p=P), 2, 0, 66)]
            for src, pack, row, n in PAR:
                pool.dma_start(prows[row:row + n, pack, :], src).then_inc(s["params_in"], 16)
            pool.dma_start(dnrows[0:24, :], a["state_dn_conv"][0].rearrange("b k c -> (b k) c")).then_inc(s["hist_in"], 16)
            with nc.allow_non_contiguous_dma(reason="eight gate columns of a wide row"):
                pool.dma_start(wba[:, :, :], a["w_in_mix"][0].rearrange("(k p) c -> p k c", p=P)[:, :, 2048:2056])\
                    .then_inc(s["wba_in"], 16)
            pool.dma_start(dtal[:, 0, :], a["dn_dt_bias"][0:1, :].to_broadcast([P, H])).then_inc(s["wba_in"], 16)
            pool.dma_start(dtal[:, 1, :], a["dn_a_log"][0:1, :].to_broadcast([P, H])).then_inc(s["wba_in"], 16)

            made = [0]

            def link(ins):
                PO.up(ins, f"const{made[0]}")
                PO.wait(pool, f"const{made[0]}")
                made[0] += 1

            def select(x, pattern, base, cm, fill, op=ALU.is_ge):
                link(pool.affine_select(out=x, in_=x, compare_op=op, fill=fill, base=base, pattern=pattern,
                                        channel_multiplier=cm))

            link(pool.memset(ident[:], 0.0))
            select(ident[:], [[-1, P]], 0, 1, 1.0, ALU.not_equal)
            PO.up(pool.memset(ones[:], 1.0), "ident_done")
            link(pool.memset(onesD[:], 1.0 / D))
            link(pool.memset(eps6[:], NORM_EPS))
            cin3 = cin[:, :].rearrange("p (c w) -> p c w", w=WD)
            PO.up(pool.memset(cin3[:, :, 0:3], 0.0), "cin_zero")
            link(pool.memset(upper[:], 1.0))
            select(upper[:], [[1, P]], 0, -1, 0.0)
            link(pool.memset(lower[:], 1.0))
            select(lower[:], [[-1, P]], -1, 1, 0.0)
            link(pool.memset(bs[:, 7, :], 1.0))
            link(pool.tensor_copy(bs[:, 0, :], ident[:]))
            for l in range(1, 7):
                z, n = 1 << l, P >> l
                link(pool.memset(bs[:, l, :], 1.0))
                x = bs[:, l, :].rearrange("p (n z) -> p n z", z=z)
                select(x, [[-z, n], [0, z]], 0, 1, 0.0)
                select(x, [[z, n], [0, z]], z - 1, -1, 0.0)
            link(pool.tensor_sub(bdiff[:, :, :], bs[:, 1:8, :], bs[:, 0:7, :]))
            link(pool.tensor_copy(same8[:], bs[0:SMP, 3, 0:SMP]))
            link(pool.tensor_mul(upper8[:], upper[0:SMP, 0:SMP], same8[:]))
            link(pool.tensor_mul(lower8[:], lower[0:SMP, 0:SMP], same8[:]))
            link(pool.memset(ltri[:], 1.0))
            select(ltri[:], [[1, NBLK], [-1, NBLK]], -1, 0, 0.0)
            link(pool.iota(iot[:, 128:384], pattern=[[1, 256]], base=-128, channel_multiplier=-1))
            link(pool.iota(iot[:, 0:128], pattern=[[1, 128]], base=0, channel_multiplier=0))
            link(pool.iota(iot[:, 384:401], pattern=[[-PAGE, NPG + 1]], base=PAST, channel_multiplier=1))
            link(pool.tensor_copy(iof[:, 0:401], iot[:, 0:401]))
            for h in range(H):
                link(pool.tensor_scalar(promptb[:, h, :], iof[:, 128:384], SLOPES[h], None, ALU.mult))
            select(promptb[:, :, :], [[0, H], [-1, 256]], 128, 1, NEG)
            link(pool.tensor_copy(c128[:], iof[0:32, 0:128]))
            link(pool.memset(slope[:], SLOPES[H - 1]))
            link(pool.memset(back[:], NT * (H - 1.0)))
            for h in range(H - 1, 0, -1):
                select(slope[:], [[0, 1]], -NT * h, 1, SLOPES[h - 1])
                select(back[:], [[0, NPG + 1]], -NT * h, 1, NT * (h - 1.0))
            link(pool.tensor_sub(back[:], iof[0:32, 384:401], back[:]))
            link(pool.tensor_scalar(ownb[:], c128[:, 0:120], 56.0, None, ALU.subtract))
            link(pool.tensor_sub(ownb[:], ownb[:], back[:, NPG:NPG + 1].to_broadcast([32, 120])))
            link(pool.tensor_scalar(iof[0:32, 0:120], ownb[:], 0.0, NEG, ALU.is_gt, ALU.mult))
            link(pool.tensor_mul(ownb[:], ownb[:], slope[:, 0:1].to_broadcast([32, 120])))
            link(pool.tensor_add(ownb[:], ownb[:], iof[0:32, 0:120]))
            select(ownb[:], [[1, 120]], -56, 0, NEG)
            PO.up(pool.tensor_copy(iof[0:1, 0:1], iof[0:1, 1:2]), "consts")

            pool.wait_ge(s["rel_act"], 12 + CREDIT)
            PO.wait(pool, "consts")
            PO.up(pool.tensor_copy(iof[:, 0:324].rearrange("p (c b s) -> p c b s", c=12, s=3),
                                   cin3[:, :, SEQ:SEQ + 99].rearrange("p c (b s) -> p c b s", s=11)[:, :, :, 0:3]), "dnlast")
            AC.wait(pool, "dntail2")
            pool.dma_start(o["dnc_p"][0, 0], dnrows[32:35, :]).then_inc(s["stores"], 16)
            pool.dma_start(o["dnc_s"][0].rearrange("b k c -> (b k) c"), dnrows[35:59, :]).then_inc(s["stores"], 16)

            for n, (l, t) in enumerate(INV):
                sz = TILES[t][1]
                if n == 0:
                    DV.wait(pool, "tok2")
                DV.wait(pool, f"L{t}")
                if n >= 2:
                    PE.wait(pool, f"invw{n - 2}")
                    if INV[n - 2][0] == 0:
                        DV.wait(pool, f"inv{n - 2}")
                x = t4(lmb[n % 2][0:sz, 0:H * sz])
                PO.up(pool.tensor_tensor(x, t4(L_[t]), mid(bdiff[0:sz, l, 0:sz], H), ALU.mult), f"lm{n}")

            DV.wait(pool, "qg2")
            PE.wait(pool, f"invu{len(INV) - 1}")
            PE.wait(pool, f"invw{len(INV) - 1}")
            for h in range(H):
                pool.dma_start(s0[:, NB * h:NB * h + NB, :], a["state_dn"][0, :, h].rearrange("b d v -> d b v"))\
                    .then_inc(s["s0_in0"], 16)
            DV.wait(pool, "state1")
            pool.dma_start(o["dn_p"][0, 0].rearrange("h d v -> d h v"), t4(spr[:, :])).then_inc(s["stores"], 16)
            for h in range(H):
                DV.wait(pool, f"stS{h}")
                pool.dma_start(o["dn_s"][0, :, h].rearrange("b d v -> d b v"), s0[:, NB * h:NB * h + NB, :])\
                    .then_inc(s["stores"], 16)
            for kv, (op, os_) in enumerate((("k_p", "k_s"), ("v_p", "v_s"))):
                AC.wait(pool, f"kvtok{3 * kv + 2}")
                pool.dma_start(o[op][0, 0].rearrange("(t p) h d -> p t (h d)", p=P), kvtok[:, kv, 0:2, :]).then_inc(s["stores"], 16)
                pool.dma_start(o[os_][0].rearrange("b t h d -> (b t) (h d)"), kvtok[0:SMP, kv, 2, :]).then_inc(s["stores"], 16)

            with pool.Fori(0, NB) as b:
                for w in range(VUNITS):
                    pool.wait_ge(s["v_hi"], b * VUNITS + (w + 1))
                    pool.tensor_tensor(vl[:, w % 2], vring[:, w // 2 % 2, 2 * (w % 2):2 * (w % 2) + 2, :], vh[:, w % 2],
                                       ALU.subtract).then_inc(s["v_lo"], 1)

            def accumulate(n):
                for m in range(1, KD - 1):
                    DV.wait(pool, f"r{n}_{m}")
                    if m > 1:
                        PO.wait(pool, f"accs{n}_{m - 1}")
                    PO.up(pool.tensor_tensor(lnt[:, 0, :], xres[:, 0, :] if m == 1 else lnt[:, 0, :], xres[:, m, :],
                                             ALU.add), f"accs{n}_{m}")
                    if m == 1:
                        AC.wait(pool, f"sq{n}_0")
                        PO.up(pool.tensor_copy(lnt[:, 1, :], sq[:, 0, :]), f"accq{n}_0")
                    AC.wait(pool, f"sq{n}_{m}")
                    PO.wait(pool, f"accq{n}_{m - 1}")
                    PO.up(pool.tensor_tensor(lnt[:, 1, :], lnt[:, 1, :], sq[:, m % 2, :], ALU.add), f"accq{n}_{m}")

            cb3 = cb[:, :].rearrange("p (c w) -> p c w", w=WF)

            def history(name, src, n):
                pool.dma_start(rows[32:48, 0:P * n], src.rearrange("b k c -> (b k) c")).then_inc(s["hist_in"], 16)
                PO.up(pool.memset(cb3[:, 0:n, 0:2], 0.0), f"{name}_zero")

            def tails(name, n, op, os_):
                if name == "sc":
                    pool.wait_ge(s["sc_prod"], KD + 2)
                else:
                    pool.wait_ge(s["rel_act"], REL[int(name[1])] + KF)
                PO.up(pool.tensor_copy(last2[:, 0:18 * n].rearrange("p (c b s) -> p c b s", c=n, s=2),
                                       cb3[:, 0:n, SEQ:SEQ + 90].rearrange("p c (b s) -> p c b s", s=10)[:, :, :, 0:2]),
                      f"{name}_last")
                AC.wait(pool, f"{name}_tail{(n - 1) // 4}")
                pool.dma_start(op, rows[0:2, 0:P * n]).then_inc(s["stores"], 16)
                pool.dma_start(os_.rearrange("b k c -> (b k) c"), rows[2:18, 0:P * n]).then_inc(s["stores"], 16)

            DV.wait(pool, "attn_end")
            AC.wait(pool, "attn_endh")
            pool.wait_ge(s["stores"], 16 * 11)
            history("f0", a["state_ffn_conv"][0], KF)
            accumulate(0)
            tails("f0", KF, o["ffc_p"][0, 0], o["ffc_s"][0])
            PE.wait(pool, "f0_hist")
            history("sc", a["state_sc_conv"][0], KD)
            accumulate(1)
            pool.wait_ge(s["stores"], 16 * 13)
            tails("sc", KD, o["scc_p"][0, 0], o["scc_s"][0])
            PE.wait(pool, "sc_hist")
            DV.wait(pool, "sc_gated")
            history("f1", a["state_ffn_conv"][1], KF)
            accumulate(2)
            pool.wait_ge(s["stores"], 16 * 15)
            tails("f1", KF, o["ffc_p"][1, 0], o["ffc_s"][1])
            accumulate(3)
            for t in range(3):
                for half in range(2):
                    AC.wait(pool, f"y{2 * t + half}")
                cols = hraw_y(t)
                if t < 2:
                    pool.dma_start(o["y_p"][0, P * t:P * t + P, :], cols).then_inc(s["stores"], 16)
                else:
                    pool.dma_start(o["y_s"].rearrange("b t d -> (b t) d"), cols).then_inc(s["stores"], 16)
            pool.wait_ge(s["stores"], 16 * (17 + 3))

        @block.scalar
        def _(act):
            def copy(out, in_):
                return act.activation(out, in_, ACT.Copy)

            def split_hi(n, p):
                act.wait_ge(s["raw_in"], 32 * n + 32)
                act.wait_ge(s["chunk_done"], 4 * n + (2 * p - 2 + CREDIT))
                copy(hi[:, p], weight(n)[:, :, 256 * p:256 * p + 256]).then_inc(s["hi_done"], 1)

            def chunk(n, j):
                act.wait_ge(s["chunk_done"], 4 * n + (j + 1 + CREDIT))

            for _ in range(CREDIT):
                act.memzero(spare(0)).then_inc(s["rel_act"], 1)
            for i, n in enumerate((PA_N, PB_N, PC_N)):
                PE.wait(act, "parT")
                AC.up(copy(par[:, i, 0:n], bank[4][:, 128 * i:128 * i + n]), f"par{i}")
            for k in range(KD):
                DV.wait(act, f"xres{k}")
                AC.up(copy(xh[:, k, :], xres[:, k, :]), f"xh{k}")
            PE.wait(act, "histT")
            PO.wait(act, "cin_zero")
            cin3 = cin[:, :].rearrange("p (c w) -> p c w", w=WD)
            AC.up(copy(cin3[:, :, 259:347].rearrange("p c (b s) -> p c b s", s=11)[:, :, :, 0:3],
                       bank[5][:, 0:288].rearrange("p (c b k) -> p c b k", c=12, b=NB)), "hist")

            split_hi(0, 0)

            def mix_slot(n, evacuate):
                split_hi(n, 1)
                for j in (0, 1):
                    chunk(n, j)
                    evacuate(j)
                split_hi(n + 1, 0)
                for j in (2, 3):
                    chunk(n, j)
                    evacuate(j)

            with act.Fori(0, 3) as i:
                def to_rows(j):
                    copy(cin[:, bass.ds((4 * i + j) * WD + 3, SEQ)], bank[j][:, 0:SEQ])
                    copy(cin[:, bass.ds((4 * i + j) * WD + 259, 88)].rearrange("p (b s) -> p b s", s=11)[:, :, 3:11],
                         bank[j][:, SEQ:TOK].rearrange("p (b t) -> p b t", t=NT)).then_inc(s["rel_act"], 1)
                mix_slot(i, to_rows)
            mix_slot(3, lambda j: act.activation(zsb[:, j, :], bank[j][:, 0:TOK], ACT.Silu).then_inc(s["rel_act"], 1))
            act.wait_ge(s["conv_step"], 48)
            for c in range(12):
                ins = act.activation(qkv[:, c * WF:c * WF + LD], qkv[:, c * WF:c * WF + LD], ACT.Silu)
            AC.up(ins, "silu")
            with act.Fori(0, 3) as i:
                mix_slot(i + 4, lambda j: copy(mb[:, bass.ds((4 * i + j) * TOK, TOK)], bank[j][:, 0:TOK])
                         .then_inc(s["rel_act"], 1))
            for g in range(3):
                PE.wait(act, f"dntail{g}")
                AC.up(copy(dnrows[32:59, 512 * g:512 * g + 512], bank[4 + g][0:27, :]), f"dntail{g}")

            DV.wait(act, "gx")
            act.activation(gates[:, L1, :], gates[:, NX, :], ACT.Exp)
            act.activation(gates[:, EB, :], gates[:, B_, :], ACT.Exp, scale=-1.0)
            AC.up(act.activation(dtal[:, 1, :], dtal[:, 1, :], ACT.Exp), "gexp")
            DV.wait(act, "gone")
            AC.up(act.activation(gates[:, L1, :], gates[:, L1, :], ACT.Ln), "gln")

            act.wait_ge(s["stores"], 32)
            AC.wait(act, "silu")
            PO.wait(act, "consts")
            for c in range(10):
                if c >= 2:
                    PE.wait(act, f"ss{c - 2}")
                if c < 8:
                    AC.up(act.activation(l2s(c), qkv[:, c * WF:c * WF + LD], ACT.Square), f"l2sq{c}")
                if c >= 2:
                    AC.up(act.activation(l2n[:, c - 2, :], bank[(c - 2) % 4][:, 0:LD], ACT.Ln, bias=eps6[:, 0:1]),
                          f"ssln{c - 2}")
            AC.wait(act, "ssln7")
            AC.up(act.activation(l2n[:, :, :], l2n[:, :, :], ACT.Exp, scale=-0.5), "rn")

            for t, (_, n) in enumerate(TILES):
                bk = 4 * (t % 2)
                gcb, small = bank[bk + 2], bank[bk + 3]
                PE.wait(act, f"cum{t}")
                DV.wait(act, f"cumsb{t}")
                AC.up(act.activation(gate(EGC, t, n), gate(GC, t, n), ACT.Exp), f"egc{t}")
                act.activation(gate(KD_, t, n), gate(KD_, t, n), ACT.Exp)
                if t < 2:
                    act.activation(gate(EGL, t), gate(GL, t), ACT.Exp)
                else:
                    act.activation(eglS[:, :], small[:, 8:40], ACT.Exp)
                if t:
                    DV.wait(act, f"qg{t - 1}")
                DV.wait(act, f"dmat{t}")
                AC.up(act.activation(t4(vnew[:, 0:H * n]), gcb[:, 0:H * n].rearrange("p (h c) -> p h c", h=H), ACT.Exp),
                      f"egcb{t}")
                act.activation(dsc[0][0:n, 0:H * n], dsc[0][0:n, 0:H * n], ACT.Exp)
                AC.up(act.activation(dsc[1][0:n, 0:H * n], dsc[1][0:n, 0:H * n], ACT.Exp, scale=-1.0), f"decay{t}")

            for n, (l, t) in enumerate(INV):
                sz = TILES[t][1]
                if l == 0:
                    continue
                PE.wait(act, f"invw{n}")
                AC.up(copy(wsb[t][0:sz, 0:H * sz], bank[(0, 3, 6)[t]][0:sz, 0:H * sz]), f"wsb{n}")

            for t in range(2):
                PE.wait(act, f"vn{t}")
                AC.up(copy(vnew[:, :], bank[0][:, :]), f"vnsb{t}")
                PE.wait(act, f"o{t}")
                AC.up(copy(oT[:, :, 128 * t:128 * t + 128], t4(bank[1][:, :])), f"oT{t}")
            PE.wait(act, "ksT")
            for u in range(2):
                ins = copy(kq[:, 256 * u:256 * u + 256].rearrange("p (a t) -> p a t", t=NT),
                           bank[4][:, :].rearrange("p (a u t) -> p a u t", u=2, t=NT)[:, :, u, :])
            AC.up(ins, "ksTsb")
            PE.wait(act, "vn2")
            AC.up(copy(vnew[0:SMP, :], bank[7][0:SMP, :]), "vnsb2")

            for h in range(H):
                DV.wait(act, "oT2")
                AC.wait(act, "oT1")
                AC.up(act.activation(qg[:, h, :], oT[:, h, :], ACT.Square), f"osq{h}")
            for h in range(H):
                PE.wait(act, f"oss{h}")
                AC.up(act.activation(qg[:, h, :], bank[h][:, 0:TOK], ACT.Ln, scale=1.0 / HD, bias=eps6[:, 0:1]), f"oln{h}")
            AC.wait(act, "oln3")
            AC.up(act.activation(qg[:, :, :], qg[:, :, :], ACT.Exp, scale=-0.5), "orn")
            DV.wait(act, "mixo")
            AC.up(copy(xh[:, 0:4, :], oT), "mixh_done")

            act.wait_ge(s["stores"], 16 * 7)
            for i in range(6):
                n = TILES[i % 3][1]
                PE.wait(act, f"kvT{i}")
                if i == 0:
                    DV.wait(act, "mixl_done")
                AC.up(copy(kvtok[0:n, i // 3, i % 3, :], bank[i][0:n, :]), f"kvtok{i}")

            for i in range(8):
                t, h = divmod(i, 4)
                DV.wait(act, f"pmax{t}")
                x = pl0[:, h, :] if t == 0 else pl1[:, h, :]
                AC.up(act.activation(x, x, ACT.Exp, bias=pst[:, 0, i:i + 1], accum_out=pst[:, 1, i:i + 1]), f"pexp{i}")
            for g in range(3):
                PE.wait(act, f"pT{g}")
                AC.up(copy(pT[:, 512 * g:512 * g + 512], bank[3 + g][:, :]), f"pTsb{g}")
            for t in range(2):
                PE.wait(act, f"po{t}")
                AC.up(copy(xh[:, 4:8, 128 * t:128 * t + 128], t4(bank[6 + t][:, :])), f"poh{t}")

            AC.up(copy(voh[:, :], kvtok[0:SMP, 1, 2, :]), "voh")

            def attend(b, c, d):
                def kT_hi(u):
                    if b is not None:
                        act.wait_ge(s["kT_mm"], b * UNITS + (u + 1))
                        after(act, "s_mm", b * UNITS + (u - 1))
                        copy(kTh[:, u % 2, :], bank[u % 2][:, :]).then_inc(s["kT_hi"], 1)

                def v_hi(x, w):
                    if x is not None:
                        act.wait_ge(s[f"v_in{w // 2 % 2}"], x * 128 + 64 * (w // 4 + 1))
                        after(act, "v_mm", x * VUNITS + (w - 1))
                        copy(vh[:, w % 2], vring[:, w // 2 % 2, 2 * (w % 2):2 * (w % 2) + 2, :]).then_inc(s["v_hi"], 1)

                def exponentials(blocks):
                    for n in blocks:
                        x = slice(BLK * n, min(BLK * n + BLK, PAST + SMP))
                        ins = act.activation(prob[0:32, x], sbias[0:32, x], ACT.Exp, bias=shift[:, n:n + 1],
                                             accum_out=dn[:, n:n + 1])
                    return ins

                if b is not None:
                    act.wait_ge(s["q_fp"], b + 1)
                    copy(qph[:, :, :], qpf[:, :, :]).then_inc(s["q_hi"], 1)
                for u in range(UNITS):
                    kT_hi(u)
                    if u % 2 == 0 and u < 14:
                        v_hi(d, u // 2 + 1)
                    if c is not None:
                        if u == 1:
                            act.wait_ge(s["shifted"], c + 1)
                            exponentials(range(3))
                        if u == 2:
                            exponentials(range(3, 6))
                        if u == 3:
                            exponentials(range(6, NBLK + 1)).then_inc(s["p_exp"], 1)
                    if u == 14:
                        v_hi(c, 0)
                if d is not None:
                    act.wait_ge(s["v_mm"], d * VUNITS + VUNITS)
                    copy(orow[:, :], bank[4][0:SMP, :]).then_inc(s["o_row"], 1)
                if c is not None:
                    act.wait_ge(s["pT_mm"], c + 1)
                    copy(pTs[:, 0:NPG, 0, :], bank[5][:, :].rearrange("p (j r) -> p j r", r=32))
                    copy(pTs[0:SMP, NPG, 0, :], bank[7][0:SMP, 256:288]).then_inc(s["pT_hi"], 1)

            attend(0, None, None)
            attend(1, 0, None)
            with act.Fori(2, NB) as b:
                attend(b, b - 1, b - 2)
            attend(None, NB - 1, NB - 2)
            attend(None, None, NB - 1)
            PE.wait(act, "attn_mm")
            AC.up(copy(xh[:, 4:8, SEQ:TOK], bank[6][:, 0:256].rearrange("p (h c) -> p h c", h=H)), "attn_endh")

            def square(n, m):
                DV.wait(act, f"r{n}_{m}")
                if m >= 2:
                    PO.wait(act, f"accq{n}_{m - 2}")
                AC.up(act.activation(sq[:, m % 2, :], xres[:, m, :], ACT.Square), f"sq{n}_{m}")

            def norm(n, gpack, grow, bpack, brow):
                PE.wait(act, f"stat{n}")
                AC.up(act.activation(lnt[:, 2, :], bank[4][:, 0:TOK], ACT.Square), f"msq{n}")
                DV.wait(act, f"var{n}")
                AC.up(act.activation(lnt[:, 3, :], lnt[:, 3, :], ACT.Ln), f"lnv{n}")
                AC.wait(act, f"lnv{n}")
                AC.up(act.activation(lnt[:, 3, :], lnt[:, 3, :], ACT.Exp, scale=-0.5), f"rstd{n}")
                for m in range(KD):
                    DV.wait(act, f"t2_{n}_{m}")
                    AC.up(act.activation(xres[:, m, :], hraw[:, m % 2, :], ACT.Identity, scale=vec(gpack, grow + m),
                                         bias=vec(bpack, brow + m)), f"ln{n}_{m}")
                    if n < 3:
                        AC.wait(act, f"ln{n}_{m}")
                        AC.up(copy(xh[:, m, :], xres[:, m, :]), f"lnh{n}_{m}")

            cb3 = cb[:, :].rearrange("p (c w) -> p c w", w=WF)

            def history(name, n):
                PE.wait(act, f"{name}_hist")
                PO.wait(act, f"{name}_zero")
                AC.up(copy(cb3[:, 0:n, 258:338].rearrange("p c (b s) -> p c b s", s=10)[:, :, :, 0:2],
                           bank[6][:, 0:16 * n].rearrange("p (c b k) -> p c b k", c=n, b=NB)), f"{name}_hist")

            def tails(name, n):
                for g in range((n + 3) // 4):
                    w = min(512, P * n - 512 * g)
                    PE.wait(act, f"{name}_tail{g}")
                    AC.up(copy(rows[0:18, 512 * g:512 * g + w], bank[4 + g % 2 * 3][0:18, 0:w]), f"{name}_tail{g}")

            def feed_forward(layer):
                base = S_UP[layer]
                with act.Fori(0, SLOT_FFN) as i:
                    split_hi(i + base, 1)
                    for j in (0, 1):
                        chunk(i + base, j)
                        copy(cb[:, bass.ds((2 * i + j) * WF + 2, SEQ)], bank[j][:, 0:SEQ])
                        copy(cb[:, bass.ds((2 * i + j) * WF + 258, 80)].rearrange("p (b s) -> p b s", s=10)[:, :, 2:10],
                             bank[j][:, SEQ:TOK].rearrange("p (b t) -> p b t", t=NT)).then_inc(s["rel_act"], 1)
                    split_hi(i + (base + 1), 0)
                    for j in (0, 1):
                        act.wait_ge(s["conv_step"], 6 * i + (CONV[layer] + 5 + j))
                        act.activation(acc[:, WF * j:WF * j + LF], acc[:, WF * j:WF * j + LF], ACT.Gelu)\
                            .then_inc(s["gelu_done"], 1)
                    for j in (0, 1):
                        act.wait_ge(s["h_done"], 2 * i + (KF * layer + j + 3))
                        copy(hh[:, bass.ds(2 * i + j, 1), :], hraw[:, j:j + 1, :]).then_inc(s["hh_done"], 1)

            def down(layer, n):
                for i in range(2):
                    for k in range(3):
                        slot = S_DOWN[layer] + 3 * i + k
                        split_hi(slot, 1)
                        if k == 2:
                            square(n, 4 * i)
                            square(n, 4 * i + 1)
                        if slot + 1 < S_END:
                            split_hi(slot + 1, 0)
                        if k == 2:
                            square(n, 4 * i + 2)
                            square(n, 4 * i + 3)

            def out_proj(base, n):
                for i in range(SLOT_OUT):
                    split_hi(base + i, 1)
                    square(n, 4 * i)
                    square(n, 4 * i + 1)
                    split_hi(base + i + 1, 0)
                    square(n, 4 * i + 2)
                    square(n, 4 * i + 3)

            out_proj(S_OUT, 0)
            norm(0, 0, PA_LMG, 0, PA_LMB)
            history("f0", KF)
            feed_forward(0)
            tails("f0", KF)
            down(0, 1)
            norm(1, 1, PB_LFG, 1, PB_LFB)
            history("sc", KD)
            with act.Fori(0, 4) as i:
                n = i + S_SC
                split_hi(n, 1)
                for j in (0, 1):
                    chunk(n, j)
                    act.wait_ge(s["sc_prod"], 2 * i + (j + 1))
                    copy(hraw[:, j, :], bank[j][:, 0:TOK]).then_inc(s["rel_act"], 1)
                split_hi(i + (S_SC + 1), 0)
            for n in range(S_SC + 4, S_SC + 6):
                split_hi(n, 1)
                split_hi(n + 1, 0)
                for j in range(4):
                    DV.wait(act, f"scp{4 * (n - S_SC - 4) + j}")
                    AC.up(copy(hh[:, 4 * (n - S_SC - 4) + j, :], hraw[:, j % 2, :]), f"sch{4 * (n - S_SC - 4) + j}")
            tails("sc", KD)
            out_proj(S_SCO, 2)
            norm(2, 0, PA_LMG + KD, 0, PA_LMB + KD)
            history("f1", KF)
            feed_forward(1)
            tails("f1", KF)
            down(1, 3)
            norm(3, 1, PB_LFG + KD, 1, PB_LFB + KD)
            for i in range(6):
                n = TILES[i // 2][1]
                PE.wait(act, f"yT{i}")
                AC.up(copy(hraw_y(i // 2)[:, 512 * (i % 2):512 * (i % 2) + 512], bank[i][0:n, :]), f"y{i}")

        @block.vector
        def _(dve):
            def split_lo(n, p):
                dve.wait_ge(s["hi_done"], 2 * n + (p + 1))
                dve.tensor_tensor(lo[:, p], weight(n)[:, :, 256 * p:256 * p + 256], hi[:, p], ALU.subtract)\
                   .then_inc(s["lo_done"], 1)

            def chunk(n, j):
                dve.wait_ge(s["chunk_done"], 4 * n + (j + 1 + CREDIT))

            def tt(out, a_, b_, op):
                return dve.tensor_tensor(out, a_, b_, op)

            dve.memset(spare(1), 0.0).then_inc(s["h_done"], 1)
            dve.memset(spare(1), 0.0).then_inc(s["h_done"], 1)
            dve.memset(spare(1), 0.0).then_inc(s["sc_prod"], 1)
            dve.memset(spare(1), 0.0).then_inc(s["sc_prod"], 1)
            DV.up(dve.memset(gates[:, :, :], 0.0), "gz")
            dve.wait_ge(s["pt_in"], 16)
            two = ptab[:, :].rearrange("o (a u) -> o a u", u=2)
            DV.up(dve.scalar_tensor_tensor(out=pair[:, :], in0=two[:, :, 1], scalar=float(POOL), in1=two[:, :, 0],
                                           op0=ALU.mult, op1=ALU.add), "pages")
            for k in range(KD):
                PE.wait(dve, f"xT{k}")
                DV.up(dve.tensor_copy(xres[:, k, :], bank[k % 4][:, 0:TOK]), f"xres{k}")
            for k in range(KD):
                AC.wait(dve, f"xh{k}")
                DV.up(tt(xl[:, k, :], xres[:, k, :], xh[:, k, :], ALU.subtract), f"xl{k}")
            PE.wait(dve, "ba")
            DV.wait(dve, "gz")
            for i, at in ((B_, 0), (X_, 4)):
                dve.tensor_copy(gates[:, i, 0:8].rearrange("p (t h) -> p t h", h=H),
                                bank[6][:, 0:16].rearrange("p (t h) -> p t h", h=8)[:, :, at:at + 4])
                ins = dve.tensor_copy(gates[0:SMP, i, 8:12], bank[6][0:SMP, 16 + at:20 + at])
            DV.up(ins, "ba")

            split_lo(0, 0)
            AC.wait(dve, "par2")
            AC.wait(dve, "hist")
            with dve.Fori(0, 3) as i:
                for q in range(2):
                    if q == 0:
                        split_lo(i, 1)
                    else:
                        split_lo(i + 1, 0)
                    for r in range(4):
                        for jj in range(2):
                            c = 4 * i + (2 * q + jj)
                            if r == 0:
                                dve.wait_ge(s["rel_act"], 4 * i + (2 * q + jj + 5))
                            else:
                                dve.wait_ge(s["conv_step"], 16 * i + (8 * q + 2 * (r - 1) + jj + 1))
                            x = cin[:, bass.ds(c * WD + r, LD)]
                            y = qkv[:, bass.ds(c * WF, LD)]
                            w = par2[:, bass.ds(c + (PA_DN + 12 * r), 1)]
                            if r == 0:
                                ins = dve.tensor_scalar(y, x, w, None, ALU.mult)
                            else:
                                ins = dve.scalar_tensor_tensor(out=y, in0=x, scalar=w, in1=y, op0=ALU.mult, op1=ALU.add)
                            ins.then_inc(s["conv_step"], 1)
            with dve.Fori(3, SLOT_MIX) as i:
                split_lo(i, 1)
                split_lo(i + 1, 0)

            dve.wait_ge(s["wba_in"], 48)
            DV.wait(dve, "ba")
            dt3 = dtal[:, 0:1, :].to_broadcast([P, 3, H])
            g3 = [gates[:, i, :].rearrange("p (t h) -> p t h", h=H) for i in range(13)]
            DV.up(tt(g3[X_], g3[X_], dt3, ALU.add), "gxa")
            DV.wait(dve, "gxa")
            DV.up(dve.scalar_tensor_tensor(out=gates[:, NX, :], in0=gates[:, X_, :], scalar=-1.0, in1=gates[:, X_, :],
                                           op0=ALU.mult, op1=ALU.min), "gx")
            AC.wait(dve, "gexp")
            dve.tensor_scalar(gates[:, L1, :], gates[:, L1, :], 1.0, None, ALU.add)
            DV.up(dve.tensor_scalar(gates[:, EB, :], gates[:, EB, :], 1.0, None, ALU.add), "gone")
            DV.wait(dve, "gone")
            DV.up(dve.reciprocal(gates[:, BETA, :], gates[:, EB, :]), "beta")
            AC.wait(dve, "gln")
            DV.up(dve.scalar_tensor_tensor(out=gates[:, X_, :], in0=gates[:, X_, :], scalar=0.0, in1=gates[:, L1, :],
                                           op0=ALU.max, op1=ALU.add), "gsp")
            DV.wait(dve, "gsp")
            DV.up(dve.scalar_tensor_tensor(out=g3[G_], in0=g3[X_], scalar=-1.0, in1=dtal[:, 1:2, :].to_broadcast([P, 3, H]),
                                           op0=ALU.mult, op1=ALU.mult), "g")

            AC.wait(dve, "rn")
            for c in range(8):
                x = qkv[:, c * WF:c * WF + LD]
                ins = dve.scalar_tensor_tensor(out=x, in0=x, scalar=SCALE if c < 4 else 1.0, in1=l2n[:, c, :],
                                               op0=ALU.mult, op1=ALU.mult)
            DV.up(ins, "qknorm")
            DV.wait(dve, "qknorm")
            DV.up(dve.tensor_copy(smp.rearrange("p c (b s) -> p c b s", s=NT),
                                  qk3[:, :, 259:347].rearrange("p c (b s) -> p c b s", s=11)[:, :, :, 0:NT]), "qkn")

            DV.wait(dve, "g")
            for t, (_, n) in enumerate(TILES):
                bk = 4 * (t % 2)
                kkb, qkb, gcb, small = bank[bk], bank[bk + 1], bank[bk + 2], bank[bk + 3]
                up_, lo_ = tri(t)
                if t:
                    PE.wait(dve, f"cum{t - 1}")
                else:
                    PO.wait(dve, "consts")
                if t == 2:
                    tt(rtmp[0:SMP, 0:32].rearrange("p (h b) -> p h b", h=H), last(gate(G_, t, n), NB), mid(member, H), ALU.mult)
                DV.up(tt(t4(spr[0:n, 0:H * n]), mid(up_, H), last(gate(G_, t, n), n), ALU.mult), f"ug{t}")
                PE.wait(dve, f"cum{t}")
                dve.tensor_copy(gate(GC, t, n), small[0:n, 0:4])
                DV.up(dve.tensor_copy(gate(GL, t, n), small[0:n, 4:8]), f"gcl{t}")
                DV.wait(dve, f"gcl{t}")
                tt(t4(dsc[0][0:n, 0:H * n]), t4(gcb[0:n, 0:H * n]), last(gate(GC, t, n), n), ALU.subtract)
                DV.up(tt(gate(KD_, t, n), gate(GL, t, n), gate(GC, t, n), ALU.subtract), f"cumsb{t}")
                DV.wait(dve, f"cumsb{t}")
                DV.up(dve.tensor_scalar(dsc[1][0:n, 0:H * n], dsc[0][0:n, 0:H * n], 0.0, None, ALU.max), f"dmax{t}")
                DV.up(dve.tensor_scalar(dsc[0][0:n, 0:H * n], dsc[0][0:n, 0:H * n], 0.0, None, ALU.min), f"dmat{t}")
                AC.wait(dve, f"egc{t}")
                dve.scalar_tensor_tensor(out=gate(NBE, t, n), in0=gate(BETA, t, n), scalar=-1.0, in1=gate(EGC, t, n),
                                         op0=ALU.mult, op1=ALU.mult)
                AC.wait(dve, f"decay{t}")
                tt(t4(dsc[0][0:n, 0:H * n]), t4(dsc[0][0:n, 0:H * n]), mid(up_, H), ALU.mult)
                DV.up(tt(t4(dsc[1][0:n, 0:H * n]), t4(dsc[1][0:n, 0:H * n]), mid(lo_, H), ALU.mult), f"mask{t}")
                DV.wait(dve, f"mask{t}")
                PE.wait(dve, f"kk{t}")
                DV.up(tt(L_[t], kkb[0:n, 0:H * n], dsc[1][0:n, 0:H * n], ALU.mult), f"La{t}")
                DV.up(tt(IN[t], qkb[0:n, 0:H * n], dsc[0][0:n, 0:H * n], ALU.mult), f"intra{t}")
                DV.wait(dve, f"La{t}")
                DV.up(tt(t4(L_[t]), t4(L_[t]), last(gate(BETA, t, n), n), ALU.mult), f"L{t}")
                PE.wait(dve, f"tok{t}")
                tt(t4(ktok[0:n, t, :]), t4(kkb[0:n, :]), last(gate(KD_, t, n), HD), ALU.mult)
                DV.up(tt(t4(vtok[0:n, t, :]), t4(qkb[0:n, :]), last(gate(BETA, t, n), HD), ALU.mult), f"tok{t}")
                AC.wait(dve, f"egcb{t}")
                if t < 2:
                    DV.up(tt(qg[:, :, 128 * t:128 * t + 128], qk3[:, 0:4, 128 * t:128 * t + 128], t4(vnew[:, :]), ALU.mult), f"qg{t}")
                else:
                    kq5 = kq.rearrange("p (h b u t) -> p h b u t", h=H, b=NB, u=2)
                    for h in range(H):
                        dve.tensor_copy(kq5[:, h, :, 0, :], head(4 + h, 2).rearrange("p (b t) -> p b t", t=NT))
                        ins = tt(kq5[:, h, :, 1, :], head(h, 2).rearrange("p (b t) -> p b t", t=NT), vnew[:, 64 * h:64 * h + 64].rearrange("p (b t) -> p b t", t=NT),
                                 ALU.mult)
                    DV.up(ins, "qg2")

            for n, (l, t) in enumerate(INV):
                sz = TILES[t][1]
                w, u, v = ((0, 1, 2), (3, 4, 5), (6, 7, 7))[t]
                if l == 0:
                    PE.wait(dve, f"invw{n}")
                    PO.wait(dve, f"lm{n}")
                    tt(t4(TT[t]), mid(ident[0:sz, 0:sz], H), t4(bank[w][0:sz, 0:H * sz]), ALU.subtract)
                    DV.up(tt(t4(T_[t]), mid(ident[0:sz, 0:sz], H), t4(lmb[n % 2][0:sz, 0:H * sz]), ALU.subtract), f"inv{n}")
                else:
                    PE.wait(dve, f"invu{n}")
                    off = 256 if t == 2 else 0
                    tt(T_[t], T_[t], bank[u][0:sz, 0:H * sz], ALU.subtract)
                    DV.up(tt(TT[t], TT[t], bank[v][0:sz, off:off + H * sz], ALU.subtract), f"inv{n}")

            PE.wait(dve, "st0")
            DV.up(dve.tensor_copy(spr[:, :], bank[2][:, :]), "state0")
            PE.wait(dve, "ks1")
            DV.up(tt(t4(rtmp[:, :]), t4(bank[3][:, :]), last(gate(NBE, 1), HD), ALU.mult), "rhsa1")
            DV.wait(dve, "rhsa1")
            DV.up(tt(rtmp[:, :], rtmp[:, :], vtok[:, 1, :], ALU.add), "rhs1")
            PE.wait(dve, "st1")
            DV.up(tt(t4(spr[:, :]), t4(spr[:, :]), last(gate(EGL, 1), HD), ALU.mult), "statea")
            DV.wait(dve, "statea")
            DV.up(tt(spr[:, :], spr[:, :], bank[2][:, :], ALU.add), "state1")
            PE.wait(dve, "ks2")
            DV.up(tt(t4(rtmp[0:SMP, :]), t4(bank[6][0:SMP, :]), last(gate(NBE, 2, SMP), HD), ALU.mult), "rhsa2")
            DV.wait(dve, "rhsa2")
            DV.up(tt(rtmp[0:SMP, :], rtmp[0:SMP, :], vtok[0:SMP, 2, :], ALU.add), "rhs2")
            PE.wait(dve, "o2")
            qs = kq[:, 256:512].rearrange("p (h b t) -> p h b t", h=H, t=NT)
            DV.up(tt(oT[:, :, SEQ:TOK].rearrange("p h (b t) -> p h b t", t=NT),
                     bank[5][:, 0:256].rearrange("p (h b t) -> p h b t", h=H, t=NT), qs, ALU.add), "oT2")
            AC.wait(dve, "vnsb2")
            for h in range(H):
                if h:
                    PE.wait(dve, f"stS{h - 1}")
                DV.up(tt(vnm.rearrange("p (b v) -> p b v", v=HD), mid(vnew[0:SMP, 128 * h:128 * h + 128], NB),
                         last(member, HD), ALU.mult), f"vnm{h}")
                x = s0[:, NB * h:NB * h + NB, :]
                DV.up(tt(x, x, last(eglS[:, NB * h:NB * h + NB], HD), ALU.mult), f"s0g{h}")
                DV.wait(dve, f"s0g{h}")
                PE.wait(dve, f"stS{h}")
                y = x.rearrange("p b v -> p (b v)")
                bk = 0 if h % 2 else 2
                tt(y[:, 0:512], y[:, 0:512], bank[bk][:, :], ALU.add)
                DV.up(tt(y[:, 512:1024], y[:, 512:1024], bank[bk + 1][:, :], ALU.add), f"stS{h}")

            AC.wait(dve, "orn")
            DV.up(tt(oT, oT, qg[:, :, :], ALU.mult), "on1")
            DV.wait(dve, "on1")
            DV.up(dve.scalar_tensor_tensor(out=oT, in0=oT, scalar=vec(0, PA_NW), in1=zsb[:, :, :], op0=ALU.mult,
                                           op1=ALU.mult), "mixo")
            AC.wait(dve, "mixh_done")
            DV.up(tt(xl[:, 0:4, :], oT, xh[:, 0:4, :], ALU.subtract), "mixl_done")

            dve.wait_ge(s["stores"], 16 * 7)
            PE.wait(dve, "ps0")
            DV.up(dve.scalar_tensor_tensor(out=pl0, in0=t4(bank[0][:, :]), scalar=SCALE, in1=promptb[:, :, 128:256],
                                           op0=ALU.mult, op1=ALU.add), "plog0")
            PE.wait(dve, "ps1")
            for q in range(2):
                ins = dve.scalar_tensor_tensor(out=pl1[:, 2 * q:2 * q + 2, :],
                                               in0=bank[1 + q][:, :].rearrange("p (h c) -> p h c", h=2), scalar=SCALE,
                                               in1=promptb[:, 2 * q:2 * q + 2, :], op0=ALU.mult, op1=ALU.add)
            DV.up(ins, "plog1")
            for t, x in enumerate((pl0, pl1)):
                DV.wait(dve, f"plog{t}")
                DV.up(dve.tensor_reduce(pst[:, 2, 4 * t:4 * t + 4], x, AX.X, ALU.max), f"pmaxa{t}")
                DV.wait(dve, f"pmaxa{t}")
                DV.up(dve.tensor_scalar(pst[:, 0, 4 * t:4 * t + 4], pst[:, 2, 4 * t:4 * t + 4], -1.0, None, ALU.mult), f"pmax{t}")
            for t, x in enumerate((pl0, pl1)):
                AC.wait(dve, f"pexp{4 * t + 3}")
                DV.up(dve.reciprocal(pst[:, 2, 4 * t:4 * t + 4], pst[:, 1, 4 * t:4 * t + 4]), f"prec{t}")
                DV.wait(dve, f"prec{t}")
                DV.up(tt(x, x, last(pst[:, 2, 4 * t:4 * t + 4], 128 + 128 * t), ALU.mult), f"pnorm{t}")
            for t in range(2):
                AC.wait(dve, f"poh{t}")
                DV.up(tt(xl[:, 4:8, 128 * t:128 * t + 128], t4(bank[6 + t][:, :]), xh[:, 4:8, 128 * t:128 * t + 128],
                         ALU.subtract), f"pol{t}")

            AC.wait(dve, "voh")
            DV.up(tt(vol[:, :], kvtok[0:SMP, 1, 2, :], voh[:, :], ALU.subtract), "vol")
            for g in range(NPG):
                dve.tensor_scalar(keyb[:, PAGE * g:PAGE * g + PAGE], c128[:, :], back[:, g:g + 1], slope[:, 0:1],
                                  ALU.subtract, ALU.mult)
            dve.tensor_copy(twice[:, :], ident[0:SMP, 0:32])
            dve.memset(pen[:, NBLK:NBLK + 1], 0.0)
            DV.up(dve.memset(qpf[:, :, :], 0.0), "rowc0")
            DV.wait(dve, "rowc0")
            DV.up(tt(twice[:, :], twice[:, :], ident[0:SMP, 32:SMP], ALU.add), "rowc")
            DV.wait(dve, "rowc")
            ROW = 9

            def attend(b, c):
                made = [0]

                def link(ins):
                    made[0] += 1
                    ins.then_inc(s["row"], 1)
                    dve.wait_ge(s["row"], c * ROW + made[0])

                def kT_lo(u):
                    if b is not None:
                        dve.wait_ge(s["kT_hi"], b * UNITS + (u + 1))
                        tt(kTl[:, u % 2, :], bank[u % 2][:, :], kTh[:, u % 2, :], ALU.subtract).then_inc(s["kT_lo"], 1)

                def own_bias():
                    dve.scalar_tensor_tensor(out=sbias[0:32, PAST:], in0=bank[7][0:32, 0:SMP], scalar=SCALE,
                                             in1=ownb[:, bass.ds(b * -NT + (SMP - NT), SMP)], op0=ALU.mult, op1=ALU.add)\
                       .then_inc(s["s_bias"], 1)

                def bias(g):
                    dve.wait_ge(s["s_mm"], b * UNITS + (4 * g + 4))
                    dve.scalar_tensor_tensor(out=sbias[0:32, 512 * g:512 * g + 512], in0=bank[2 + g % 2][0:32, :], scalar=SCALE,
                                             in1=keyb[:, 512 * g:512 * g + 512], op0=ALU.mult, op1=ALU.add)\
                       .then_inc(s["s_bias"], 1)

                def sums(g):
                    dve.tensor_reduce(gsum[:, 2 * g:2 * g + 2], bank[2 + g % 2][0:32, :].rearrange("p (n k) -> p n k", n=2),
                                      AX.X, ALU.add).then_inc(s["s_row"], 1)

                def maxima(x, g):
                    dve.wait_ge(s["s_bias"], x * 5 + (g + 2))
                    dve.tensor_reduce(bmax[:, 2 * g:2 * g + 2],
                                      sbias[0:32, 512 * g:512 * g + 512].rearrange("p (n k) -> p n k", n=2), AX.X, ALU.max)\
                       .then_inc(s["s_max"], 1)

                def ranks():
                    A, B = [rk[:, i, :].rearrange("p (n m) -> p n m", m=NBLK) for i in range(2)]
                    gm, gn = mid(gsum[:, :], NBLK), last(gsum[:, :], NBLK)
                    dve.wait_ge(s["s_row"], c * 4 + 4)
                    dve.wait_ge(s["s_max"], c * 4 + 4)
                    tt(A, gm, gn, ALU.is_gt)
                    link(tt(B, gm, gn, ALU.is_equal))
                    link(tt(B, B, ltri[:, :, :], ALU.mult))
                    link(tt(A, A, B, ALU.add))
                    link(dve.tensor_reduce(rank[:, :], A, AX.X, ALU.add))
                    link(dve.tensor_scalar(pen[:, 0:NBLK], rank[:, :], TOPK - 0.5, NEG, ALU.is_gt, ALU.mult))
                    link(tt(bmax[:, :], bmax[:, :], pen[:, :], ALU.add))
                    link(dve.tensor_reduce(r1[:, 0:1], bmax[:, :], AX.X, ALU.max))
                    tt(shift[:, :], pen[:, :], r1[:, 0:1].to_broadcast([32, NBLK + 1]), ALU.subtract).then_inc(s["shifted"], 1)

                def normalise():
                    dve.wait_ge(s["p_exp"], c + 1)
                    link(dve.tensor_reduce(r1[:, 1:2], dn[:, :], AX.X, ALU.add))
                    link(dve.reciprocal(r1[:, 2:3], r1[:, 1:2]))
                    dve.tensor_scalar(prob[0:32, :], prob[0:32, :], r1[:, 2:3], None, ALU.mult).then_inc(s["p_norm"], 1)

                if b is not None:
                    after(dve, "s_mm", b * UNITS)
                    for h in range(H):
                        ins = dve.tensor_copy(qpf[:, h, NT * h:NT * h + NT], mb[:, bass.ds(b * NT + (TOK * h + SEQ), NT)])
                    ins.then_inc(s["q_fp"], 1)
                if c is not None:
                    sums(3)
                kT_lo(0)
                if b is not None:
                    dve.wait_ge(s["q_hi"], b + 1)
                    tt(qpl[:, :, :], qpf[:, :, :], qph[:, :, :], ALU.subtract).then_inc(s["q_lo"], 1)
                if c is not None:
                    maxima(c, 3)
                kT_lo(1)
                if c is not None:
                    ranks()
                for u in range(2, UNITS):
                    kT_lo(u)
                    g, at = divmod(u - 5, 4)
                    if b is not None and g >= 0:
                        if u == 5:
                            after(dve, "p_exp", b)
                            own_bias()
                        if at == 0:
                            bias(g)
                        if at == 1:
                            sums(g)
                        if at == 2:
                            maxima(b, g)
                        if u == 12:
                            dve.tensor_reduce(bmax[:, NBLK:NBLK + 1], sbias[0:32, PAST:], AX.X, ALU.max)
                    if u == 8 and c is not None:
                        normalise()
                if c is not None:
                    dve.wait_ge(s["pT_hi"], c + 1)
                    tt(pTs[:, 0:NPG, 1, :], bank[5][:, :].rearrange("p (j r) -> p j r", r=32), pTs[:, 0:NPG, 0, :],
                       ALU.subtract)
                    tt(pTs[0:SMP, NPG, 1, :], bank[7][0:SMP, 256:288], pTs[0:SMP, NPG, 0, :], ALU.subtract)\
                        .then_inc(s["pT_lo"], 1)
                if b is not None:
                    bias(3)

            attend(0, None)
            with dve.Fori(1, NB) as b:
                attend(b, b - 1)
            attend(None, NB - 1)
            AC.wait(dve, "attn_endh")
            DV.up(tt(xl[:, 4:8, SEQ:TOK], bank[6][:, 0:256].rearrange("p (h c) -> p h c", h=H), xh[:, 4:8, SEQ:TOK],
                     ALU.subtract), "attn_end")

            def residual(n, m, slot):
                chunk(slot, m % 4)
                DV.up(dve.scalar_tensor_tensor(out=xres[:, m, :], in0=xres[:, m, :], scalar=ALPHA, in1=bank[m % 4][:, 0:TOK],
                                               op0=ALU.mult, op1=ALU.add), f"r{n}_{m}")

            def norm(n):
                AC.wait(dve, f"msq{n}")
                DV.up(tt(lnt[:, 3, :], bank[5][:, 0:TOK], lnt[:, 2, :], ALU.subtract), f"vara{n}")
                DV.wait(dve, f"vara{n}")
                DV.up(dve.tensor_scalar(lnt[:, 3, :], lnt[:, 3, :], 0.0, LN_EPS, ALU.max, ALU.add), f"var{n}")
                AC.wait(dve, f"rstd{n}")
                DV.up(tt(lnt[:, 4, :], bank[4][:, 0:TOK], lnt[:, 3, :], ALU.mult), f"bm{n}")
                DV.wait(dve, f"bm{n}")
                for m in range(KD + 1):
                    if m < KD:
                        if m >= 2:
                            AC.wait(dve, f"ln{n}_{m - 2}")
                        DV.up(tt(hraw[:, m % 2, :], xres[:, m, :], lnt[:, 3, :], ALU.mult), f"t1_{n}_{m}")
                        DV.wait(dve, f"t1_{n}_{m}")
                        DV.up(tt(hraw[:, m % 2, :], hraw[:, m % 2, :], lnt[:, 4, :], ALU.subtract), f"t2_{n}_{m}")
                    if m and n < 3:
                        AC.wait(dve, f"lnh{n}_{m - 1}")
                        DV.up(tt(xl[:, m - 1, :], xres[:, m - 1, :], xh[:, m - 1, :], ALU.subtract), f"x{n}_{m - 1}")

            def out_proj(base, n):
                for i in range(SLOT_OUT):
                    split_lo(base + i, 1)
                    residual(n, 4 * i, base + i)
                    residual(n, 4 * i + 1, base + i)
                    split_lo(base + i + 1, 0)
                    residual(n, 4 * i + 2, base + i)
                    residual(n, 4 * i + 3, base + i)

            def down(layer, n):
                for i in range(2):
                    for k in range(3):
                        slot = S_DOWN[layer] + 3 * i + k
                        split_lo(slot, 1)
                        if k == 2:
                            residual(n, 4 * i, slot)
                            residual(n, 4 * i + 1, slot)
                        if slot + 1 < S_END:
                            split_lo(slot + 1, 0)
                        if k == 2:
                            residual(n, 4 * i + 2, slot)
                            residual(n, 4 * i + 3, slot)

            def convolve(c, w0, nch, y, i, jj, r, base):
                if r:
                    dve.wait_ge(s["conv_step"], 6 * i + (base + 2 * (r - 1) + jj + 1))
                x = cb[:, bass.ds(c * WF + r, LF)]
                w = par2[:, bass.ds(c + (w0 + nch * r), 1)]
                if r == 0:
                    ins = dve.tensor_scalar(y, x, w, None, ALU.mult)
                else:
                    ins = dve.scalar_tensor_tensor(out=y, in0=x, scalar=w, in1=y, op0=ALU.mult, op1=ALU.add)
                ins.then_inc(s["conv_step"], 1)

            def padded(x):
                return x.rearrange("p (b s) -> p b s", s=10)[:, :, 0:NT]

            def feed_forward(layer):
                base = S_UP[layer]
                w0 = P + PB_F if layer == 0 else 2 * P
                with dve.Fori(0, SLOT_FFN) as i:
                    split_lo(i + base, 1)
                    for r in range(3):
                        for j in (0, 1):
                            if r == 0:
                                dve.wait_ge(s["rel_act"], 2 * i + (REL[layer] + j + 1))
                            convolve(2 * i + j, w0, KF, acc[:, WF * j:WF * j + LF], i, j, r, CONV[layer])
                    split_lo(i + (base + 1), 0)
                    for j in (0, 1):
                        dve.wait_ge(s["gelu_done"], 2 * i + (KF * layer + j + 1))
                        chunk(i + base, 2 + j)
                        tt(hraw[:, j, 0:SEQ], acc[:, WF * j:WF * j + SEQ], bank[2 + j][:, 0:SEQ], ALU.mult)
                        tt(hraw[:, j, SEQ:TOK].rearrange("p (b t) -> p b t", t=NT), padded(acc[:, WF * j + 258:WF * j + 338]),
                           bank[2 + j][:, SEQ:TOK].rearrange("p (b t) -> p b t", t=NT), ALU.mult).then_inc(s["h_done"], 1)
                    for j in (0, 1):
                        dve.wait_ge(s["hh_done"], 2 * i + (KF * layer + j + 1))
                        tt(hl[:, bass.ds(2 * i + j, 1), :], hraw[:, j:j + 1, :], hh[:, bass.ds(2 * i + j, 1), :], ALU.subtract)\
                            .then_inc(s["hid_ready"], 1)

            out_proj(S_OUT, 0)
            norm(0)
            AC.wait(dve, "f0_hist")
            feed_forward(0)
            down(0, 1)
            norm(1)
            AC.wait(dve, "sc_hist")
            with dve.Fori(0, 4) as i:
                split_lo(i + S_SC, 1)
                split_lo(i + (S_SC + 1), 0)
                for j in (0, 1):
                    dve.wait_ge(s["rel_act"], 2 * i + (REL_SC + j + 1))
                    chunk(i + S_SC, 2 + j)
                    tt(cb[:, bass.ds((2 * i + j) * WF + 2, SEQ)], hraw[:, j, 0:SEQ], bank[2 + j][:, 0:SEQ], ALU.mult)
                    tt(cb[:, bass.ds((2 * i + j) * WF + 258, 80)].rearrange("p (b s) -> p b s", s=10)[:, :, 2:10],
                       hraw[:, j, SEQ:TOK].rearrange("p (b t) -> p b t", t=NT),
                       bank[2 + j][:, SEQ:TOK].rearrange("p (b t) -> p b t", t=NT), ALU.mult).then_inc(s["sc_prod"], 1)
                for r in range(3):
                    for j in (0, 1):
                        if r == 0:
                            dve.wait_ge(s["sc_prod"], 2 * i + (j + 3))
                        convolve(2 * i + j, PA_SC, KD, cb[:, bass.ds((2 * i + j) * WF + KD * WF, LF)], i, j, r, CONV_SC)
            dve.wait_ge(s["conv_step"], CONV_SC + 24)
            for i in range(2):
                n = S_SC + 4 + i
                split_lo(n, 1)
                for j in range(4):
                    m = 4 * i + j
                    if j == 2:
                        split_lo(n + 1, 0)
                    chunk(n, j)
                    if m >= 2:
                        AC.wait(dve, f"sch{m - 2}")
                    y = cb[:, (KD + m) * WF:(KD + m) * WF + WF]
                    tt(hraw[:, m % 2, 0:SEQ], y[:, 0:SEQ], bank[j][:, 0:SEQ], ALU.mult)
                    DV.up(tt(hraw[:, m % 2, SEQ:TOK].rearrange("p (b t) -> p b t", t=NT), padded(y[:, 258:338]),
                             bank[j][:, SEQ:TOK].rearrange("p (b t) -> p b t", t=NT), ALU.mult), f"scp{m}")
                    AC.wait(dve, f"sch{m}")
                    DV.up(tt(hl[:, m, :], hraw[:, m % 2, :], hh[:, m, :], ALU.subtract), f"schl{m}")
            DV.up(dve.memset(spare(1), 0.0), "sc_gated")
            out_proj(S_SCO, 2)
            norm(2)
            AC.wait(dve, "f1_hist")
            feed_forward(1)
            down(1, 3)
            norm(3)

        @block.tensor
        def _(pe):
            def mm(out, lhsT, rhs, start=True, stop=True, **kw):
                return pe.matmul(out, lhsT, rhs, start=start, stop=stop, **kw)

            PO.wait(pe, "ident_done")
            PO.wait(pe, "const1")
            pe.wait_ge(s["xtok_in"], 32)
            for k in range(KD):
                if k >= 4:
                    DV.wait(pe, f"xres{k - 4}")
                for t, (at, n) in enumerate(TILES):
                    ins = pe.transpose(bank[k % 4][:, at:at + n], xtok[0:n, t, P * k:P * k + P], ident[0:n, 0:n])
                    if t == 0 and k < CREDIT:
                        ins.then_inc(s["chunk_done"], 1)
                PE.up(ins, f"xT{k}")
            pe.wait_ge(s["params_in"], 16 * 9)
            for i, n in enumerate((PA_N, PB_N, PC_N)):
                ins = pe.transpose(bank[4][:, 128 * i:128 * i + n], prows[0:n, i, :], ident[0:n, 0:n])
            PE.up(ins, "parT")
            pe.wait_ge(s["hist_in"], 16)
            for c in range(12):
                ins = pe.transpose(bank[5][:, 24 * c:24 * c + 24], dnrows[0:24, P * c:P * c + P], ident[0:24, 0:24])
            PE.up(ins, "histT")
            pe.wait_ge(s["wba_in"], 48)
            DV.wait(pe, "xres7")
            for t, (at, n) in enumerate(TILES):
                for k in range(KD):
                    ins = mm(bank[6][0:n, 8 * t:8 * t + 8], xres[:, k, at:at + n], wba[:, k, :], k == 0, k == KD - 1)
            PE.up(ins, "ba")

            def project(n, xa, xb, nk, free, ready, k0=0, start=True, stop=True):
                for p in range(2):
                    pe.wait_ge(s["lo_done"], 2 * n + (p + 1))
                    for c in range(2):
                        j = 2 * p + c
                        if start:
                            free(j)
                        for k in range(nk):
                            if j == 0:
                                ready(k0 + k)
                            out = bank[j][:, 0:TOK]
                            w, v = hi[:, p, k, P * c:P * c + P], lo[:, p, k, P * c:P * c + P]
                            mm(out, w, xa[:, k0 + k, :], start and k == 0, False)
                            mm(out, w, xb[:, k0 + k, :], False, False)
                            ins = mm(out, v, xa[:, k0 + k, :], False, stop and k == nk - 1)
                        ins.then_inc(s["chunk_done"], 1)

            with pe.Fori(0, SLOT_MIX) as i:
                project(i, xh, xl, KD, lambda j: pe.wait_ge(s["rel_act"], 4 * i + (j + 1)), lambda k: DV.wait(pe, f"xl{k}"))
            AC.wait(pe, "par2")
            AC.wait(pe, "hist")
            DV.wait(pe, "ba")
            PO.wait(pe, "dnlast")
            for g in range(3):
                for c in range(4):
                    ins = pe.transpose(bank[4 + g][0:27, P * c:P * c + P], iof[:, 27 * (4 * g + c):27 * (4 * g + c) + 27],
                                       ident[:, :])
                PE.up(ins, f"dntail{g}")

            for c in range(8):
                AC.wait(pe, f"l2sq{c}")
                if c >= 4:
                    AC.wait(pe, f"ssln{c - 4}")
                elif c == 0:
                    pe.wait_ge(s["rel_act"], 32)
                PE.up(mm(bank[c % 4][:, 0:LD], ones[:, :], l2s(c)), f"ss{c}")

            for t, (at, n) in enumerate(TILES):
                bk = 4 * (t % 2)
                kkb, qkb, gcb, small = bank[bk], bank[bk + 1], bank[bk + 2], bank[bk + 3]
                up_ = tri(t)[0]
                DV.wait(pe, f"ug{t}")
                if t == 0:
                    AC.wait(pe, "ssln7")
                if t == 1:
                    AC.wait(pe, "dntail2")
                if t == 2:
                    DV.wait(pe, "tok0")
                    AC.wait(pe, "decay0")
                mm(gcb[:, 0:H * n], ones[0:n, :], spr[0:n, 0:H * n])
                mm(small[0:n, 0:4], up_, gate(G_, t, n))
                if t < 2:
                    ins = mm(small[:, 4:8], ones[0:n, :], gate(G_, t, n))
                else:
                    mm(small[0:n, 4:8], same8[:, :], gate(G_, t, n))
                    ins = mm(small[:, 8:40], ones[0:n, :], rtmp[0:n, 0:32])
                PE.up(ins, f"cum{t}")
                DV.wait(pe, "qkn")
                for h in range(H):
                    mm(kkb[0:n, n * h:n * h + n], head(4 + h, t), head(4 + h, t))
                for h in range(H):
                    ins = mm(qkb[0:n, n * h:n * h + n], head(4 + h, t), head(h, t))
                PE.up(ins, f"kk{t}")
                DV.wait(pe, f"L{t}")
                DV.wait(pe, f"intra{t}")
                for h in range(H):
                    pe.transpose(kkb[0:n, P * h:P * h + P], head(4 + h, t), ident[:, :])
                for h in range(H):
                    ins = pe.transpose(qkb[0:n, P * h:P * h + P], head(8 + h, t), ident[:, :])
                PE.up(ins, f"tok{t}")

            BK = ((0, 1, 2), (3, 4, 5), (6, 7, 7))
            for l in range(7):
                todo = [(n, t) for n, (l_, t) in enumerate(INV) if l_ == l]
                for n, t in todo:
                    sz = TILES[t][1]
                    PO.wait(pe, f"lm{n}")
                    if l == 0:
                        DV.wait(pe, "tok2")
                        AC.wait(pe, "decay2")
                    else:
                        DV.wait(pe, f"inv{INV.index((l - 1, t))}")
                    for h in range(H):
                        ins = mm(bank[BK[t][0]][0:sz, sz * h:sz * h + sz], lmb[n % 2][0:sz, sz * h:sz * h + sz],
                                 ident[0:sz, 0:sz] if l == 0 else TT[t][:, sz * h:sz * h + sz])
                    PE.up(ins, f"invw{n}")
                if l:
                    for n, t in todo:
                        sz = TILES[t][1]
                        off = 256 if t == 2 else 0
                        AC.wait(pe, f"wsb{n}")
                        for h in range(H):
                            q = slice(sz * h, sz * h + sz)
                            mm(bank[BK[t][1]][0:sz, q], wsb[t][0:sz, q], T_[t][:, q])
                            ins = mm(bank[BK[t][2]][0:sz, off + sz * h:off + sz * h + sz], T_[t][:, q], wsb[t][0:sz, q])
                        PE.up(ins, f"invu{n}")

            for t in range(2):
                DV.wait(pe, f"inv{INV.index((6, t))}")
                rhs = vtok[:, 0, :] if t == 0 else rtmp[:, :]
                if t:
                    DV.wait(pe, "state0")
                    for h in range(H):
                        q = slice(P * h, P * h + P)
                        ins = mm(bank[3][:, q], head(4 + h, 1), spr[:, q])
                    PE.up(ins, "ks1")
                    DV.wait(pe, "rhs1")
                    AC.wait(pe, "oT0")
                for h in range(H):
                    q = slice(P * h, P * h + P)
                    ins = mm(bank[0][:, q], TT[t][:, q], rhs[:, q])
                PE.up(ins, f"vn{t}")
                AC.wait(pe, f"vnsb{t}")
                for h in range(H):
                    q = slice(P * h, P * h + P)
                    ins = mm(bank[1][:, q], vnew[:, q], IN[t][:, q], True, t == 0)
                    if t:
                        ins = mm(bank[1][:, q], spr[:, q], qg[:, h, P:2 * P], False, True)
                PE.up(ins, f"o{t}")
                for h in range(H):
                    q = slice(P * h, P * h + P)
                    ins = mm(bank[2][:, q], ktok[:, t, q], vnew[:, q])
                PE.up(ins, f"st{t}")
            pe.wait_ge(s["s0_in0"], 64)
            DV.wait(pe, "qg2")
            for i in range(32):
                ins = mm(bank[4][:, 16 * i:16 * i + 16], s0[:, i, :], kq[:, 16 * i:16 * i + 16])
            PE.up(ins, "ksT")
            AC.wait(pe, "ksTsb")
            for h in range(H):
                ins = pe.transpose(bank[6][0:SMP, P * h:P * h + P], kq[:, SMP * h:SMP * h + SMP], ident[:, :])
            PE.up(ins, "ks2")
            DV.wait(pe, "rhs2")
            for h in range(H):
                ins = mm(bank[7][0:SMP, P * h:P * h + P], TT[2][:, SMP * h:SMP * h + SMP], rtmp[0:SMP, P * h:P * h + P])
            PE.up(ins, "vn2")
            AC.wait(pe, "vnsb2")
            for h in range(H):
                ins = mm(bank[5][:, SMP * h:SMP * h + SMP], vnew[0:SMP, P * h:P * h + P], IN[2][:, SMP * h:SMP * h + SMP])
            PE.up(ins, "o2")
            for h in range(H):
                DV.wait(pe, f"vnm{h}")
                if h == 0:
                    DV.wait(pe, "state1")
                if h == 1:
                    AC.wait(pe, "oT1")
                if h >= 2:
                    DV.wait(pe, f"stS{h - 2}")
                bk = 0 if h % 2 else 2
                mm(bank[bk][:, :], ktok[0:SMP, 2, P * h:P * h + P], vnm[:, 0:512])
                PE.up(mm(bank[bk + 1][:, :], ktok[0:SMP, 2, P * h:P * h + P], vnm[:, 512:1024]), f"stS{h}")
            for h in range(H):
                AC.wait(pe, f"osq{h}")
                DV.wait(pe, "stS3")
                PE.up(mm(bank[h][:, 0:TOK], ones[:, :], qg[:, h, :]), f"oss{h}")

            for i in range(6):
                at, n = TILES[i % 3]
                if i < 4:
                    AC.wait(pe, f"oln{i}")
                for h in range(H):
                    ins = pe.transpose(bank[i][0:n, P * h:P * h + P], mbh[:, 4 + 4 * (i // 3) + h, at:at + n], ident[:, :])
                PE.up(ins, f"kvT{i}")
            AC.wait(pe, "kvtok0")
            for h in range(H):
                ins = mm(bank[0][:, P * h:P * h + P], mbh[:, h, 0:P], mbh[:, 4 + h, 0:P])
            PE.up(ins, "ps0")
            AC.wait(pe, "kvtok2")
            for h in range(H):
                ins = mm(bank[1 + h // 2][:, 256 * (h % 2):256 * (h % 2) + 256], mbh[:, h, P:2 * P], mbh[:, 4 + h, 0:2 * P])
            PE.up(ins, "ps1")
            AC.wait(pe, "kvtok5")
            for g, (x, c0, t) in enumerate(((pl0, 0, 0), (pl1, 0, 1), (pl1, P, 1))):
                DV.wait(pe, f"pnorm{t}")
                for h in range(H):
                    ins = pe.transpose(bank[3 + g][:, P * h:P * h + P], x[:, h, c0:c0 + P], ident[:, :])
                PE.up(ins, f"pT{g}")
            for t in range(2):
                AC.wait(pe, f"pTsb{2 * t}")
                for h in range(H):
                    for c in range(t + 1):
                        ins = mm(bank[6 + t][:, P * h:P * h + P], kvtok[:, 1, c, P * h:P * h + P],
                                 pT[:, 512 * (t + c) + P * h:512 * (t + c) + P * h + P], c == 0, c == t)
                PE.up(ins, f"po{t}")

            DV.wait(pe, "pol1")
            DV.wait(pe, "rowc")
            DV.wait(pe, "vol")
            PO.wait(pe, "consts")

            def attend(b, c, d):
                def transpose(u):
                    g, h = divmod(u, H)
                    if h == 0:
                        pe.wait_ge(s[f"k_in{g % 2}"], b * 128 + 64 * (g // 2 + 1))
                    after(pe, "kT_lo", b * UNITS + (u - 1))
                    for j in range(4):
                        ins = pe.transpose(bank[u % 2][:, P * j:P * j + P], kring[:, g % 2, j, P * h:P * h + P], ident[:, :])
                    ins.then_inc(s["kT_mm"], 1)

                def score(u):
                    g, h = divmod(u, H)
                    pe.wait_ge(s["kT_lo"], b * UNITS + (u + 1))
                    if h == 0:
                        after(pe, "s_row", b * 4 + (g - 1))
                    out = bank[2 + g % 2][0:32, :]
                    mm(out, qph[:, h, :], kTh[:, u % 2, :], h == 0, False)
                    mm(out, qpl[:, h, :], kTh[:, u % 2, :], False, False)
                    mm(out, qph[:, h, :], kTl[:, u % 2, :], False, h == H - 1).then_inc(s["s_mm"], 1)

                def turn_probabilities():
                    PO.wait(pe, "ident_done")
                    pe.wait_ge(s["p_norm"], c + 1)
                    for j in range(NPG):
                        pe.transpose(bank[5][:, 32 * j:32 * j + 32], prob[0:32, PAGE * j:PAGE * j + PAGE], ident[0:32, 0:32])
                    pe.transpose(bank[7][0:SMP, 256:288], prob[0:32, PAST:], ident[0:32, 0:32]).then_inc(s["pT_mm"], 1)

                def values(w):
                    if w == 0:
                        after(pe, "o_row", d)
                        pe.wait_ge(s["pT_lo"], d + 1)
                    pe.wait_ge(s["v_lo"], d * VUNITS + (w + 1))
                    for j in range(2):
                        page = 2 * w + j
                        mm(bank[4][0:64, :], pTs[:, page, :, :].rearrange("p u r -> p (u r)"), vh[:, w % 2, j, :], page == 0,
                           False)
                        ins = mm(bank[4][0:32, :], pTs[:, page, 0, :], vl[:, w % 2, j, :], False, False)
                    if w == VUNITS - 1:
                        mm(bank[4][0:32, :], pTs[0:SMP, NPG, 0, :], vol[:, :], False, False)
                        ins = mm(bank[4][0:64, :], pTs[0:SMP, NPG, :, :].rearrange("p u r -> p (u r)"), voh[:, :], False, True)
                    ins.then_inc(s["v_mm"], 1)

                if b is not None:
                    transpose(0)
                for u in range(UNITS):
                    if b is not None:
                        if u + 1 < UNITS:
                            transpose(u + 1)
                        if u == 0:
                            pe.wait_ge(s["q_lo"], b + 1)
                            for h in range(H):
                                mm(bank[7][0:32, 0:SMP], qpf[:, h, :], mbh[:, 4 + h, SEQ:TOK], h == 0, h == H - 1)
                        score(u)
                    if d is not None and u % 2 == 0:
                        values(u // 2)
                    if c is not None and u == 10:
                        turn_probabilities()
                if d is not None:
                    pe.wait_ge(s["o_row"], d + 1)
                    for h in range(H):
                        ins = mm(bank[6][:, bass.ds(d * NT + SMP * h, NT)], orow[:, P * h:P * h + P],
                                 twice[:, NT * h:NT * h + NT])
                    return ins

            attend(0, None, None)
            attend(1, 0, None)
            with pe.Fori(2, NB) as b:
                attend(b, b - 1, b - 2)
            attend(None, NB - 1, NB - 2)
            PE.up(attend(None, None, NB - 1), "attn_mm")

            def stats(n):
                PO.wait(pe, f"accs{n}_6")
                mm(bank[4][:, 0:TOK], onesD[:, :], lnt[:, 0, :], True, False)
                DV.wait(pe, f"r{n}_7")
                mm(bank[4][:, 0:TOK], onesD[:, :], xres[:, 7, :], False, True)
                PO.wait(pe, f"accq{n}_6")
                mm(bank[5][:, 0:TOK], onesD[:, :], lnt[:, 1, :], True, False)
                AC.wait(pe, f"sq{n}_7")
                PE.up(mm(bank[5][:, 0:TOK], onesD[:, :], sq[:, 1, :], False, True), f"stat{n}")

            hist_loads = [1]

            def history(name, n):
                hist_loads[0] += 1
                pe.wait_ge(s["hist_in"], 16 * hist_loads[0])
                for c in range(n):
                    ins = pe.transpose(bank[6][:, 16 * c:16 * c + 16], rows[32:48, P * c:P * c + P], ident[32:48, 32:48])
                PE.up(ins, f"{name}_hist")

            def tails(name, n):
                PO.wait(pe, f"{name}_last")
                for g in range((n + 3) // 4):
                    if g >= 2:
                        AC.wait(pe, f"{name}_tail{g - 2}")
                    for c in range(4 * g, min(n, 4 * g + 4)):
                        ins = pe.transpose(bank[4 + g % 2 * 3][0:18, P * (c % 4):P * (c % 4) + P],
                                           last2[:, 18 * c:18 * c + 18], ident[:, :])
                    PE.up(ins, f"{name}_tail{g}")

            def nothing(_):
                pass

            def feed_forward(layer, n):
                base = S_UP[layer]
                with pe.Fori(0, SLOT_FFN) as i:
                    def free(j):
                        if j < 2:
                            pe.wait_ge(s["rel_act"], 2 * i + (REL[layer] - 2 + j + 1))
                        else:
                            pe.wait_ge(s["h_done"], 2 * i + (KF * layer + j - 2 + 1))
                    project(i + base, xh, xl, KD, free, lambda k: DV.wait(pe, f"x{n - 1}_{k}"))
                pe.wait_ge(s["h_done"], KF * (layer + 1) + 2)
                tails(f"f{layer}", KF)
                for i in range(2):
                    for k in range(3):
                        nk = min(KD, KF - KD * k)

                        def free(j):
                            if i:
                                DV.wait(pe, f"r{n}_{j}")
                        project(S_DOWN[layer] + 3 * i + k, hh, hl, nk, free,
                                lambda q: pe.wait_ge(s["hid_ready"], KF * layer + q + 1), KD * k, k == 0, k == 2)
                stats(n)

            def out_proj(base, xa, xb, ready, n, free0):
                for i in range(SLOT_OUT):
                    project(base + i, xa, xb, KD, free0 if i == 0 else lambda j: DV.wait(pe, f"r{n}_{j}"), ready)
                stats(n)

            DV.wait(pe, "attn_end")
            history("f0", KF)
            out_proj(S_OUT, xh, xl, nothing, 0, nothing)
            feed_forward(0, 1)
            history("sc", KD)
            with pe.Fori(0, 4) as i:
                def free(j):
                    if j < 2:
                        pe.wait_ge(s["rel_act"], 2 * i + (REL_SC - 2 + j + 1))
                    else:
                        pe.wait_ge(s["sc_prod"], 2 * i + (j - 2 + 1))
                project(i + S_SC, xh, xl, KD, free, lambda k: DV.wait(pe, f"x1_{k}"))
            for i in range(2):
                def free(j):
                    if i:
                        DV.wait(pe, f"scp{j}")
                    elif j < 2:
                        pe.wait_ge(s["rel_act"], REL_SC + KD)
                    else:
                        pe.wait_ge(s["sc_prod"], KD + 2)
                project(S_SC + 4 + i, xh, xl, KD, free, nothing)
            tails("sc", KD)
            out_proj(S_SCO, hh, hl, lambda k: DV.wait(pe, f"schl{k}"), 2, lambda j: DV.wait(pe, f"scp{4 + j}"))
            history("f1", KF)
            feed_forward(1, 3)
            for i in range(6):
                at, n = TILES[i // 2]
                for c in range(4):
                    m = 4 * (i % 2) + c
                    AC.wait(pe, f"ln3_{m}")
                    ins = pe.transpose(bank[i][0:n, P * c:P * c + P], xres[:, m, at:at + n], ident[:, :])
                PE.up(ins, f"yT{i}")



_INS = ["x_prompt", "x_sample", "cache_k", "cache_v", "state_dn", "state_dn_conv", "state_sc_conv", "state_ffn_conv",
        "page_table", "w_in_mix", "dn_conv_w", "dn_a_log", "dn_dt_bias", "dn_norm_w", "w_out_mix", "w_in_sc", "sc_conv_w",
        "w_out_sc", "ln_mix_g", "ln_mix_b", "w_up", "ffn_conv_w", "w_down", "ln_ffn_g", "ln_ffn_b"]
_OUTS = [("y_p", (1, SEQ, D)), ("y_s", (NB, NT, D)), ("k_p", (1, 1, SEQ, H, HD)), ("v_p", (1, 1, SEQ, H, HD)),
         ("k_s", (1, NB, NT, H, HD)), ("v_s", (1, NB, NT, H, HD)), ("dn_p", (1, 1, H, HD, HD)),
         ("dn_s", (1, NB, H, HD, HD)), ("dnc_p", (1, 1, 3, DNW)), ("dnc_s", (1, NB, 3, DNW)), ("scc_p", (1, 1, 2, D)),
         ("scc_s", (1, NB, 2, D)), ("ffc_p", (2, 1, 2, DFF)), ("ffc_s", (2, NB, 2, DFF))]


def kernel(**inputs):
    import numpy as np
    import concourse.bacc as bacc
    from concourse.bass_utils import run_bass_kernel_spmd as run

    nc = bacc.Bacc("TRN2", target_bir_lowering=False, num_devices=1)
    arrays = {n: np.ascontiguousarray(inputs[n]) for n in _INS}
    a = {n: nc.dram_tensor(n, x.shape, mybir.dt.from_np(x.dtype), kind="ExternalInput").ap() for n, x in arrays.items()}
    o = {n: nc.dram_tensor(n, shape, F32, kind="ExternalOutput").ap() for n, shape in _OUTS}
    trunk_program(nc, a, o)
    r = run(nc, [arrays], core_ids=[0])
    return tuple(r.results[0][n] for n, _ in _OUTS)
```

```python
from contextlib import ExitStack

import concourse.bass as bass
from concourse import mybir

F32 = mybir.dt.float32
F32R = mybir.dt.float32r
I32 = mybir.dt.int32
ALU = mybir.AluOpType
ACT = mybir.ActivationFunctionType
AX = mybir.AxisListType

P = 128
D = 1024
KD = D // P
SEQ, NB, NT = 256, 8, 8
SMP = NB * NT
TOK = SEQ + SMP
H, HD = 4, 128
PAST, PAGE, POOL = 2048, 128, 160
NPG = PAST // PAGE
BLK = 256
NBLK = PAST // BLK
TOPK = 3
DFF = 2816
KF = DFF // P
DNW = 3 * H * HD
ALPHA = 4.0 ** 0.25
SCALE = HD ** -0.5
LN_EPS, NORM_EPS = 1e-5, 1e-6
NEG = -1e30
SLOPES = [2.0 ** (-8.0 * (h + 1) / H) for h in range(H)]
TILES = [(0, 128), (128, 128), (256, 64)]

WD = 356
WF = 348
LD, LF = 344, 336

SLOT_MIX, SLOT_OUT, SLOT_FFN, SLOT_DOWN, SLOT_SC = 7, 2, KF // 2, 6, 6
S_MIX = 0
S_OUT = S_MIX + SLOT_MIX
S_UP = [S_OUT + SLOT_OUT]
S_DOWN = [S_UP[0] + SLOT_FFN]
S_SC = S_DOWN[0] + SLOT_DOWN
S_SCO = S_SC + SLOT_SC
S_UP.append(S_SCO + SLOT_OUT)
S_DOWN.append(S_UP[1] + SLOT_FFN)
S_END = S_DOWN[1] + SLOT_DOWN
CREDIT = 4

PA_DN, PA_SC, PA_LMG, PA_LMB, PA_NW, PA_N = 0, 48, 72, 88, 104, 105
PB_F, PB_LFG, PB_LFB, PB_N = 0, 66, 82, 98
PC_N = 66

SEMS = """
params_in xtok_in hist_in wba_in pt_in raw_in k_in0 k_in1 v_in0 v_in1 s0_in0 stores
hi_done lo_done chunk_done rel_act conv_step
kT_mm kT_hi kT_lo q_fp q_hi q_lo s_mm s_bias s_row s_max row shifted p_exp p_norm pT_mm pT_hi pT_lo
v_hi v_lo v_mm o_row
gelu_done h_done hh_done hid_ready sc_prod
pe_step act_step dve_step pool_step
""".split()


class Steps:

    def __init__(self, sem, names):
        self.sem, self.names, self.made = sem, names, []
        self.value = {n: i + 1 for i, n in enumerate(names)}

    def up(self, ins, name):
        self.made.append(name)
        assert self.names[len(self.made) - 1] == name, (name, len(self.made))
        ins.then_inc(self.sem, 1)

    def wait(self, eng, name):
        eng.wait_ge(self.sem, self.value[name])


STEPS = {
    "pe": """
xT0 xT1 xT2 xT3 xT4 xT5 xT6 xT7 parT histT ba dntail0 dntail1 dntail2 ss0 ss1 ss2 ss3 ss4 ss5 ss6 ss7 cum0 kk0 tok0
cum1 kk1 cum2 tok1 kk2 tok2 invw0 invw1 invw2 ksT invw3 invw4 invw5 ks2 invu3 invu4 invu5 invw6 invw7 invw8 invu6
invu7 invu8 invw9 invw10 invu9 invu10 invw11 invw12 invu11 invu12 invw13 invw14 invu13 invu14 invw15 invw16 invu15
invu16 vn0 vn2 o0 st0 o2 ks1 stS0 vn1 stS1 o1 st1 stS2 stS3 oss0 oss1 oss2 oss3 kvT0 kvT1 kvT2 ps0 ps1 kvT3 kvT4 kvT5
pT0 pT1 pT2 po0 po1 attn_mm f0_hist mean0 stat0 f0_tail0 f0_tail1 f0_tail2 f0_tail3 f0_tail4 f0_tail5 mean1 stat1
sc_hist sc_tail0 sc_tail1 f1_hist mean2 stat2 f1_tail0 f1_tail1 f1_tail2 f1_tail3 f1_tail4 f1_tail5 mean3 stat3 yT0
yT1 yT2 yT3 yT4 yT5
""".split(),
    "act": """
xh0 xh1 xh2 xh3 xh4 xh5 xh6 xh7 par0 par1 par2 hist silu gexp dntail0 dntail1 dntail2 gln l2sq0 l2sq1 l2sq2 l2sq3
l2sq4 l2sq5 l2sq6 l2sq7 ssln0 ssln1 ssln2 ssln3 rn0 ssln4 ssln5 ssln6 ssln7 rn1 egc0 egcb0 decay0 egc1 egcb1 decay1
egc2 egcb2 decay2 ksTsb wsb3 wsb4 wsb5 wsb6 wsb7 wsb8 wsb9 wsb10 wsb11 wsb12 wsb13 wsb14 wsb15 wsb16 vnsb0 vnsb2 oT0
vnsb1 oT1 osq0 osq1 osq2 osq3 oln0 oln1 oln2 oln3 orn mixh_done kvtok0 kvtok1 kvtok2 kvtok3 kvtok4 kvtok5 pexp0 pexp1
pexp2 pexp3 pexp4 pexp5 pexp6 pexp7 pTsb0 pTsb1 pTsb2 poh0 poh1 voh attn_endh sq0_0 sq0_1 sq0_2 sq0_3 sq0_4 sq0_5
sq0_6 sq0_7 msq0 lnv0 rstd0 ln0_0 lnh0_0 ln0_1 lnh0_1 ln0_2 lnh0_2 ln0_3 lnh0_3 ln0_4 lnh0_4 ln0_5 lnh0_5 ln0_6 lnh0_6
ln0_7 lnh0_7 f0_hist f0_tail0 f0_tail1 f0_tail2 f0_tail3 f0_tail4 f0_tail5 sq1_0 sq1_1 sq1_2 sq1_3 sq1_4 sq1_5 sq1_6
sq1_7 msq1 lnv1 rstd1 ln1_0 lnh1_0 ln1_1 lnh1_1 ln1_2 lnh1_2 ln1_3 lnh1_3 ln1_4 lnh1_4 ln1_5 lnh1_5 ln1_6 lnh1_6 ln1_7
lnh1_7 sc_hist sch0 sch1 sch2 sch3 sch4 sch5 sch6 sch7 sc_tail0 sc_tail1 sq2_0 sq2_1 sq2_2 sq2_3 sq2_4 sq2_5 sq2_6
sq2_7 msq2 lnv2 rstd2 ln2_0 lnh2_0 ln2_1 lnh2_1 ln2_2 lnh2_2 ln2_3 lnh2_3 ln2_4 lnh2_4 ln2_5 lnh2_5 ln2_6 lnh2_6 ln2_7
lnh2_7 f1_hist f1_tail0 f1_tail1 f1_tail2 f1_tail3 f1_tail4 f1_tail5 sq3_0 sq3_1 sq3_2 sq3_3 sq3_4 sq3_5 sq3_6 sq3_7
msq3 lnv3 rstd3 ln3_0 ln3_1 ln3_2 ln3_3 ln3_4 ln3_5 ln3_6 ln3_7 y0 y1 y2 y3 y4 y5
""".split(),
    "dve": """
gz pages xres0 xres1 xres2 xres3 xres4 xres5 xres6 xres7 xl0 xl1 xl2 xl3 xl4 xl5 xl6 xl7 ba gxa gx gone beta gsp g ug0
qknorm qkn gcl0 cumsb0 dmax0 dmat0 ug1 mask0 La0 intra0 L0 tok0 qg0 gcl1 cumsb1 dmax1 dmat1 ug2 mask1 La1 intra1 L1
tok1 qg1 gcl2 cumsb2 dmax2 dmat2 mask2 La2 intra2 L2 tok2 qg2 inv0 inv1 inv2 rhsa2 rhs2 inv3 inv4 inv5 inv6 inv7 inv8
inv9 inv10 inv11 inv12 inv13 inv14 inv15 inv16 vnm0 state0 rhsa1 rhs1 vnm1 oT2 stS0 vnm2 statea state1 stS1 vnm3 stS2
stS3 rowc0 rowc on1 mixo keyb mixl_done plog0 pmaxa0 pmax0 plog1 pmaxa1 pmax1 prec0 pnorm0 prec1 pnorm1 pol0 pol1 vol
attn_end r0_0 r0_1 r0_2 r0_3 r0_4 r0_5 r0_6 r0_7 mean0 vara0 var0 centred0 t2_0_0 t2_0_1 t2_0_2 t2_0_3 t2_0_4 t2_0_5
t2_0_6 t2_0_7 r1_0 r1_1 r1_2 r1_3 r1_4 r1_5 r1_6 r1_7 mean1 vara1 var1 centred1 t2_1_0 t2_1_1 t2_1_2 t2_1_3 t2_1_4
t2_1_5 t2_1_6 t2_1_7 scp0 schl0 scp1 schl1 scp2 schl2 scp3 schl3 scp4 schl4 scp5 schl5 scp6 schl6 scp7 schl7 sc_gated
r2_0 r2_1 r2_2 r2_3 r2_4 r2_5 r2_6 r2_7 mean2 vara2 var2 centred2 t2_2_0 t2_2_1 t2_2_2 t2_2_3 t2_2_4 t2_2_5 t2_2_6
t2_2_7 r3_0 r3_1 r3_2 r3_3 r3_4 r3_5 r3_6 r3_7 mean3 vara3 var3 centred3 t2_3_0 t2_3_1 t2_3_2 t2_3_3 t2_3_4 t2_3_5
t2_3_6 t2_3_7
""".split(),
    "pool": """
const0 const1 ident_done const2 const3 cin_zero const4 const5 const6 const7 const8 const9 const10 const11 const12
const13 const14 const15 const16 const17 const18 const19 const20 const21 const22 const23 const24 const25 const26
const27 const28 const29 const30 const31 const32 const33 const34 const35 const36 const37 const38 const39 const40
const41 const42 const43 const44 const45 const46 const47 const48 const49 const50 const51 const52 const53 const54
const55 const56 const57 const58 consts dnlast lm0 lm1 lm2 lm3 lm4 lm5 lm6 lm7 lm8 lm9 lm10 lm11 lm12 lm13 lm14 lm15
lm16 s0g0 s0g1 s0g2 s0g3 f0_zero accs0_1 accq0_0 accq0_1 accs0_2 accq0_2 accs0_3 accq0_3 accs0_4 accq0_4 accs0_5
accq0_5 x0_0 x0_1 x0_2 x0_3 x0_4 x0_5 x0_6 x0_7 f0_last sc_zero accs1_1 accq1_0 accq1_1 accs1_2 accq1_2 accs1_3
accq1_3 accs1_4 accq1_4 accs1_5 accq1_5 x1_0 x1_1 x1_2 x1_3 x1_4 x1_5 x1_6 x1_7 sc_last f1_zero accs2_1 accq2_0
accq2_1 accs2_2 accq2_2 accs2_3 accq2_3 accs2_4 accq2_4 accs2_5 accq2_5 x2_0 x2_1 x2_2 x2_3 x2_4 x2_5 x2_6 x2_7
f1_last accs3_1 accq3_0 accq3_1 accs3_2 accq3_2 accs3_3 accq3_3 accs3_4 accq3_4 accs3_5 accq3_5
""".split(),
}


def trunk_program(nc, a, o):
    ctx = ExitStack()
    with ctx:
        def sb(name, shape, dt=F32, stack=ctx):
            return stack.enter_context(nc.sbuf_tensor(name, shape, dt))

        s = {n: ctx.enter_context(nc.semaphore(n)) for n in SEMS}
        bank = [ctx.enter_context(nc.psum_tensor(f"bank{i}", [P, 512], F32)) for i in range(8)]

        raw = sb("raw", [P, 2 * KD * 512])
        hi = sb("hi", [P, 2, KD, 256], F32R)
        lo = sb("lo", [P, 2, KD, 256], F32R)
        xh = sb("xh", [P, KD, TOK], F32R)
        xl = sb("xl", [P, KD, TOK], F32R)
        xres = sb("xres", [P, KD, TOK])
        par = sb("par", [P, 3, P])
        ident = sb("ident", [P, P])
        ptab = sb("ptab", [1, NB * NPG], I32)
        pair = sb("pair", [1, NB * NPG // 2], I32)
        ones = sb("ones", [P, P])
        onesD = sb("onesD", [P, P])
        eps6 = sb("eps6", [P, 2])
        scrap = sb("scrap", [P, 3, 8])

        sA = ExitStack()
        mb = sb("mb", [P, 12 * TOK], stack=sA)
        upper = sb("upper", [P, P], stack=sA)
        lower = sb("lower", [P, P], stack=sA)
        bdiff = sb("bdiff", [P, 7, P], stack=sA)
        same8 = sb("same8", [SMP, SMP], stack=sA)
        upper8 = sb("upper8", [SMP, SMP], stack=sA)
        lower8 = sb("lower8", [SMP, SMP], stack=sA)
        ltri = sb("ltri", [32, NBLK, NBLK], stack=sA)
        promptb = sb("promptb", [P, H, 256], stack=sA)
        c128 = sb("c128", [32, 128], stack=sA)
        back = sb("back", [32, NPG + 1], stack=sA)
        slope = sb("slope", [32, 1], stack=sA)
        ownb = sb("ownb", [32, 120], stack=sA)
        gates = sb("gates", [P, 14, 12], stack=sA)
        dtal = sb("dtal", [P, 2, H], stack=sA)
        s1 = ExitStack()
        zsb = sb("zsb", [P, H, TOK], stack=s1)
        qkv = sb("qkv", [P, 12 * WF], stack=s1)
        s11 = ExitStack()
        cin = sb("cin", [P, 12 * WD], stack=s11)
        xtok = sb("xtok", [P, 3, D], stack=s11)
        prows = sb("prows", [P, 3, P], stack=s11)
        dnrows = sb("dnrows", [64, DNW], stack=s11)
        wba = sb("wba", [P, KD, 8], stack=s11)
        iot = sb("iot", [P, 512], I32, stack=s11)
        iof = sb("iof", [P, 512], stack=s11)
        bs = sb("bs", [P, 8, P], stack=s11)
        s11.close()
        s2 = ExitStack()
        tP = sb("tP", [P, 2, 512], stack=s2)
        ttP = sb("ttP", [P, 2, 512], stack=s2)
        lP = sb("lP", [P, 2, 512], stack=s2)
        inP = sb("inP", [P, 2, 512], stack=s2)
        tS = sb("tS", [SMP, 256], stack=s2)
        ttS = sb("ttS", [SMP, 256], stack=s2)
        lS = sb("lS", [SMP, 256], stack=s2)
        inS = sb("inS", [SMP, 256], stack=s2)
        work = sb("work", [P, 4096], stack=s2)
        ktok = sb("ktok", [P, 3, 512], stack=s2)
        vtok = sb("vtok", [P, 3, 512], stack=s2)
        qg = sb("qg", [P, H, TOK], stack=s2)
        spr = sb("spr", [P, 512], stack=s2)
        rtmp = sb("rtmp", [P, 512], stack=s2)
        vnew = sb("vnew", [P, 512], stack=s2)
        eglS = sb("eglS", [P, 32], stack=s2)
        s2.close()
        s1.close()
        s3 = ExitStack()
        vring = sb("vring", [P, 2, 4, 512], stack=s3)
        sbias = sb("sbias", [P, PAST + SMP], stack=s3)
        prob = sb("prob", [P, PAST + SMP], stack=s3)
        kTh = sb("kTh", [P, 2, 512], F32R, stack=s3)
        kTl = sb("kTl", [P, 2, 512], F32R, stack=s3)
        qpf = sb("qpf", [P, 2, H, 32], stack=s3)
        qph = sb("qph", [P, 2, H, 32], F32R, stack=s3)
        qpl = sb("qpl", [P, 2, H, 32], F32R, stack=s3)
        kring = sb("kring", [P, 2, 4, 512], stack=s3)
        pTs = sb("pTs", [P, NPG + 1, 2, 32], F32R, stack=s3)
        kvtok = sb("kvtok", [P, 2, 3, 512], stack=s3)
        voh = sb("voh", [SMP, 512], F32R, stack=s3)
        vol = sb("vol", [SMP, 512], F32R, stack=s3)
        pst = sb("pst", [P, 3, 8], stack=s3)
        twice = sb("twice", [SMP, 32], stack=s3)
        gsum = sb("gsum", [32, NBLK], stack=s3)
        bmax = sb("bmax", [32, NBLK + 1], stack=s3)
        pen = sb("pen", [32, NBLK + 1], stack=s3)
        shift = sb("shift", [32, NBLK + 1], stack=s3)
        dn = sb("dn", [32, NBLK + 1], stack=s3)
        rk = sb("rk", [32, 2, NBLK * NBLK], stack=s3)
        r1 = sb("r1", [32, 4], stack=s3)
        rank = sb("rank", [32, NBLK], stack=s3)
        s3.close()
        sA.close()

        hh = sb("hh", [P, KF, TOK], F32R)
        hl = sb("hl", [P, KF, TOK], F32R)
        cb = sb("cb", [P, KF * WF])
        rows = sb("rows", [64, DFF])
        acc = sb("acc", [P, 2 * WF])
        hraw = sb("hraw", [P, 2, TOK])
        sq = sb("sq", [P, 2, TOK])
        lnt = sb("lnt", [P, 5, TOK])

        step = {e: Steps(s[f"{e}_step"], STEPS[e]) for e in ("pe", "act", "dve", "pool")}
        PE, AC, DV, PO = step["pe"], step["act"], step["dve"], step["pool"]

        spares = [0, 0, 0]

        def spare(e):
            spares[e] += 1
            return scrap[:, e, spares[e] - 1:spares[e]]

        def t4(x, n=P):
            return x.rearrange("p (h c) -> p h c", h=H)

        def tri(t):
            return (upper[:], lower[:]) if t < 2 else (upper8[:], lower8[:])

        def mid(x, n):
            return x.rearrange("p (a c) -> p a c", a=1).to_broadcast([x.shape[0], n, x.shape[1]])

        def last(x, n):
            return x.rearrange("p (c a) -> p c a", a=1).to_broadcast([x.shape[0], x.shape[1], n])

        def gate(i, t, n=P):
            return gates[0:n, i, 4 * t:4 * t + 4]

        B_, X_, NX, L1, EB, BETA, G_, GC, EGC, NBE, KD_, GL, EGL = range(13)
        T_ = [tP[:, 0, :], tP[:, 1, :], tS[:]]
        TT = [ttP[:, 0, :], ttP[:, 1, :], ttS[:]]
        L_ = [lP[:, 0, :], lP[:, 1, :], lS[:]]
        IN = [inP[:, 0, :], inP[:, 1, :], inS[:]]
        member = same8[:, 0:SMP:NT]
        sc0 = work[:, :]
        s0 = raw[:, 0:4096].rearrange("p (i v) -> p i v", v=HD)
        lmb = [sc0[:, 512 * i:512 * i + 512] for i in range(2)]
        wsb = [sc0[:, 1024:1536], sc0[:, 1536:2048], sc0[0:SMP, 2048:2304]]
        dsc = [sc0[:, 2304:2816], sc0[:, 2816:3328]]
        kq = qkv[:, 8 * WF:8 * WF + 512]
        vnm = [tP[0:SMP, :, :].rearrange("p a c -> p (a c)"), sc0[0:SMP, 1024:2048]]
        rhsS, vnewS = dsc[0][0:SMP, :], dsc[1][0:SMP, :]
        qk3 = qkv[:, :].rearrange("p (c w) -> p c w", w=WF)
        oT = qk3[:, 0:4, 0:TOK]
        INV = [(l, t) for l in range(7) for t in range(3) if t < 2 or l < 3]

        smp = sc0[:, 3328:4096].rearrange("p (c w) -> p c w", w=SMP)

        def head(c, t):
            return qk3[:, c, 128 * t:128 * t + 128] if t < 2 else smp[:, c, :]

        def weight(i):
            return raw[:, bass.ds(i % 2 * (KD * 512), KD * 512)].rearrange("p (k c) -> p k c", c=512)

        def vec(pack, row):
            return par[:, pack, row:row + 1]

        par2 = par[:, :, :].rearrange("p a c -> p (a c)")

        l2n = sc0[:, 0:8 * LD].rearrange("p (c w) -> p c w", w=LD)
        vr = vring[:, :, :, :].rearrange("p a j c -> p (a j c)")
        pl0 = vr[:, 0:512].rearrange("p (h c) -> p h c", h=H)
        pl1 = vr[:, 512:1536].rearrange("p (h c) -> p h c", h=H)
        pT = vr[:, 1536:3072]
        PROMPT = {1: "kv0", 3: "scores", 5: "kv1", 10: "turn", 13: "values"}

        vh = hi[:, 1].rearrange("p k c -> p (k c)").rearrange("p (w j c) -> p w j c", w=2, c=512)
        vl = lo[:, 1].rearrange("p k c -> p (k c)").rearrange("p (w j c) -> p w j c", w=2, c=512)
        keyb = raw[0:32, 0:PAST]
        orow = raw[0:SMP, PAST:PAST + 512]
        UNITS, VUNITS = 16, 8

        pTf = raw[:, PAST + 512:PAST + 512 + 32 * (NPG + 1)].rearrange("p (j r) -> p j r", r=32)
        WHOLE = NB - 2

        def whole(c):
            return isinstance(c, int) and c >= WHOLE

        def after(eng, sem, value):
            if not isinstance(value, int) or value > 0:
                eng.wait_ge(s[sem], value)

        last2 = acc[:, :]
        mbh = mb[:, :].rearrange("p (c w) -> p c w", w=TOK)
        CONV = [48, 48 + 3 * KF + 3 * KD]
        REL = [32, 32 + KF + KD]
        TAIL_BANK = (4, 7, 6)
        REL_SC, CONV_SC = 32 + KF, 48 + 3 * KF

        def hraw_y(t):
            return cb[0:TILES[t][1], D * t:D * t + D]

        block = ctx.enter_context(nc.Block())

        @block.sync
        def _(sp_):
            w_mix = a["w_in_mix"][0].rearrange("(k p) c -> p k c", p=P)
            w_out = a["w_out_mix"][0].rearrange("(k p) c -> p k c", p=P)
            w_sc = a["w_in_sc"][0].rearrange("(k p) c -> p k c", p=P)
            w_so = a["w_out_sc"][0].rearrange("(k p) c -> p k c", p=P)

            def slot_free(n):
                sp_.wait_ge(s["lo_done"], 2 * (n - 1))
                sp_.wait_ge(s["raw_in"], 32 * n)

            def load_whole(n, src, nk=KD):
                sp_.dma_start(weight(n)[:, 0:nk, :], src).then_inc(s["raw_in"], 32)

            sp_.dma_start(ptab[:, :], a["page_table"].rearrange("(a b) n -> a (b n)", a=1)).then_inc(s["pt_in"], 16)
            sp_.dma_start(xtok[:, 0:2, :], a["x_prompt"][0].rearrange("(t p) d -> p t d", p=P)).then_inc(s["xtok_in"], 16)
            sp_.dma_start(xtok[0:SMP, 2, :], a["x_sample"].rearrange("b t d -> (b t) d")).then_inc(s["xtok_in"], 16)
            for n in range(SLOT_MIX):
                if n == 1:
                    sp_.wait_ge(s["raw_in"], 32)
                if n > 1:
                    slot_free(n)
                c0 = 512 * n if n < 4 else 2056 + 512 * (n - 4)
                load_whole(n, w_mix[:, :, c0:c0 + 512])
            slot_free(S_OUT)
            load_whole(S_OUT, w_out[:, :, 0:512])

            DV.wait(sp_, "stS3")
            AC.wait(sp_, "oT1")
            DV.wait(sp_, "pages")

            def load_pages(ring, cache, landed, b, g):
                words = [sp_.value_load(pair[0:1, bass.ds(b * (NPG // 2) + (2 * g + j), 1)], min_val=0,
                                        max_val=POOL * POOL - 1) for j in range(2)]
                return [(ring[:, g % 2, 2 * j + u, :], cache[bass.ds(x, 1)].rearrange("o p h d -> (o p) (h d)"), landed)
                        for j, w in enumerate(words) for u, x in enumerate((w % POOL, w // POOL))]

            def start(loads):
                for dst, src, landed in loads:
                    sp_.dma_start(dst, src).then_inc(s[landed], 16)

            def load_k(b, g):
                loads = load_pages(kring, a["cache_k"][0], f"k_in{g % 2}", b, g)
                after(sp_, "kT_mm", b * UNITS + 4 * (g - 1))
                start(loads)

            def load_v(b, g):
                loads = load_pages(vring, a["cache_v"][0], f"v_in{g % 2}", b, g)
                before = b if g >= 2 else b - 1
                after(sp_, "v_mm" if whole(before) else "v_lo", b * VUNITS + (2 * g - 2))
                start(loads)

            def pages(b, c, d, n):
                for g in range(2):
                    if d is not None:
                        load_v(d, 2 + g)
                    if b is not None:
                        load_k(b, 2 + g)
                for g in range(2):
                    if c is not None:
                        load_v(c, g)
                    if n is not None:
                        load_k(n, g)

            pages(None, None, None, 0)
            pages(0, None, None, 1)
            PE.wait(sp_, "po1")
            DV.wait(sp_, "pnorm1")
            pages(1, 0, None, 2)
            with sp_.Fori(2, NB - 1) as b:
                pages(b, b - 1, b - 2, b + 1)
            pages(NB - 1, NB - 2, NB - 3, None)
            pages(None, NB - 1, NB - 2, None)
            pages(None, None, NB - 1, None)
            PE.wait(sp_, "attn_mm")
            slot_free(S_OUT + 1)
            load_whole(S_OUT + 1, w_out[:, :, 512:1024])

            def feed_forward(layer):
                w_up = a["w_up"][layer].rearrange("(k p) c -> p k c", p=P)
                w_dn = a["w_down"][layer].rearrange("(k p) c -> p k c", p=P)
                with sp_.Fori(0, SLOT_FFN) as i:
                    slot_free(i + S_UP[layer])
                    w = weight(i + S_UP[layer])
                    sp_.dma_start(w[:, :, 0:256], w_up[:, :, bass.ds(i * 256, 256)]).then_inc(s["raw_in"], 16)
                    sp_.dma_start(w[:, :, 256:512], w_up[:, :, bass.ds(i * 256 + DFF, 256)]).then_inc(s["raw_in"], 16)
                with sp_.Fori(0, 2) as i:
                    for k in range(3):
                        n = 3 * i + (S_DOWN[layer] + k)
                        nk = min(KD, KF - KD * k)
                        slot_free(n)
                        load_whole(n, w_dn[:, KD * k:KD * k + nk, bass.ds(i * 512, 512)], nk)

            feed_forward(0)
            with sp_.Fori(0, 4) as i:
                slot_free(i + S_SC)
                w = weight(i + S_SC)
                sp_.dma_start(w[:, :, 0:256], w_sc[:, :, bass.ds(i * 256 + D, 256)]).then_inc(s["raw_in"], 16)
                sp_.dma_start(w[:, :, 256:512], w_sc[:, :, bass.ds(i * 256 + 2 * D, 256)]).then_inc(s["raw_in"], 16)
            with sp_.Fori(0, 2) as i:
                slot_free(i + (S_SC + 4))
                load_whole(i + (S_SC + 4), w_sc[:, :, bass.ds(i * 512, 512)])
            with sp_.Fori(0, SLOT_OUT) as i:
                slot_free(i + S_SCO)
                load_whole(i + S_SCO, w_so[:, :, bass.ds(i * 512, 512)])
            feed_forward(1)

        @block.gpsimd
        def _(pool):
            made = [0]

            def link(ins):
                PO.up(ins, f"const{made[0]}")
                PO.wait(pool, f"const{made[0]}")
                made[0] += 1

            def select(x, pattern, base, cm, fill, op=ALU.is_ge):
                link(pool.affine_select(out=x, in_=x, compare_op=op, fill=fill, base=base, pattern=pattern,
                                        channel_multiplier=cm))

            link(pool.memset(ident[:], 0.0))
            select(ident[:], [[-1, P]], 0, 1, 1.0, ALU.not_equal)
            PO.up(pool.memset(ones[:], 1.0), "ident_done")

            PAR = [(a["dn_conv_w"].rearrange("l k (c p) -> (l k c) p", p=P), 0, PA_DN, 48),
                   (a["sc_conv_w"].rearrange("l k (c p) -> (l k c) p", p=P), 0, PA_SC, 24),
                   (a["ln_mix_g"].rearrange("l (c p) -> (l c) p", p=P), 0, PA_LMG, 16),
                   (a["ln_mix_b"].rearrange("l (c p) -> (l c) p", p=P), 0, PA_LMB, 16),
                   (a["dn_norm_w"], 0, PA_NW, 1),
                   (a["ffn_conv_w"][0].rearrange("k (c p) -> (k c) p", p=P), 1, PB_F, 66),
                   (a["ln_ffn_g"].rearrange("l (c p) -> (l c) p", p=P), 1, PB_LFG, 16),
                   (a["ln_ffn_b"].rearrange("l (c p) -> (l c) p", p=P), 1, PB_LFB, 16),
                   (a["ffn_conv_w"][1].rearrange("k (c p) -> (k c) p", p=P), 2, 0, 66)]
            for src, pack, row, n in PAR:
                pool.dma_start(prows[row:row + n, pack, :], src).then_inc(s["params_in"], 16)
            pool.dma_start(dnrows[0:24, :], a["state_dn_conv"][0].rearrange("b k c -> (b k) c")).then_inc(s["hist_in"], 16)
            with nc.allow_non_contiguous_dma(reason="eight gate columns of a wide row"):
                pool.dma_start(wba[:, :, :], a["w_in_mix"][0].rearrange("(k p) c -> p k c", p=P)[:, :, 2048:2056])\
                    .then_inc(s["wba_in"], 16)
            pool.dma_start(dtal[:, 0, :], a["dn_dt_bias"][0:1, :].to_broadcast([P, H])).then_inc(s["wba_in"], 16)
            pool.dma_start(dtal[:, 1, :], a["dn_a_log"][0:1, :].to_broadcast([P, H])).then_inc(s["wba_in"], 16)

            link(pool.memset(onesD[:], 1.0 / D))
            link(pool.memset(eps6[:], NORM_EPS))
            cin3 = cin[:, :].rearrange("p (c w) -> p c w", w=WD)
            PO.up(pool.memset(cin3[:, :, 0:3], 0.0), "cin_zero")
            link(pool.memset(upper[:], 1.0))
            select(upper[:], [[1, P]], 0, -1, 0.0)
            link(pool.memset(lower[:], 1.0))
            select(lower[:], [[-1, P]], -1, 1, 0.0)
            link(pool.memset(bs[:, 7, :], 1.0))
            link(pool.tensor_copy(bs[:, 0, :], ident[:]))
            for l in range(1, 7):
                z, n = 1 << l, P >> l
                link(pool.memset(bs[:, l, :], 1.0))
                x = bs[:, l, :].rearrange("p (n z) -> p n z", z=z)
                select(x, [[-z, n], [0, z]], 0, 1, 0.0)
                select(x, [[z, n], [0, z]], z - 1, -1, 0.0)
            link(pool.tensor_sub(bdiff[:, :, :], bs[:, 1:8, :], bs[:, 0:7, :]))
            link(pool.tensor_copy(same8[:], bs[0:SMP, 3, 0:SMP]))
            link(pool.tensor_mul(upper8[:], upper[0:SMP, 0:SMP], same8[:]))
            link(pool.tensor_mul(lower8[:], lower[0:SMP, 0:SMP], same8[:]))
            link(pool.memset(ltri[:], 1.0))
            select(ltri[:], [[1, NBLK], [-1, NBLK]], -1, 0, 0.0)
            link(pool.iota(iot[:, 128:384], pattern=[[1, 256]], base=-128, channel_multiplier=-1))
            link(pool.iota(iot[:, 0:128], pattern=[[1, 128]], base=0, channel_multiplier=0))
            link(pool.iota(iot[:, 384:401], pattern=[[-PAGE, NPG + 1]], base=PAST, channel_multiplier=1))
            link(pool.tensor_copy(iof[:, 0:401], iot[:, 0:401]))
            for h in range(H):
                link(pool.tensor_scalar(promptb[:, h, :], iof[:, 128:384], SLOPES[h], None, ALU.mult))
            select(promptb[:, :, :], [[0, H], [-1, 256]], 128, 1, NEG)
            link(pool.tensor_copy(c128[:], iof[0:32, 0:128]))
            link(pool.memset(slope[:], SLOPES[H - 1]))
            link(pool.memset(back[:], NT * (H - 1.0)))
            for h in range(H - 1, 0, -1):
                select(slope[:], [[0, 1]], -NT * h, 1, SLOPES[h - 1])
                select(back[:], [[0, NPG + 1]], -NT * h, 1, NT * (h - 1.0))
            link(pool.tensor_sub(back[:], iof[0:32, 384:401], back[:]))
            link(pool.tensor_scalar(ownb[:], c128[:, 0:120], 56.0, None, ALU.subtract))
            link(pool.tensor_sub(ownb[:], ownb[:], back[:, NPG:NPG + 1].to_broadcast([32, 120])))
            link(pool.tensor_scalar(iof[0:32, 0:120], ownb[:], 0.0, NEG, ALU.is_gt, ALU.mult))
            link(pool.tensor_mul(ownb[:], ownb[:], slope[:, 0:1].to_broadcast([32, 120])))
            link(pool.tensor_add(ownb[:], ownb[:], iof[0:32, 0:120]))
            select(ownb[:], [[1, 120]], -56, 0, NEG)
            PO.up(pool.tensor_copy(iof[0:1, 0:1], iof[0:1, 1:2]), "consts")

            pool.wait_ge(s["rel_act"], 12 + CREDIT)
            PO.wait(pool, "consts")
            PO.up(pool.tensor_copy(iof[:, 0:324].rearrange("p (c b s) -> p c b s", c=12, s=3),
                                   cin3[:, :, SEQ:SEQ + 99].rearrange("p c (b s) -> p c b s", s=11)[:, :, :, 0:3]), "dnlast")
            AC.wait(pool, "dntail2")
            pool.dma_start(o["dnc_p"][0, 0], dnrows[32:35, :]).then_inc(s["stores"], 16)
            pool.dma_start(o["dnc_s"][0].rearrange("b k c -> (b k) c"), dnrows[35:59, :]).then_inc(s["stores"], 16)

            pool.wait_ge(s["lo_done"], 2 * SLOT_MIX)
            for h in range(H):
                pool.dma_start(s0[:, NB * h:NB * h + NB, :], a["state_dn"][0, :, h].rearrange("b d v -> d b v"))\
                    .then_inc(s["s0_in0"], 16)

            for n, (l, t) in enumerate(INV):
                sz = TILES[t][1]
                if n == 0:
                    DV.wait(pool, "qkn")
                DV.wait(pool, f"L{t}")
                if n >= 2:
                    PE.wait(pool, f"invw{n - 2}")
                    if INV[n - 2][0] == 0:
                        DV.wait(pool, f"inv{n - 2}")
                x = t4(lmb[n % 2][0:sz, 0:H * sz])
                PO.up(pool.tensor_tensor(x, t4(L_[t]), mid(bdiff[0:sz, l, 0:sz], H), ALU.mult), f"lm{n}")

            AC.wait(pool, "decay2")
            PE.wait(pool, "ksT")
            for h in range(H):
                x = s0[:, NB * h:NB * h + NB, :]
                PO.up(pool.tensor_tensor(x, x, last(eglS[:, NB * h:NB * h + NB], HD), ALU.mult), f"s0g{h}")
            DV.wait(pool, "state1")
            pool.dma_start(o["dn_p"][0, 0].rearrange("h d v -> d h v"), t4(spr[:, :])).then_inc(s["stores"], 16)
            for h in range(H):
                DV.wait(pool, f"stS{h}")
                pool.dma_start(o["dn_s"][0, :, h].rearrange("b d v -> d b v"), s0[:, NB * h:NB * h + NB, :])\
                    .then_inc(s["stores"], 16)
            DV.wait(pool, "keyb")
            for kv, (op, os_) in enumerate((("k_p", "k_s"), ("v_p", "v_s"))):
                AC.wait(pool, f"kvtok{3 * kv + 2}")
                pool.dma_start(o[op][0, 0].rearrange("(t p) h d -> p t (h d)", p=P), kvtok[:, kv, 0:2, :]).then_inc(s["stores"], 16)
                pool.dma_start(o[os_][0].rearrange("b t h d -> (b t) (h d)"), kvtok[0:SMP, kv, 2, :]).then_inc(s["stores"], 16)

            with pool.Fori(0, WHOLE) as b:
                for w in range(VUNITS):
                    pool.wait_ge(s["v_hi"], b * VUNITS + (w + 1))
                    pool.tensor_tensor(vl[:, w % 2], vring[:, w // 2 % 2, 2 * (w % 2):2 * (w % 2) + 2, :], vh[:, w % 2],
                                       ALU.subtract).then_inc(s["v_lo"], 1)

            def accumulate(n):
                for m in range(1, KD - 2):
                    DV.wait(pool, f"r{n}_{m}")
                    if m > 1:
                        PO.wait(pool, f"accs{n}_{m - 1}")
                    PO.up(pool.tensor_tensor(lnt[:, 0, :], xres[:, 0, :] if m == 1 else lnt[:, 0, :], xres[:, m, :],
                                             ALU.add), f"accs{n}_{m}")
                    if m == 1:
                        AC.wait(pool, f"sq{n}_0")
                        PO.up(pool.tensor_copy(lnt[:, 1, :], sq[:, 0, :]), f"accq{n}_0")
                    AC.wait(pool, f"sq{n}_{m}")
                    PO.wait(pool, f"accq{n}_{m - 1}")
                    PO.up(pool.tensor_tensor(lnt[:, 1, :], lnt[:, 1, :], sq[:, m % 2, :], ALU.add), f"accq{n}_{m}")

            def normed_lo(n):
                for m in range(KD):
                    AC.wait(pool, f"lnh{n}_{m}")
                    PO.up(pool.tensor_tensor(xl[:, m, :], xres[:, m, :], xh[:, m, :], ALU.subtract), f"x{n}_{m}")

            cb3 = cb[:, :].rearrange("p (c w) -> p c w", w=WF)

            def history(name, src, n):
                pool.dma_start(rows[32:48, 0:P * n], src.rearrange("b k c -> (b k) c")).then_inc(s["hist_in"], 16)
                PO.up(pool.memset(cb3[:, 0:n, 0:2], 0.0), f"{name}_zero")

            def tails(name, n, op, os_):
                if name == "sc":
                    pool.wait_ge(s["sc_prod"], KD + 2)
                else:
                    pool.wait_ge(s["h_done"], KF * (int(name[1]) + 1) + 2)
                PO.up(pool.tensor_copy(last2[:, 0:18 * n].rearrange("p (c b s) -> p c b s", c=n, s=2),
                                       cb3[:, 0:n, SEQ:SEQ + 90].rearrange("p c (b s) -> p c b s", s=10)[:, :, :, 0:2]),
                      f"{name}_last")
                AC.wait(pool, f"{name}_tail{(n - 1) // 4}")
                pool.dma_start(op, rows[0:2, 0:P * n]).then_inc(s["stores"], 16)
                pool.dma_start(os_.rearrange("b k c -> (b k) c"), rows[2:18, 0:P * n]).then_inc(s["stores"], 16)

            DV.wait(pool, "attn_end")
            AC.wait(pool, "attn_endh")
            pool.wait_ge(s["stores"], 16 * 11)
            history("f0", a["state_ffn_conv"][0], KF)
            accumulate(0)
            normed_lo(0)
            tails("f0", KF, o["ffc_p"][0, 0], o["ffc_s"][0])
            PE.wait(pool, "f0_hist")
            history("sc", a["state_sc_conv"][0], KD)
            accumulate(1)
            normed_lo(1)
            pool.wait_ge(s["stores"], 16 * 13)
            tails("sc", KD, o["scc_p"][0, 0], o["scc_s"][0])
            PE.wait(pool, "sc_hist")
            DV.wait(pool, "sc_gated")
            history("f1", a["state_ffn_conv"][1], KF)
            accumulate(2)
            normed_lo(2)
            pool.wait_ge(s["stores"], 16 * 15)
            tails("f1", KF, o["ffc_p"][1, 0], o["ffc_s"][1])
            accumulate(3)
            for t in range(3):
                for half in range(2):
                    AC.wait(pool, f"y{2 * t + half}")
                cols = hraw_y(t)
                if t < 2:
                    pool.dma_start(o["y_p"][0, P * t:P * t + P, :], cols).then_inc(s["stores"], 16)
                else:
                    pool.dma_start(o["y_s"].rearrange("b t d -> (b t) d"), cols).then_inc(s["stores"], 16)
            pool.wait_ge(s["stores"], 16 * (17 + 3))

        @block.scalar
        def _(act):
            def copy(out, in_):
                return act.activation(out, in_, ACT.Copy)

            def split_hi(n, p):
                act.wait_ge(s["raw_in"], 32 * n + 32)
                act.wait_ge(s["chunk_done"], 4 * n + (2 * p - 2 + CREDIT))
                copy(hi[:, p], weight(n)[:, :, 256 * p:256 * p + 256]).then_inc(s["hi_done"], 1)

            def chunk(n, j):
                act.wait_ge(s["chunk_done"], 4 * n + (j + 1 + CREDIT))

            for _ in range(CREDIT):
                act.memzero(spare(0)).then_inc(s["rel_act"], 1)
            for k in range(KD):
                DV.wait(act, f"xres{k}")
                AC.up(copy(xh[:, k, :], xres[:, k, :]), f"xh{k}")
            split_hi(0, 0)
            for i, n in enumerate((PA_N, PB_N, PC_N)):
                PE.wait(act, "parT")
                AC.up(copy(par[:, i, 0:n], bank[4][:, 128 * i:128 * i + n]), f"par{i}")
            PE.wait(act, "histT")
            PO.wait(act, "cin_zero")
            cin3 = cin[:, :].rearrange("p (c w) -> p c w", w=WD)
            AC.up(copy(cin3[:, :, 259:347].rearrange("p c (b s) -> p c b s", s=11)[:, :, :, 0:3],
                       bank[5][:, 0:288].rearrange("p (c b k) -> p c b k", c=12, b=NB)), "hist")

            split_hi(0, 1)

            def mix_slot(n, evacuate):
                for j in (0, 1):
                    chunk(n, j)
                    evacuate(j)
                split_hi(n + 1, 0)
                for j in (2, 3):
                    chunk(n, j)
                    evacuate(j)
                split_hi(n + 1, 1)

            with act.Fori(0, 3) as i:
                def to_rows(j):
                    copy(cin[:, bass.ds((4 * i + j) * WD + 3, SEQ)], bank[j][:, 0:SEQ])
                    copy(cin[:, bass.ds((4 * i + j) * WD + 259, 88)].rearrange("p (b s) -> p b s", s=11)[:, :, 3:11],
                         bank[j][:, SEQ:TOK].rearrange("p (b t) -> p b t", t=NT)).then_inc(s["rel_act"], 1)
                mix_slot(i, to_rows)
            mix_slot(3, lambda j: act.activation(zsb[:, j, :], bank[j][:, 0:TOK], ACT.Silu).then_inc(s["rel_act"], 1))
            act.wait_ge(s["conv_step"], 48)
            for c in range(12):
                ins = act.activation(qkv[:, c * WF:c * WF + LD], qkv[:, c * WF:c * WF + LD], ACT.Silu)
            AC.up(ins, "silu")
            DV.wait(act, "gx")
            act.activation(gates[:, L1, :], gates[:, NX, :], ACT.Exp)
            act.activation(gates[:, EB, :], gates[:, B_, :], ACT.Exp, scale=-1.0)
            AC.up(act.activation(dtal[:, 1, :], dtal[:, 1, :], ACT.Exp), "gexp")

            def to_heads(i):
                return lambda j: copy(mbh[:, 4 * i + j, :], bank[j][:, 0:TOK]).then_inc(s["rel_act"], 1)

            def l2_logs(cs):
                for c in cs:
                    PE.wait(act, f"ss{c}")
                    AC.up(act.activation(l2n[:, c, :], bank[4 + c % 4][:, 0:LD], ACT.Ln, bias=eps6[:, 0:1]), f"ssln{c}")
                AC.wait(act, f"ssln{cs[-1]}")
                AC.up(act.activation(l2n[:, cs[0]:cs[-1] + 1, :], l2n[:, cs[0]:cs[-1] + 1, :], ACT.Exp, scale=-0.5),
                      f"rn{cs[0] // 4}")

            mix_slot(4, to_heads(0))
            for g in range(3):
                PE.wait(act, f"dntail{g}")
                AC.up(copy(dnrows[32:59, 512 * g:512 * g + 512], bank[4 + g][0:27, :]), f"dntail{g}")
            DV.wait(act, "gone")
            AC.up(act.activation(gates[:, L1, :], gates[:, L1, :], ACT.Ln), "gln")
            for j in (0, 1):
                chunk(5, j)
                to_heads(1)(j)
            split_hi(6, 0)
            act.wait_ge(s["stores"], 32)
            AC.wait(act, "silu")
            PO.wait(act, "consts")
            for c in range(8):
                AC.up(act.activation(l2n[:, c, :], qkv[:, c * WF:c * WF + LD], ACT.Square), f"l2sq{c}")
            for j in (2, 3):
                chunk(5, j)
                to_heads(1)(j)
            split_hi(6, 1)
            l2_logs(range(4))
            l2_logs(range(4, 8))
            for j in (0, 1):
                chunk(6, j)
                to_heads(2)(j)
            split_hi(S_OUT, 0)

            for t, (_, n) in enumerate(TILES):
                bk = (4, 0, 4)[t]
                gcb, small = bank[bk + 2], bank[bk + 3]
                PE.wait(act, f"cum{t}")
                DV.wait(act, f"cumsb{t}")
                AC.up(act.activation(gate(EGC, t, n), gate(GC, t, n), ACT.Exp), f"egc{t}")
                act.activation(gate(KD_, t, n), gate(KD_, t, n), ACT.Exp)
                if t < 2:
                    act.activation(gate(EGL, t), gate(GL, t), ACT.Exp)
                else:
                    act.activation(eglS[:, :], small[:, 8:40], ACT.Exp)
                if t:
                    DV.wait(act, f"qg{t - 1}")
                DV.wait(act, f"dmat{t}")
                AC.up(act.activation(t4(vnew[:, 0:H * n]), gcb[:, 0:H * n].rearrange("p (h c) -> p h c", h=H), ACT.Exp),
                      f"egcb{t}")
                act.activation(dsc[0][0:n, 0:H * n], dsc[0][0:n, 0:H * n], ACT.Exp)
                AC.up(act.activation(dsc[1][0:n, 0:H * n], dsc[1][0:n, 0:H * n], ACT.Exp, scale=-1.0), f"decay{t}")
                if t == 0:
                    for j in (2, 3):
                        chunk(6, j)
                        to_heads(2)(j)

            PE.wait(act, "ksT")
            for u in range(2):
                ins = copy(kq[:, 256 * u:256 * u + 256].rearrange("p (a t) -> p a t", t=NT),
                           bank[5][:, :].rearrange("p (a u t) -> p a u t", u=2, t=NT)[:, :, u, :])
            AC.up(ins, "ksTsb")
            for n, (l, t) in enumerate(INV):
                sz = TILES[t][1]
                if l == 0:
                    continue
                PE.wait(act, f"invw{n}")
                AC.up(copy(wsb[t][0:sz, 0:H * sz], bank[(0, 3, 6)[t]][0:sz, 0:H * sz]), f"wsb{n}")

            PE.wait(act, "vn0")
            AC.up(copy(vnew[:, :], bank[0][:, :]), "vnsb0")
            PE.wait(act, "vn2")
            AC.up(copy(vnewS, bank[7][0:SMP, :]), "vnsb2")
            PE.wait(act, "o0")
            AC.up(copy(oT[:, :, 0:128], t4(bank[1][:, :])), "oT0")
            PE.wait(act, "st0")
            PE.wait(act, "vn1")
            AC.up(copy(vnew[:, :], bank[0][:, :]), "vnsb1")
            PE.wait(act, "o1")
            AC.up(copy(oT[:, :, 128:256], t4(bank[1][:, :])), "oT1")

            for h in range(H):
                DV.wait(act, "oT2")
                AC.wait(act, "oT1")
                AC.up(act.activation(qg[:, h, :], oT[:, h, :], ACT.Square), f"osq{h}")
            for h in range(H):
                PE.wait(act, f"oss{h}")
                AC.up(act.activation(qg[:, h, :], bank[h][:, 0:TOK], ACT.Ln, scale=1.0 / HD, bias=eps6[:, 0:1]), f"oln{h}")
            def kv_rows(cs):
                for i in cs:
                    n = TILES[i % 3][1]
                    PE.wait(act, f"kvT{i}")
                    AC.up(copy(kvtok[0:n, i // 3, i % 3, :], bank[4 + i % 3][0:n, :]), f"kvtok{i}")

            def prompt(u):
                if u == 0:
                    AC.wait(act, "oln3")
                    AC.up(act.activation(qg[:, :, :], qg[:, :, :], ACT.Exp, scale=-0.5), "orn")
                if u == 2:
                    DV.wait(act, "mixo")
                    AC.up(copy(xh[:, 0:4, :], oT), "mixh_done")
                if u == 3:
                    kv_rows(range(3))
                if u == 6:
                    kv_rows(range(3, 6))
                if u in (7, 8):
                    for h in range(H):
                        t, i = u - 7, 4 * (u - 7) + h
                        DV.wait(act, f"pmax{t}")
                        x = pl0[:, h, :] if t == 0 else pl1[:, h, :]
                        AC.up(act.activation(x, x, ACT.Exp, bias=pst[:, 0, i:i + 1], accum_out=pst[:, 1, i:i + 1]),
                              f"pexp{i}")
                if u == 12:
                    for g in range(3):
                        PE.wait(act, f"pT{g}")
                        AC.up(copy(pT[:, 512 * g:512 * g + 512], bank[4 + g][:, :]), f"pTsb{g}")
                if u == 15:
                    for t in range(2):
                        PE.wait(act, f"po{t}")
                        AC.up(copy(xh[:, 4:8, 128 * t:128 * t + 128], t4(bank[4 + t][:, :])), f"poh{t}")
                    AC.wait(act, "kvtok5")
                    AC.up(copy(voh[:, :], kvtok[0:SMP, 1, 2, :]), "voh")


            def queries(b, x):
                act.wait_ge(s["q_fp"], b + 1)
                copy(qph[:, x], qpf[:, x]).then_inc(s["q_hi"], 1)

            def attend(b, c, d, n=None, x=0):
                def kT_hi(u):
                    if b is not None:
                        act.wait_ge(s["kT_mm"], b * UNITS + (u + 1))
                        after(act, "s_mm", b * UNITS + (u - 1))
                        copy(kTh[:, u % 2, :], bank[u % 2][:, :]).then_inc(s["kT_hi"], 1)

                def v_hi(x, w):
                    if x is not None and not whole(x):
                        act.wait_ge(s[f"v_in{w // 2 % 2}"], x * 128 + 64 * (w // 4 + 1))
                        after(act, "v_mm", x * VUNITS + (w - 1))
                        copy(vh[:, w % 2], vring[:, w // 2 % 2, 2 * (w % 2):2 * (w % 2) + 2, :]).then_inc(s["v_hi"], 1)

                def exponentials(blocks):
                    for n in blocks:
                        x = slice(BLK * n, min(BLK * n + BLK, PAST + SMP))
                        ins = act.activation(prob[0:32, x], sbias[0:32, x], ACT.Exp, bias=shift[:, n:n + 1],
                                             accum_out=dn[:, n:n + 1])
                    return ins

                for u in range(UNITS):
                    kT_hi(u)
                    if u == 12 and n is not None:
                        queries(n, 1 - x)
                    if c is None and d is None:
                        prompt(u)
                    if u % 2 == 0 and u < 14:
                        v_hi(d, u // 2 + 1)
                    if c is not None:
                        if u == 3:
                            act.wait_ge(s["shifted"], c + 1)
                            exponentials(range(4))
                        if u == 4:
                            exponentials(range(4, NBLK + 1)).then_inc(s["p_exp"], 1)
                    if u == 14:
                        v_hi(c, 0)
                if d is not None:
                    act.wait_ge(s["v_mm"], d * VUNITS + VUNITS)
                    rows_ = 32 if whole(d) else SMP
                    copy(orow[0:rows_, :], bank[4][0:rows_, :]).then_inc(s["o_row"], 1)
                if c is not None:
                    act.wait_ge(s["pT_mm"], c + 1)
                    if whole(c):
                        if d is not None:
                            after(act, "v_mm", d * VUNITS + VUNITS)
                        past, own = pTf[:, 0:NPG, :], pTf[0:SMP, NPG, :]
                    else:
                        past, own = pTs[:, 0:NPG, 0, :], pTs[0:SMP, NPG, 0, :]
                    copy(past, bank[5][:, :].rearrange("p (j r) -> p j r", r=32))
                    copy(own, bank[7][0:SMP, 256:288]).then_inc(s["pT_hi"], 1)

            act.preload_act_table(ACT.Exp)
            queries(0, 0)
            attend(0, None, None, 1)
            attend(1, 0, None, 2, 1)
            with act.Fori(1, NB // 2 - 1) as i:
                attend(2 * i, 2 * i - 1, 2 * i - 2, 2 * i + 1)
                attend(2 * i + 1, 2 * i, 2 * i - 1, 2 * i + 2, 1)
            attend(NB - 2, NB - 3, NB - 4, NB - 1)
            attend(NB - 1, NB - 2, NB - 3, None, 1)
            attend(None, NB - 1, NB - 2)
            split_hi(S_OUT, 1)
            attend(None, None, NB - 1)
            PE.wait(act, "attn_mm")
            AC.up(copy(xh[:, 4:8, SEQ:TOK], bank[6][:, 0:256].rearrange("p (h c) -> p h c", h=H)), "attn_endh")

            def square(n, m):
                DV.wait(act, f"r{n}_{m}")
                if m >= 2:
                    PO.wait(act, f"accq{n}_{m - 2}")
                AC.up(act.activation(sq[:, m % 2, :], xres[:, m, :], ACT.Square), f"sq{n}_{m}")

            def norm(n, gpack, grow, bpack, brow):
                act.preload_act_table(ACT.Ln)
                DV.wait(act, f"mean{n}")
                AC.up(act.activation(lnt[:, 2, :], lnt[:, 4, :], ACT.Square), f"msq{n}")
                DV.wait(act, f"var{n}")
                AC.up(act.activation(lnt[:, 3, :], lnt[:, 3, :], ACT.Ln), f"lnv{n}")
                AC.wait(act, f"lnv{n}")
                AC.up(act.activation(lnt[:, 3, :], lnt[:, 3, :], ACT.Exp, scale=-0.5), f"rstd{n}")
                for m in range(KD):
                    DV.wait(act, f"t2_{n}_{m}")
                    AC.up(act.activation(xres[:, m, :], hraw[:, m % 2, :], ACT.Identity, scale=vec(gpack, grow + m),
                                         bias=vec(bpack, brow + m)), f"ln{n}_{m}")
                    if n < 3:
                        AC.wait(act, f"ln{n}_{m}")
                        AC.up(copy(xh[:, m, :], xres[:, m, :]), f"lnh{n}_{m}")

            cb3 = cb[:, :].rearrange("p (c w) -> p c w", w=WF)

            def history(name, n):
                PE.wait(act, f"{name}_hist")
                PO.wait(act, f"{name}_zero")
                AC.up(copy(cb3[:, 0:n, 258:338].rearrange("p c (b s) -> p c b s", s=10)[:, :, :, 0:2],
                           bank[6][:, 0:16 * n].rearrange("p (c b k) -> p c b k", c=n, b=NB)), f"{name}_hist")

            def tails(name, n, groups):
                for g in groups:
                    w = min(512, P * n - 512 * g)
                    PE.wait(act, f"{name}_tail{g}")
                    AC.up(copy(rows[0:18, 512 * g:512 * g + w], bank[TAIL_BANK[g % 3]][0:18, 0:w]), f"{name}_tail{g}")

            def feed_forward(layer):
                base = S_UP[layer]
                act.preload_act_table(ACT.Gelu)
                with act.Fori(0, SLOT_FFN) as i:
                    for j in (0, 1):
                        chunk(i + base, j)
                        copy(cb[:, bass.ds((2 * i + j) * WF + 2, SEQ)], bank[j][:, 0:SEQ])
                        copy(cb[:, bass.ds((2 * i + j) * WF + 258, 80)].rearrange("p (b s) -> p b s", s=10)[:, :, 2:10],
                             bank[j][:, SEQ:TOK].rearrange("p (b t) -> p b t", t=NT)).then_inc(s["rel_act"], 1)
                    split_hi(i + (base + 1), 0)
                    for j in (0, 1):
                        act.wait_ge(s["conv_step"], 6 * i + (CONV[layer] + 5 + j))
                        act.activation(acc[:, WF * j:WF * j + LF], acc[:, WF * j:WF * j + LF], ACT.Gelu)\
                            .then_inc(s["gelu_done"], 1)
                    for j in (0, 1):
                        act.wait_ge(s["h_done"], 2 * i + (KF * layer + j + 3))
                        copy(hh[:, bass.ds(2 * i + j, 1), :], hraw[:, j:j + 1, :]).then_inc(s["hh_done"], 1)
                    split_hi(i + (base + 1), 1)

            def down(layer, n):
                for i in range(2):
                    for k in range(3):
                        slot = S_DOWN[layer] + 3 * i + k
                        if i == 0 and k:
                            tails(f"f{layer}", KF, range(3 * k - 3, 3 * k))
                        if k == 2:
                            square(n, 4 * i)
                            square(n, 4 * i + 1)
                        if slot + 1 < S_END:
                            split_hi(slot + 1, 0)
                        if k == 2:
                            square(n, 4 * i + 2)
                            square(n, 4 * i + 3)
                        if slot + 1 < S_END:
                            split_hi(slot + 1, 1)

            def out_proj(base, n):
                for i in range(SLOT_OUT):
                    square(n, 4 * i)
                    square(n, 4 * i + 1)
                    split_hi(base + i + 1, 0)
                    square(n, 4 * i + 2)
                    square(n, 4 * i + 3)
                    split_hi(base + i + 1, 1)

            act.wait_ge(s["stores"], 16 * 11)
            out_proj(S_OUT, 0)
            norm(0, 0, PA_LMG, 0, PA_LMB)
            history("f0", KF)
            feed_forward(0)
            down(0, 1)
            norm(1, 1, PB_LFG, 1, PB_LFB)
            history("sc", KD)
            with act.Fori(0, 4) as i:
                n = i + S_SC
                for j in (0, 1):
                    chunk(n, j)
                    act.wait_ge(s["sc_prod"], 2 * i + (j + 1))
                    copy(hraw[:, j, :], bank[j][:, 0:TOK]).then_inc(s["rel_act"], 1)
                split_hi(i + (S_SC + 1), 0)
                split_hi(i + (S_SC + 1), 1)
            for n in range(S_SC + 4, S_SC + 6):
                split_hi(n + 1, 0)
                for j in range(4):
                    DV.wait(act, f"scp{4 * (n - S_SC - 4) + j}")
                    AC.up(copy(hh[:, 4 * (n - S_SC - 4) + j, :], hraw[:, j % 2, :]), f"sch{4 * (n - S_SC - 4) + j}")
                split_hi(n + 1, 1)
            tails("sc", KD, range(2))
            out_proj(S_SCO, 2)
            norm(2, 0, PA_LMG + KD, 0, PA_LMB + KD)
            history("f1", KF)
            feed_forward(1)
            down(1, 3)
            norm(3, 1, PB_LFG + KD, 1, PB_LFB + KD)
            for i in range(6):
                n = TILES[i // 2][1]
                PE.wait(act, f"yT{i}")
                AC.up(copy(hraw_y(i // 2)[:, 512 * (i % 2):512 * (i % 2) + 512], bank[i][0:n, :]), f"y{i}")

        @block.vector
        def _(dve):
            def split_lo(n, p):
                dve.wait_ge(s["hi_done"], 2 * n + (p + 1))
                dve.tensor_tensor(lo[:, p], weight(n)[:, :, 256 * p:256 * p + 256], hi[:, p], ALU.subtract)\
                   .then_inc(s["lo_done"], 1)

            def chunk(n, j):
                dve.wait_ge(s["chunk_done"], 4 * n + (j + 1 + CREDIT))

            def tt(out, a_, b_, op):
                return dve.tensor_tensor(out, a_, b_, op)

            dve.memset(spare(1), 0.0).then_inc(s["h_done"], 1)
            dve.memset(spare(1), 0.0).then_inc(s["h_done"], 1)
            dve.memset(spare(1), 0.0).then_inc(s["sc_prod"], 1)
            dve.memset(spare(1), 0.0).then_inc(s["sc_prod"], 1)
            DV.up(dve.memset(gates[:, :, :], 0.0), "gz")
            dve.wait_ge(s["pt_in"], 16)
            two = ptab[:, :].rearrange("o (a u) -> o a u", u=2)
            DV.up(dve.scalar_tensor_tensor(out=pair[:, :], in0=two[:, :, 1], scalar=float(POOL), in1=two[:, :, 0],
                                           op0=ALU.mult, op1=ALU.add), "pages")
            for k in range(KD):
                PE.wait(dve, f"xT{k}")
                DV.up(dve.tensor_copy(xres[:, k, :], bank[k % 4][:, 0:TOK]), f"xres{k}")
            for k in range(KD):
                AC.wait(dve, f"xh{k}")
                DV.up(tt(xl[:, k, :], xres[:, k, :], xh[:, k, :], ALU.subtract), f"xl{k}")
            split_lo(0, 0)
            split_lo(0, 1)
            AC.wait(dve, "par2")
            AC.wait(dve, "hist")
            with dve.Fori(0, 3) as i:
                for q in range(2):
                    if q == 1:
                        split_lo(i + 1, 0)
                        split_lo(i + 1, 1)
                    for r in range(4):
                        for jj in range(2):
                            c = 4 * i + (2 * q + jj)
                            if r == 0:
                                dve.wait_ge(s["rel_act"], 4 * i + (2 * q + jj + 5))
                            else:
                                dve.wait_ge(s["conv_step"], 16 * i + (8 * q + 2 * (r - 1) + jj + 1))
                            x = cin[:, bass.ds(c * WD + r, LD)]
                            y = qkv[:, bass.ds(c * WF, LD)]
                            w = par2[:, bass.ds(c + (PA_DN + 12 * r), 1)]
                            if r == 0:
                                ins = dve.tensor_scalar(y, x, w, None, ALU.mult)
                            else:
                                ins = dve.scalar_tensor_tensor(out=y, in0=x, scalar=w, in1=y, op0=ALU.mult, op1=ALU.add)
                            ins.then_inc(s["conv_step"], 1)
            dve.wait_ge(s["wba_in"], 48)
            PE.wait(dve, "ba")
            DV.wait(dve, "gz")
            for i, at in ((B_, 0), (X_, 4)):
                dve.tensor_copy(gates[:, i, 0:8].rearrange("p (t h) -> p t h", h=H),
                                bank[7][:, 0:16].rearrange("p (t h) -> p t h", h=8)[:, :, at:at + 4])
                ins = dve.tensor_copy(gates[0:SMP, i, 8:12], bank[7][0:SMP, 16 + at:20 + at])
            DV.up(ins, "ba")
            DV.wait(dve, "ba")
            dt3 = dtal[:, 0:1, :].to_broadcast([P, 3, H])
            g3 = [gates[:, i, :].rearrange("p (t h) -> p t h", h=H) for i in range(13)]
            DV.up(tt(g3[X_], g3[X_], dt3, ALU.add), "gxa")
            DV.wait(dve, "gxa")
            DV.up(dve.scalar_tensor_tensor(out=gates[:, NX, :], in0=gates[:, X_, :], scalar=-1.0, in1=gates[:, X_, :],
                                           op0=ALU.mult, op1=ALU.min), "gx")
            split_lo(4, 0)
            split_lo(4, 1)
            AC.wait(dve, "gexp")
            dve.tensor_scalar(gates[:, L1, :], gates[:, L1, :], 1.0, None, ALU.add)
            DV.up(dve.tensor_scalar(gates[:, EB, :], gates[:, EB, :], 1.0, None, ALU.add), "gone")
            DV.wait(dve, "gone")
            DV.up(dve.reciprocal(gates[:, BETA, :], gates[:, EB, :]), "beta")
            split_lo(5, 0)
            split_lo(5, 1)
            AC.wait(dve, "gln")
            DV.up(dve.scalar_tensor_tensor(out=gates[:, X_, :], in0=gates[:, X_, :], scalar=0.0, in1=gates[:, L1, :],
                                           op0=ALU.max, op1=ALU.add), "gsp")
            DV.wait(dve, "gsp")
            DV.up(dve.scalar_tensor_tensor(out=g3[G_], in0=g3[X_], scalar=-1.0, in1=dtal[:, 1:2, :].to_broadcast([P, 3, H]),
                                           op0=ALU.mult, op1=ALU.mult), "g")
            split_lo(6, 0)
            split_lo(6, 1)
            DV.wait(dve, "g")
            PO.wait(dve, "consts")

            def cumulate(t):
                n = TILES[t][1]
                DV.up(tt(t4(spr[0:n, 0:H * n]), mid(tri(t)[0], H), last(gate(G_, t, n), n), ALU.mult), f"ug{t}")

            dve.wait_ge(s["stores"], 32)
            cumulate(0)

            for c in range(8):
                AC.wait(dve, f"rn{c // 4}")
                x = qkv[:, c * WF:c * WF + LD]
                ins = dve.scalar_tensor_tensor(out=x, in0=x, scalar=SCALE if c < 4 else 1.0, in1=l2n[:, c, :],
                                               op0=ALU.mult, op1=ALU.mult)
            DV.up(ins, "qknorm")
            DV.wait(dve, "qknorm")
            DV.up(dve.tensor_copy(smp.rearrange("p c (b s) -> p c b s", s=NT),
                                  qk3[:, :, 259:347].rearrange("p c (b s) -> p c b s", s=11)[:, :, :, 0:NT]), "qkn")

            for t, (_, n) in enumerate(TILES):
                bk = (4, 0, 4)[t]
                kkb, qkb, gcb, small = bank[bk], bank[bk + 1], bank[bk + 2], bank[bk + 3]
                up_, lo_ = tri(t)
                PE.wait(dve, f"cum{t}")
                dve.tensor_copy(gate(GC, t, n), small[0:n, 0:4])
                DV.up(dve.tensor_copy(gate(GL, t, n), small[0:n, 4:8]), f"gcl{t}")
                DV.wait(dve, f"gcl{t}")
                tt(t4(dsc[0][0:n, 0:H * n]), t4(gcb[0:n, 0:H * n]), last(gate(GC, t, n), n), ALU.subtract)
                DV.up(tt(gate(KD_, t, n), gate(GL, t, n), gate(GC, t, n), ALU.subtract), f"cumsb{t}")
                DV.wait(dve, f"cumsb{t}")
                DV.up(dve.tensor_scalar(dsc[1][0:n, 0:H * n], dsc[0][0:n, 0:H * n], 0.0, None, ALU.max), f"dmax{t}")
                DV.up(dve.tensor_scalar(dsc[0][0:n, 0:H * n], dsc[0][0:n, 0:H * n], 0.0, None, ALU.min), f"dmat{t}")
                if t == 1:
                    m = TILES[2][1]
                    tt(rtmp[0:m, 0:32].rearrange("p (h b) -> p h b", h=H), last(gate(G_, 2, m), NB), mid(member, H), ALU.mult)
                if t < 2:
                    cumulate(t + 1)
                AC.wait(dve, f"egc{t}")
                dve.scalar_tensor_tensor(out=gate(NBE, t, n), in0=gate(BETA, t, n), scalar=-1.0, in1=gate(EGC, t, n),
                                         op0=ALU.mult, op1=ALU.mult)
                AC.wait(dve, f"decay{t}")
                tt(t4(dsc[0][0:n, 0:H * n]), t4(dsc[0][0:n, 0:H * n]), mid(up_, H), ALU.mult)
                DV.up(tt(t4(dsc[1][0:n, 0:H * n]), t4(dsc[1][0:n, 0:H * n]), mid(lo_, H), ALU.mult), f"mask{t}")
                DV.wait(dve, f"mask{t}")
                PE.wait(dve, f"kk{t}")
                DV.up(tt(L_[t], kkb[0:n, 0:H * n], dsc[1][0:n, 0:H * n], ALU.mult), f"La{t}")
                DV.up(tt(IN[t], qkb[0:n, 0:H * n], dsc[0][0:n, 0:H * n], ALU.mult), f"intra{t}")
                DV.wait(dve, f"La{t}")
                DV.up(tt(t4(L_[t]), t4(L_[t]), last(gate(BETA, t, n), n), ALU.mult), f"L{t}")
                PE.wait(dve, f"tok{t}")
                tt(t4(ktok[0:n, t, :]), t4(kkb[0:n, :]), last(gate(KD_, t, n), HD), ALU.mult)
                DV.up(tt(t4(vtok[0:n, t, :]), t4(qkb[0:n, :]), last(gate(BETA, t, n), HD), ALU.mult), f"tok{t}")
                AC.wait(dve, f"egcb{t}")
                if t < 2:
                    DV.up(tt(qg[:, :, 128 * t:128 * t + 128], qk3[:, 0:4, 128 * t:128 * t + 128], t4(vnew[:, :]), ALU.mult), f"qg{t}")
                else:
                    kq5 = kq.rearrange("p (h b u t) -> p h b u t", h=H, b=NB, u=2)
                    for h in range(H):
                        dve.tensor_copy(kq5[:, h, :, 0, :], head(4 + h, 2).rearrange("p (b t) -> p b t", t=NT))
                        ins = tt(kq5[:, h, :, 1, :], head(h, 2).rearrange("p (b t) -> p b t", t=NT), vnew[:, 64 * h:64 * h + 64].rearrange("p (b t) -> p b t", t=NT),
                                 ALU.mult)
                    DV.up(ins, "qg2")

            for n, (l, t) in enumerate(INV):
                sz = TILES[t][1]
                w, u, v = ((0, 1, 2), (3, 4, 5), (6, 7, 7))[t]
                if l == 0:
                    PE.wait(dve, f"invw{n}")
                    PO.wait(dve, f"lm{n}")
                    tt(t4(TT[t]), mid(ident[0:sz, 0:sz], H), t4(bank[w][0:sz, 0:H * sz]), ALU.subtract)
                    DV.up(tt(t4(T_[t]), mid(ident[0:sz, 0:sz], H), t4(lmb[n % 2][0:sz, 0:H * sz]), ALU.subtract), f"inv{n}")
                else:
                    PE.wait(dve, f"invu{n}")
                    off = 256 if t == 2 else 0
                    tt(T_[t], T_[t], bank[u][0:sz, 0:H * sz], ALU.subtract)
                    DV.up(tt(TT[t], TT[t], bank[v][0:sz, off:off + H * sz], ALU.subtract), f"inv{n}")
                if (l, t) == (0, 2):
                    PE.wait(dve, "ks2")
                    DV.up(tt(t4(rhsS), t4(bank[5][0:SMP, :]), last(gate(NBE, 2, SMP), HD), ALU.mult), "rhsa2")
                    DV.wait(dve, "rhsa2")
                    DV.up(tt(rhsS, rhsS, vtok[0:SMP, 2, :], ALU.add), "rhs2")

            AC.wait(dve, "vnsb2")

            def apart(h):
                if h >= 2:
                    PE.wait(dve, f"stS{h - 2}")
                DV.up(tt(vnm[h % 2].rearrange("p (b v) -> p b v", v=HD), mid(vnewS[:, 128 * h:128 * h + 128], NB),
                         last(member, HD), ALU.mult), f"vnm{h}")

            def add_state(h):
                PO.wait(dve, f"s0g{h}")
                PE.wait(dve, f"stS{h}")
                y = s0[:, NB * h:NB * h + NB, :].rearrange("p b v -> p (b v)")
                bk = 4 if h % 2 else 6
                tt(y[:, 0:512], y[:, 0:512], bank[bk][:, :], ALU.add)
                DV.up(tt(y[:, 512:1024], y[:, 512:1024], bank[bk + 1][:, :], ALU.add), f"stS{h}")

            apart(0)
            PE.wait(dve, "st0")
            DV.up(dve.tensor_copy(spr[:, :], bank[2][:, :]), "state0")
            PE.wait(dve, "ks1")
            DV.up(tt(t4(rtmp[:, :]), t4(bank[3][:, :]), last(gate(NBE, 1), HD), ALU.mult), "rhsa1")
            DV.wait(dve, "rhsa1")
            DV.up(tt(rtmp[:, :], rtmp[:, :], vtok[:, 1, :], ALU.add), "rhs1")
            apart(1)
            PE.wait(dve, "o2")
            qs = kq[:, 256:512].rearrange("p (h b t) -> p h b t", h=H, t=NT)
            DV.up(tt(oT[:, :, SEQ:TOK].rearrange("p h (b t) -> p h b t", t=NT),
                     bank[5][:, 0:256].rearrange("p (h b t) -> p h b t", h=H, t=NT), qs, ALU.add), "oT2")
            add_state(0)
            apart(2)
            PE.wait(dve, "st1")
            DV.up(tt(t4(spr[:, :]), t4(spr[:, :]), last(gate(EGL, 1), HD), ALU.mult), "statea")
            DV.wait(dve, "statea")
            DV.up(tt(spr[:, :], spr[:, :], bank[2][:, :], ALU.add), "state1")
            add_state(1)
            apart(3)
            add_state(2)
            add_state(3)


            def prompt(u):
                if u == 0:
                    AC.wait(dve, "orn")
                    DV.up(tt(oT, oT, qg[:, :, :], ALU.mult), "on1")
                if u == 1:
                    DV.wait(dve, "on1")
                    DV.up(dve.scalar_tensor_tensor(out=oT, in0=oT, scalar=vec(0, PA_NW), in1=zsb[:, :, :], op0=ALU.mult,
                                                   op1=ALU.mult), "mixo")
                if u == 3:
                    AC.wait(dve, "mixh_done")
                    DV.up(tt(xl[:, 0:4, :], oT, xh[:, 0:4, :], ALU.subtract), "mixl_done")
                if u == 4:
                    PE.wait(dve, "ps0")
                    DV.up(dve.scalar_tensor_tensor(out=pl0, in0=t4(bank[4][:, :]), scalar=SCALE, in1=promptb[:, :, 128:256],
                                                   op0=ALU.mult, op1=ALU.add), "plog0")
                if u == 5:
                    PE.wait(dve, "ps1")
                    for q in range(2):
                        ins = dve.scalar_tensor_tensor(out=pl1[:, 2 * q:2 * q + 2, :],
                                                       in0=bank[5 + q][:, :].rearrange("p (h c) -> p h c", h=2), scalar=SCALE,
                                                       in1=promptb[:, 2 * q:2 * q + 2, :], op0=ALU.mult, op1=ALU.add)
                    DV.up(ins, "plog1")
                if u in (4, 5):
                    t, x = u - 4, (pl0, pl1)[u - 4]
                    DV.wait(dve, f"plog{t}")
                    DV.up(dve.tensor_reduce(pst[:, 2, 4 * t:4 * t + 4], x, AX.X, ALU.max), f"pmaxa{t}")
                    DV.wait(dve, f"pmaxa{t}")
                    DV.up(dve.tensor_scalar(pst[:, 0, 4 * t:4 * t + 4], pst[:, 2, 4 * t:4 * t + 4], -1.0, None, ALU.mult),
                          f"pmax{t}")
                if u in (9, 10):
                    t, x = u - 9, (pl0, pl1)[u - 9]
                    AC.wait(dve, f"pexp{4 * t + 3}")
                    DV.up(dve.reciprocal(pst[:, 2, 4 * t:4 * t + 4], pst[:, 1, 4 * t:4 * t + 4]), f"prec{t}")
                    DV.wait(dve, f"prec{t}")
                    DV.up(tt(x, x, last(pst[:, 2, 4 * t:4 * t + 4], 128 + 128 * t), ALU.mult), f"pnorm{t}")
                if u == 2:
                    dve.wait_ge(s["stores"], 16 * 7)
                    for g in range(NPG):
                        ins = dve.tensor_scalar(keyb[:, PAGE * g:PAGE * g + PAGE], c128[:, :], back[:, g:g + 1],
                                                slope[:, 0:1], ALU.subtract, ALU.mult)
                    DV.up(ins, "keyb")
                if u == 15:
                    for t in range(2):
                        AC.wait(dve, f"poh{t}")
                        DV.up(tt(xl[:, 4:8, 128 * t:128 * t + 128], t4(bank[4 + t][:, :]),
                                 xh[:, 4:8, 128 * t:128 * t + 128], ALU.subtract), f"pol{t}")
                    AC.wait(dve, "voh")
                    DV.up(tt(vol[:, :], kvtok[0:SMP, 1, 2, :], voh[:, :], ALU.subtract), "vol")

            dve.tensor_copy(twice[:, :], ident[0:SMP, 0:32])
            dve.memset(pen[:, NBLK:NBLK + 1], 0.0)
            DV.up(dve.memset(qpf[:, :, :, :], 0.0), "rowc0")
            DV.wait(dve, "rowc0")
            DV.up(tt(twice[:, :], twice[:, :], ident[0:SMP, 32:SMP], ALU.add), "rowc")
            DV.wait(dve, "rowc")
            ROW = 9

            def queries(b, x):
                for h in range(H):
                    ins = dve.tensor_copy(qpf[:, x, h, NT * h:NT * h + NT], mb[:, bass.ds(b * NT + (TOK * h + SEQ), NT)])
                ins.then_inc(s["q_fp"], 1)

            def queries_lo(b, x):
                dve.wait_ge(s["q_hi"], b + 1)
                tt(qpl[:, x], qpf[:, x], qph[:, x], ALU.subtract).then_inc(s["q_lo"], 1)

            def attend(b, c, n=None, x=0):
                made = [0]

                def link(ins):
                    made[0] += 1
                    ins.then_inc(s["row"], 1)
                    dve.wait_ge(s["row"], c * ROW + made[0])

                def kT_lo(u):
                    if b is not None:
                        dve.wait_ge(s["kT_hi"], b * UNITS + (u + 1))
                        tt(kTl[:, u % 2, :], bank[u % 2][:, :], kTh[:, u % 2, :], ALU.subtract).then_inc(s["kT_lo"], 1)

                def own_bias():
                    dve.scalar_tensor_tensor(out=sbias[0:32, PAST:], in0=bank[7][0:32, 0:SMP], scalar=SCALE,
                                             in1=ownb[:, bass.ds(b * -NT + (SMP - NT), SMP)], op0=ALU.mult, op1=ALU.add)\
                       .then_inc(s["s_bias"], 1)

                def bias(g):
                    dve.wait_ge(s["s_mm"], b * UNITS + (4 * g + 4))
                    dve.scalar_tensor_tensor(out=sbias[0:32, 512 * g:512 * g + 512], in0=bank[2 + g % 2][0:32, :], scalar=SCALE,
                                             in1=keyb[:, 512 * g:512 * g + 512], op0=ALU.mult, op1=ALU.add)\
                       .then_inc(s["s_bias"], 1)

                def sums(g):
                    dve.tensor_reduce(gsum[:, 2 * g:2 * g + 2], bank[2 + g % 2][0:32, :].rearrange("p (n k) -> p n k", n=2),
                                      AX.X, ALU.add).then_inc(s["s_row"], 1)

                def maxima(x, g):
                    dve.wait_ge(s["s_bias"], x * 5 + (g + 2))
                    dve.tensor_reduce(bmax[:, 2 * g:2 * g + 2],
                                      sbias[0:32, 512 * g:512 * g + 512].rearrange("p (n k) -> p n k", n=2), AX.X, ALU.max)\
                       .then_inc(s["s_max"], 1)

                def ranks():
                    A, B = [rk[:, i, :].rearrange("p (n m) -> p n m", m=NBLK) for i in range(2)]
                    gm, gn = mid(gsum[:, :], NBLK), last(gsum[:, :], NBLK)
                    dve.wait_ge(s["s_row"], c * 4 + 4)
                    dve.wait_ge(s["s_max"], c * 4 + 4)
                    tt(A, gm, gn, ALU.is_gt)
                    link(tt(B, gm, gn, ALU.is_equal))
                    link(tt(B, B, ltri[:, :, :], ALU.mult))
                    link(tt(A, A, B, ALU.add))

                def shifts():
                    A = rk[:, 0, :].rearrange("p (n m) -> p n m", m=NBLK)
                    link(dve.tensor_reduce(rank[:, :], A, AX.X, ALU.add))
                    link(dve.tensor_scalar(pen[:, 0:NBLK], rank[:, :], TOPK - 0.5, NEG, ALU.is_gt, ALU.mult))
                    link(tt(bmax[:, :], bmax[:, :], pen[:, :], ALU.add))
                    link(dve.tensor_reduce(r1[:, 0:1], bmax[:, :], AX.X, ALU.max))
                    tt(shift[:, :], pen[:, :], r1[:, 0:1].to_broadcast([32, NBLK + 1]), ALU.subtract).then_inc(s["shifted"], 1)

                def normalise():
                    dve.wait_ge(s["p_exp"], c + 1)
                    link(dve.tensor_reduce(r1[:, 1:2], dn[:, :], AX.X, ALU.add))
                    link(dve.reciprocal(r1[:, 2:3], r1[:, 1:2]))
                    dve.tensor_scalar(prob[0:32, :], prob[0:32, :], r1[:, 2:3], None, ALU.mult).then_inc(s["p_norm"], 1)

                if c is not None:
                    sums(3)
                kT_lo(0)
                if c is not None:
                    maxima(c, 3)
                kT_lo(1)
                if c is not None:
                    ranks()
                else:
                    prompt(0)
                    prompt(1)
                for u in range(2, UNITS):
                    kT_lo(u)
                    if u == 2 and c is not None:
                        shifts()
                    if c is None:
                        prompt(u)
                    if u == 12 and n is not None:
                        queries(n, 1 - x)
                    if u == 14 and n is not None:
                        queries_lo(n, 1 - x)
                    g, at = divmod(u - 5, 4)
                    if b is not None and g >= 0:
                        if u == 5:
                            after(dve, "p_exp", b)
                            own_bias()
                        if at == 0:
                            bias(g)
                        if at == 1:
                            sums(g)
                        if at == 2:
                            maxima(b, g)
                        if u == 12:
                            dve.tensor_reduce(bmax[:, NBLK:NBLK + 1], sbias[0:32, PAST:], AX.X, ALU.max)
                    if u == 8 and c is not None:
                        normalise()
                if c is not None and not whole(c):
                    dve.wait_ge(s["pT_hi"], c + 1)
                    tt(pTs[:, 0:NPG, 1, :], bank[5][:, :].rearrange("p (j r) -> p j r", r=32), pTs[:, 0:NPG, 0, :],
                       ALU.subtract)
                    tt(pTs[0:SMP, NPG, 1, :], bank[7][0:SMP, 256:288], pTs[0:SMP, NPG, 0, :], ALU.subtract)\
                        .then_inc(s["pT_lo"], 1)
                if b is not None:
                    bias(3)

            queries(0, 0)
            queries_lo(0, 0)
            attend(0, None, 1)
            attend(1, 0, 2, 1)
            with dve.Fori(1, NB // 2 - 1) as i:
                attend(2 * i, 2 * i - 1, 2 * i + 1)
                attend(2 * i + 1, 2 * i, 2 * i + 2, 1)
            attend(NB - 2, NB - 3, NB - 1)
            attend(NB - 1, NB - 2, None, 1)
            attend(None, NB - 1)
            split_lo(S_OUT, 0)
            split_lo(S_OUT, 1)
            AC.wait(dve, "attn_endh")
            DV.up(tt(xl[:, 4:8, SEQ:TOK], bank[6][:, 0:256].rearrange("p (h c) -> p h c", h=H), xh[:, 4:8, SEQ:TOK],
                     ALU.subtract), "attn_end")

            def residual(n, m, slot):
                chunk(slot, m % 4)
                DV.up(dve.scalar_tensor_tensor(out=xres[:, m, :], in0=xres[:, m, :], scalar=ALPHA, in1=bank[m % 4][:, 0:TOK],
                                               op0=ALU.mult, op1=ALU.add), f"r{n}_{m}")

            def norm(n, following):
                PE.wait(dve, f"mean{n}")
                DV.up(dve.tensor_copy(lnt[:, 4, :], bank[4][:, 0:TOK]), f"mean{n}")
                AC.wait(dve, f"msq{n}")
                PE.wait(dve, f"stat{n}")
                DV.up(tt(lnt[:, 3, :], bank[5][:, 0:TOK], lnt[:, 2, :], ALU.subtract), f"vara{n}")
                DV.wait(dve, f"vara{n}")
                DV.up(dve.tensor_scalar(lnt[:, 3, :], lnt[:, 3, :], 0.0, LN_EPS, ALU.max, ALU.add), f"var{n}")
                for m in range(KD):
                    ins = tt(xres[:, m, :], xres[:, m, :], lnt[:, 4, :], ALU.subtract)
                DV.up(ins, f"centred{n}")
                DV.wait(dve, f"centred{n}")
                AC.wait(dve, f"rstd{n}")
                for m in range(KD):
                    if m >= 2:
                        AC.wait(dve, f"ln{n}_{m - 2}")
                    DV.up(tt(hraw[:, m % 2, :], xres[:, m, :], lnt[:, 3, :], ALU.mult), f"t2_{n}_{m}")
                if following < S_END:
                    split_lo(following, 1)

            def out_proj(base, n):
                for i in range(SLOT_OUT):
                    residual(n, 4 * i, base + i)
                    residual(n, 4 * i + 1, base + i)
                    split_lo(base + i + 1, 0)
                    residual(n, 4 * i + 2, base + i)
                    residual(n, 4 * i + 3, base + i)
                    if i < SLOT_OUT - 1:
                        split_lo(base + i + 1, 1)

            def down(layer, n):
                for i in range(2):
                    for k in range(3):
                        slot = S_DOWN[layer] + 3 * i + k
                        if k == 2:
                            residual(n, 4 * i, slot)
                            residual(n, 4 * i + 1, slot)
                        if slot + 1 < S_END:
                            split_lo(slot + 1, 0)
                        if k == 2:
                            residual(n, 4 * i + 2, slot)
                            residual(n, 4 * i + 3, slot)
                        if (i, k) != (1, 2):
                            split_lo(slot + 1, 1)

            def convolve(c, w0, nch, y, i, jj, r, base):
                if r:
                    dve.wait_ge(s["conv_step"], 6 * i + (base + 2 * (r - 1) + jj + 1))
                x = cb[:, bass.ds(c * WF + r, LF)]
                w = par2[:, bass.ds(c + (w0 + nch * r), 1)]
                if r == 0:
                    ins = dve.tensor_scalar(y, x, w, None, ALU.mult)
                else:
                    ins = dve.scalar_tensor_tensor(out=y, in0=x, scalar=w, in1=y, op0=ALU.mult, op1=ALU.add)
                ins.then_inc(s["conv_step"], 1)

            def padded(x):
                return x.rearrange("p (b s) -> p b s", s=10)[:, :, 0:NT]

            def feed_forward(layer):
                base = S_UP[layer]
                w0 = P + PB_F if layer == 0 else 2 * P
                with dve.Fori(0, SLOT_FFN) as i:
                    for r in range(3):
                        for j in (0, 1):
                            if r == 0:
                                dve.wait_ge(s["rel_act"], 2 * i + (REL[layer] + j + 1))
                            convolve(2 * i + j, w0, KF, acc[:, WF * j:WF * j + LF], i, j, r, CONV[layer])
                    split_lo(i + (base + 1), 0)
                    for j in (0, 1):
                        dve.wait_ge(s["gelu_done"], 2 * i + (KF * layer + j + 1))
                        chunk(i + base, 2 + j)
                        tt(hraw[:, j, 0:SEQ], acc[:, WF * j:WF * j + SEQ], bank[2 + j][:, 0:SEQ], ALU.mult)
                        tt(hraw[:, j, SEQ:TOK].rearrange("p (b t) -> p b t", t=NT), padded(acc[:, WF * j + 258:WF * j + 338]),
                           bank[2 + j][:, SEQ:TOK].rearrange("p (b t) -> p b t", t=NT), ALU.mult).then_inc(s["h_done"], 1)
                    for j in (0, 1):
                        dve.wait_ge(s["hh_done"], 2 * i + (KF * layer + j + 1))
                        tt(hl[:, bass.ds(2 * i + j, 1), :], hraw[:, j:j + 1, :], hh[:, bass.ds(2 * i + j, 1), :], ALU.subtract)\
                            .then_inc(s["hid_ready"], 1)
                    split_lo(i + (base + 1), 1)

            out_proj(S_OUT, 0)
            norm(0, S_UP[0])
            AC.wait(dve, "f0_hist")
            feed_forward(0)
            down(0, 1)
            norm(1, S_SC)
            AC.wait(dve, "sc_hist")
            with dve.Fori(0, 4) as i:
                split_lo(i + (S_SC + 1), 0)
                for j in (0, 1):
                    dve.wait_ge(s["rel_act"], 2 * i + (REL_SC + j + 1))
                    chunk(i + S_SC, 2 + j)
                    tt(cb[:, bass.ds((2 * i + j) * WF + 2, SEQ)], hraw[:, j, 0:SEQ], bank[2 + j][:, 0:SEQ], ALU.mult)
                    tt(cb[:, bass.ds((2 * i + j) * WF + 258, 80)].rearrange("p (b s) -> p b s", s=10)[:, :, 2:10],
                       hraw[:, j, SEQ:TOK].rearrange("p (b t) -> p b t", t=NT),
                       bank[2 + j][:, SEQ:TOK].rearrange("p (b t) -> p b t", t=NT), ALU.mult).then_inc(s["sc_prod"], 1)
                split_lo(i + (S_SC + 1), 1)
                for r in range(3):
                    for j in (0, 1):
                        if r == 0:
                            dve.wait_ge(s["sc_prod"], 2 * i + (j + 3))
                        convolve(2 * i + j, PA_SC, KD, cb[:, bass.ds((2 * i + j) * WF + KD * WF, LF)], i, j, r, CONV_SC)
            dve.wait_ge(s["conv_step"], CONV_SC + 24)
            for i in range(2):
                n = S_SC + 4 + i
                for j in range(4):
                    m = 4 * i + j
                    if j == 2:
                        split_lo(n + 1, 0)
                    chunk(n, j)
                    if m >= 2:
                        AC.wait(dve, f"sch{m - 2}")
                    y = cb[:, (KD + m) * WF:(KD + m) * WF + WF]
                    tt(hraw[:, m % 2, 0:SEQ], y[:, 0:SEQ], bank[j][:, 0:SEQ], ALU.mult)
                    DV.up(tt(hraw[:, m % 2, SEQ:TOK].rearrange("p (b t) -> p b t", t=NT), padded(y[:, 258:338]),
                             bank[j][:, SEQ:TOK].rearrange("p (b t) -> p b t", t=NT), ALU.mult), f"scp{m}")
                    AC.wait(dve, f"sch{m}")
                    DV.up(tt(hl[:, m, :], hraw[:, m % 2, :], hh[:, m, :], ALU.subtract), f"schl{m}")
                split_lo(n + 1, 1)
            DV.up(dve.memset(spare(1), 0.0), "sc_gated")
            out_proj(S_SCO, 2)
            norm(2, S_UP[1])
            AC.wait(dve, "f1_hist")
            feed_forward(1)
            down(1, 3)
            norm(3, S_END)

        @block.tensor
        def _(pe):
            def mm(out, lhsT, rhs, start=True, stop=True, **kw):
                return pe.matmul(out, lhsT, rhs, start=start, stop=stop, **kw)

            PO.wait(pe, "ident_done")
            PO.wait(pe, "const1")
            pe.wait_ge(s["xtok_in"], 32)
            for k in range(KD):
                if k >= 4:
                    DV.wait(pe, f"xres{k - 4}")
                for t, (at, n) in enumerate(TILES):
                    ins = pe.transpose(bank[k % 4][:, at:at + n], xtok[0:n, t, P * k:P * k + P], ident[0:n, 0:n])
                    if t == 0 and k < CREDIT:
                        ins.then_inc(s["chunk_done"], 1)
                PE.up(ins, f"xT{k}")
            pe.wait_ge(s["params_in"], 16 * 9)
            for i, n in enumerate((PA_N, PB_N, PC_N)):
                ins = pe.transpose(bank[4][:, 128 * i:128 * i + n], prows[0:n, i, :], ident[0:n, 0:n])
            PE.up(ins, "parT")
            pe.wait_ge(s["hist_in"], 16)
            for c in range(12):
                ins = pe.transpose(bank[5][:, 24 * c:24 * c + 24], dnrows[0:24, P * c:P * c + P], ident[0:24, 0:24])
            PE.up(ins, "histT")
            def project(n, xa, xb, nk, free, ready, k0=0, start=True, stop=True, panels=(0, 1)):
                for p in panels:
                    pe.wait_ge(s["lo_done"], 2 * n + (p + 1))
                    for k in range(nk):
                        if p == 0:
                            ready(k0 + k)
                        for j in (2 * p, 2 * p + 1):
                            if start and k == 0:
                                free(j)
                            c = j % 2
                            out = bank[j][:, 0:TOK]
                            w, v = hi[:, p, k, P * c:P * c + P], lo[:, p, k, P * c:P * c + P]
                            mm(out, w, xa[:, k0 + k, :], start and k == 0, False)
                            mm(out, w, xb[:, k0 + k, :], False, False)
                            ins = mm(out, v, xa[:, k0 + k, :], False, stop and k == nk - 1)
                            if k == nk - 1:
                                ins.then_inc(s["chunk_done"], 1)

            def mix_slot(i, **kw):
                project(i, xh, xl, KD, lambda j: pe.wait_ge(s["rel_act"], 4 * i + (j + 1)), lambda k: DV.wait(pe, f"xl{k}"), **kw)

            with pe.Fori(0, 3) as i:
                mix_slot(i)
            pe.wait_ge(s["wba_in"], 48)
            DV.wait(pe, "xres7")
            for t, (at, n) in enumerate(TILES):
                for k in range(KD):
                    ins = mm(bank[7][0:n, 8 * t:8 * t + 8], xres[:, k, at:at + n], wba[:, k, :], k == 0, k == KD - 1)
            PE.up(ins, "ba")

            with pe.Fori(3, 5) as i:
                mix_slot(i)
            AC.wait(pe, "par2")
            AC.wait(pe, "hist")
            PO.wait(pe, "dnlast")
            for g in range(3):
                for c in range(4):
                    ins = pe.transpose(bank[4 + g][0:27, P * c:P * c + P], iof[:, 27 * (4 * g + c):27 * (4 * g + c) + 27],
                                       ident[:, :])
                PE.up(ins, f"dntail{g}")

            def l2_sums(cs):
                for c in cs:
                    AC.wait(pe, f"l2sq{c}")
                    AC.wait(pe, "dntail2" if c < 4 else f"ssln{c - 4}")
                    PE.up(mm(bank[4 + c % 4][:, 0:LD], ones[:, :], l2n[:, c, :]), f"ss{c}")

            mix_slot(5)
            l2_sums(range(8))
            mix_slot(6, panels=(0,))

            def cumulative(t):
                n = TILES[t][1]
                gcb, small = bank[(4, 0, 4)[t] + 2], bank[(4, 0, 4)[t] + 3]
                DV.wait(pe, f"ug{t}")
                if t == 0:
                    AC.wait(pe, "ssln7")
                if t == 1:
                    pe.wait_ge(s["rel_act"], 32)
                if t == 2:
                    DV.wait(pe, "tok0")
                    AC.wait(pe, "decay0")
                mm(gcb[:, 0:H * n], ones[0:n, :], spr[0:n, 0:H * n])
                mm(small[0:n, 0:4], tri(t)[0], gate(G_, t, n))
                if t < 2:
                    ins = mm(small[:, 4:8], ones[0:n, :], gate(G_, t, n))
                else:
                    mm(small[0:n, 4:8], same8[:, :], gate(G_, t, n))
                    ins = mm(small[:, 8:40], ones[0:n, :], rtmp[0:n, 0:32])
                PE.up(ins, f"cum{t}")

            def products(t):
                n = TILES[t][1]
                kkb, qkb = bank[(4, 0, 4)[t]], bank[(4, 0, 4)[t] + 1]
                DV.wait(pe, "qkn")
                for h in range(H):
                    mm(kkb[0:n, n * h:n * h + n], head(4 + h, t), head(4 + h, t))
                for h in range(H):
                    ins = mm(qkb[0:n, n * h:n * h + n], head(4 + h, t), head(h, t))
                PE.up(ins, f"kk{t}")

            def token_major(t):
                n = TILES[t][1]
                kkb, qkb = bank[(4, 0, 4)[t]], bank[(4, 0, 4)[t] + 1]
                DV.wait(pe, f"L{t}")
                DV.wait(pe, f"intra{t}")
                for h in range(H):
                    pe.transpose(kkb[0:n, P * h:P * h + P], head(4 + h, t), ident[:, :])
                for h in range(H):
                    ins = pe.transpose(qkb[0:n, P * h:P * h + P], head(8 + h, t), ident[:, :])
                PE.up(ins, f"tok{t}")

            cumulative(0)
            products(0)
            mix_slot(6, panels=(1,))
            token_major(0)
            cumulative(1)
            products(1)
            cumulative(2)
            token_major(1)
            products(2)
            token_major(2)

            BK = ((0, 1, 2), (3, 4, 5), (6, 7, 7))
            for l in range(7):
                todo = [(n, t) for n, (l_, t) in enumerate(INV) if l_ == l]
                for n, t in todo:
                    sz = TILES[t][1]
                    PO.wait(pe, f"lm{n}")
                    if l == 0:
                        DV.wait(pe, "tok2")
                        AC.wait(pe, "decay2")
                    else:
                        DV.wait(pe, f"inv{INV.index((l - 1, t))}")
                    for h in range(H):
                        ins = mm(bank[BK[t][0]][0:sz, sz * h:sz * h + sz], lmb[n % 2][0:sz, sz * h:sz * h + sz],
                                 ident[0:sz, 0:sz] if l == 0 else TT[t][:, sz * h:sz * h + sz])
                    PE.up(ins, f"invw{n}")
                if l == 0:
                    pe.wait_ge(s["s0_in0"], 64)
                    DV.wait(pe, "qg2")
                    for i in range(32):
                        ins = mm(bank[5][:, 16 * i:16 * i + 16], s0[:, i, :], kq[:, 16 * i:16 * i + 16])
                    PE.up(ins, "ksT")
                if l == 1:
                    AC.wait(pe, "ksTsb")
                    for h in range(H):
                        ins = pe.transpose(bank[5][0:SMP, P * h:P * h + P], kq[:, SMP * h:SMP * h + SMP], ident[:, :])
                    PE.up(ins, "ks2")
                    DV.wait(pe, "rhs2")
                if l:
                    for n, t in todo:
                        sz = TILES[t][1]
                        off = 256 if t == 2 else 0
                        AC.wait(pe, f"wsb{n}")
                        for h in range(H):
                            q = slice(sz * h, sz * h + sz)
                            mm(bank[BK[t][1]][0:sz, q], wsb[t][0:sz, q], T_[t][:, q])
                            ins = mm(bank[BK[t][2]][0:sz, off + sz * h:off + sz * h + sz], T_[t][:, q], wsb[t][0:sz, q])
                        PE.up(ins, f"invu{n}")

            def new_values(t, rhs):
                for h in range(H):
                    q = slice(P * h, P * h + P)
                    ins = mm(bank[0][:, q], TT[t][:, q], rhs[:, q])
                PE.up(ins, f"vn{t}")

            def outputs(t):
                AC.wait(pe, f"vnsb{t}")
                for h in range(H):
                    q = slice(P * h, P * h + P)
                    ins = mm(bank[1][:, q], vnew[:, q], IN[t][:, q], True, t == 0)
                    if t:
                        ins = mm(bank[1][:, q], spr[:, q], qg[:, h, P:2 * P], False, True)
                PE.up(ins, f"o{t}")
                for h in range(H):
                    q = slice(P * h, P * h + P)
                    ins = mm(bank[2][:, q], ktok[:, t, q], vnew[:, q])
                PE.up(ins, f"st{t}")

            def sample_state(h):
                DV.wait(pe, f"vnm{h}")
                if h == 1:
                    DV.wait(pe, "oT2")
                if h >= 2:
                    DV.wait(pe, f"stS{h - 2}")
                bk = 4 if h % 2 else 6
                mm(bank[bk][:, :], ktok[0:SMP, 2, P * h:P * h + P], vnm[h % 2][:, 0:512])
                PE.up(mm(bank[bk + 1][:, :], ktok[0:SMP, 2, P * h:P * h + P], vnm[h % 2][:, 512:1024]), f"stS{h}")

            DV.wait(pe, f"inv{INV.index((6, 0))}")
            new_values(0, vtok[:, 0, :])
            DV.wait(pe, f"inv{INV.index((6, 1))}")
            for h in range(H):
                ins = mm(bank[7][0:SMP, P * h:P * h + P], TT[2][:, SMP * h:SMP * h + SMP], rhsS[:, P * h:P * h + P])
            PE.up(ins, "vn2")
            outputs(0)
            AC.wait(pe, "vnsb2")
            for h in range(H):
                ins = mm(bank[5][:, SMP * h:SMP * h + SMP], vnewS[:, P * h:P * h + P], IN[2][:, SMP * h:SMP * h + SMP])
            PE.up(ins, "o2")
            DV.wait(pe, "state0")
            for h in range(H):
                q = slice(P * h, P * h + P)
                ins = mm(bank[3][:, q], head(4 + h, 1), spr[:, q])
            PE.up(ins, "ks1")
            sample_state(0)
            DV.wait(pe, "rhs1")
            AC.wait(pe, "oT0")
            new_values(1, rtmp[:, :])
            sample_state(1)
            outputs(1)
            sample_state(2)
            sample_state(3)
            for h in range(H):
                AC.wait(pe, f"osq{h}")
                DV.wait(pe, "stS3")
                PE.up(mm(bank[h][:, 0:TOK], ones[:, :], qg[:, h, :]), f"oss{h}")

            def kv_rows(cs):
                for i in cs:
                    at, n = TILES[i % 3]
                    for h in range(H):
                        ins = pe.transpose(bank[4 + i % 3][0:n, P * h:P * h + P], mbh[:, 4 + 4 * (i // 3) + h, at:at + n],
                                           ident[:, :])
                    PE.up(ins, f"kvT{i}")

            def prompt(stage):
                if stage == "kv0":
                    kv_rows(range(3))
                if stage == "scores":
                    AC.wait(pe, "kvtok2")
                    for h in range(H):
                        ins = mm(bank[4][:, P * h:P * h + P], mbh[:, h, 0:P], mbh[:, 4 + h, 0:P])
                    PE.up(ins, "ps0")
                    for h in range(H):
                        ins = mm(bank[5 + h // 2][:, 256 * (h % 2):256 * (h % 2) + 256], mbh[:, h, P:2 * P],
                                 mbh[:, 4 + h, 0:2 * P])
                    PE.up(ins, "ps1")
                if stage == "kv1":
                    DV.wait(pe, "plog1")
                    kv_rows(range(3, 6))
                if stage == "turn":
                    AC.wait(pe, "kvtok5")
                    for g, (x, c0, t) in enumerate(((pl0, 0, 0), (pl1, 0, 1), (pl1, P, 1))):
                        DV.wait(pe, f"pnorm{t}")
                        for h in range(H):
                            ins = pe.transpose(bank[4 + g][:, P * h:P * h + P], x[:, h, c0:c0 + P], ident[:, :])
                        PE.up(ins, f"pT{g}")
                if stage == "values":
                    AC.wait(pe, "pTsb2")
                    for t in range(2):
                        for h in range(H):
                            for c in range(t + 1):
                                ins = mm(bank[4 + t][:, P * h:P * h + P], kvtok[:, 1, c, P * h:P * h + P],
                                         pT[:, 512 * (t + c) + P * h:512 * (t + c) + P * h + P], c == 0, c == t)
                        PE.up(ins, f"po{t}")

            AC.wait(pe, "oln3")
            DV.wait(pe, "rowc")
            PO.wait(pe, "consts")

            def attend(b, c, d, x=0):
                def transpose(u):
                    g, h = divmod(u, H)
                    if h == 0:
                        pe.wait_ge(s[f"k_in{g % 2}"], b * 128 + 64 * (g // 2 + 1))
                    after(pe, "kT_lo", b * UNITS + (u - 1))
                    for j in range(4):
                        ins = pe.transpose(bank[u % 2][:, P * j:P * j + P], kring[:, g % 2, j, P * h:P * h + P], ident[:, :])
                    ins.then_inc(s["kT_mm"], 1)

                def score(u):
                    g, h = divmod(u, H)
                    pe.wait_ge(s["kT_lo"], b * UNITS + (u + 1))
                    if h == 0:
                        after(pe, "s_row", b * 4 + (g - 1))
                    out = bank[2 + g % 2][0:32, :]
                    mm(out, qph[:, x, h, :], kTh[:, u % 2, :], h == 0, False)
                    mm(out, qpl[:, x, h, :], kTh[:, u % 2, :], False, False)
                    mm(out, qph[:, x, h, :], kTl[:, u % 2, :], False, h == H - 1).then_inc(s["s_mm"], 1)

                def turn_probabilities():
                    PO.wait(pe, "ident_done")
                    pe.wait_ge(s["p_norm"], c + 1)
                    for j in range(NPG):
                        pe.transpose(bank[5][:, 32 * j:32 * j + 32], prob[0:32, PAGE * j:PAGE * j + PAGE], ident[0:32, 0:32])
                    pe.transpose(bank[7][0:SMP, 256:288], prob[0:32, PAST:], ident[0:32, 0:32]).then_inc(s["pT_mm"], 1)

                def values(w):
                    if w == 0:
                        after(pe, "o_row", d)
                        pe.wait_ge(s["pT_hi" if whole(d) else "pT_lo"], d + 1)
                    if whole(d):
                        g = w // 2
                        if w % 2 == 0:
                            pe.wait_ge(s[f"v_in{g % 2}"], d * 128 + 64 * (g // 2 + 1))
                        for j in range(2):
                            page = 2 * w + j
                            ins = mm(bank[4][0:32, :], pTf[:, page, :], vring[:, g % 2, page % 4, :], page == 0, False)
                        if w == VUNITS - 1:
                            ins = mm(bank[4][0:32, :], pTf[0:SMP, NPG, :], kvtok[0:SMP, 1, 2, :], False, True)
                        ins.then_inc(s["v_mm"], 1)
                        return
                    pe.wait_ge(s["v_lo"], d * VUNITS + (w + 1))
                    for j in range(2):
                        page = 2 * w + j
                        mm(bank[4][0:64, :], pTs[:, page, :, :].rearrange("p u r -> p (u r)"), vh[:, w % 2, j, :], page == 0,
                           False)
                        ins = mm(bank[4][0:32, :], pTs[:, page, 0, :], vl[:, w % 2, j, :], False, False)
                    if w == VUNITS - 1:
                        mm(bank[4][0:32, :], pTs[0:SMP, NPG, 0, :], vol[:, :], False, False)
                        ins = mm(bank[4][0:64, :], pTs[0:SMP, NPG, :, :].rearrange("p u r -> p (u r)"), voh[:, :], False, True)
                    ins.then_inc(s["v_mm"], 1)

                if b is not None:
                    transpose(0)
                for u in range(UNITS):
                    if b is not None:
                        if u + 1 < UNITS:
                            transpose(u + 1)
                        if u == 0:
                            pe.wait_ge(s["q_lo"], b + 1)
                        if u == 2:
                            after(pe, "pT_lo", b - 1)
                            for h in range(H):
                                mm(bank[7][0:32, 0:SMP], qpf[:, x, h, :], mbh[:, 4 + h, SEQ:TOK], h == 0, h == H - 1)
                        score(u)
                    if c is None and d is None and u in PROMPT:
                        prompt(PROMPT[u])
                    if d is not None and u % 2 == 0:
                        values(u // 2)
                    if c is not None and u == 10:
                        DV.wait(pe, "vol")
                        turn_probabilities()
                if d is not None:
                    pe.wait_ge(s["o_row"], d + 1)
                    for h in range(H):
                        n = 32 if whole(d) else SMP
                        ins = mm(bank[6][:, bass.ds(d * NT + SMP * h, NT)], orow[0:n, P * h:P * h + P],
                                 twice[0:n, NT * h:NT * h + NT])
                    return ins

            attend(0, None, None)
            attend(1, 0, None, 1)
            with pe.Fori(1, NB // 2) as i:
                attend(2 * i, 2 * i - 1, 2 * i - 2)
                attend(2 * i + 1, 2 * i, 2 * i - 1, 1)
            attend(None, NB - 1, NB - 2)
            PE.up(attend(None, None, NB - 1), "attn_mm")

            def stats(n):
                PO.wait(pe, f"accs{n}_{KD - 3}")
                mm(bank[4][:, 0:TOK], onesD[:, :], lnt[:, 0, :], True, False)
                DV.wait(pe, f"r{n}_7")
                for m in (KD - 2, KD - 1):
                    ins = mm(bank[4][:, 0:TOK], onesD[:, :], xres[:, m, :], False, m == KD - 1)
                PE.up(ins, f"mean{n}")
                PO.wait(pe, f"accq{n}_{KD - 3}")
                mm(bank[5][:, 0:TOK], onesD[:, :], lnt[:, 1, :], True, False)
                AC.wait(pe, f"sq{n}_7")
                for m in (KD - 2, KD - 1):
                    ins = mm(bank[5][:, 0:TOK], onesD[:, :], sq[:, m % 2, :], False, m == KD - 1)
                PE.up(ins, f"stat{n}")

            hist_loads = [1]

            def history(name, n):
                hist_loads[0] += 1
                pe.wait_ge(s["hist_in"], 16 * hist_loads[0])
                for c in range(n):
                    ins = pe.transpose(bank[6][:, 16 * c:16 * c + 16], rows[32:48, P * c:P * c + P], ident[32:48, 32:48])
                PE.up(ins, f"{name}_hist")

            def tails(name, n, groups):
                PO.wait(pe, f"{name}_last")
                for g in groups:
                    if g >= 3:
                        AC.wait(pe, f"{name}_tail{g - 3}")
                    for c in range(4 * g, min(n, 4 * g + 4)):
                        ins = pe.transpose(bank[TAIL_BANK[g % 3]][0:18, P * (c % 4):P * (c % 4) + P],
                                           last2[:, 18 * c:18 * c + 18], ident[:, :])
                    PE.up(ins, f"{name}_tail{g}")

            def nothing(_):
                pass

            def feed_forward(layer, n):
                base = S_UP[layer]
                with pe.Fori(0, SLOT_FFN) as i:
                    def free(j):
                        if j < 2:
                            pe.wait_ge(s["rel_act"], 2 * i + (REL[layer] - 2 + j + 1))
                        else:
                            pe.wait_ge(s["h_done"], 2 * i + (KF * layer + j - 2 + 1))
                    project(i + base, xh, xl, KD, free, lambda k: PO.wait(pe, f"x{n - 1}_{k}"))
                pe.wait_ge(s["h_done"], KF * (layer + 1) + 2)
                for i in range(2):
                    for k in range(3):
                        if i == 0 and k:
                            tails(f"f{layer}", KF, range(3 * k - 3, 3 * k))
                        nk = min(KD, KF - KD * k)

                        def free(j):
                            if i:
                                DV.wait(pe, f"r{n}_{j}")
                        project(S_DOWN[layer] + 3 * i + k, hh, hl, nk, free,
                                lambda q: pe.wait_ge(s["hid_ready"], KF * layer + q + 1), KD * k, k == 0, k == 2)
                stats(n)

            def out_proj(base, xa, xb, ready, n, free0, between):
                for i in range(SLOT_OUT):
                    if i:
                        between()
                    project(base + i, xa, xb, KD, free0 if i == 0 else lambda j: DV.wait(pe, f"r{n}_{j}"), ready)
                stats(n)

            DV.wait(pe, "attn_end")
            out_proj(S_OUT, xh, xl, nothing, 0, nothing, lambda: history("f0", KF))
            feed_forward(0, 1)
            history("sc", KD)
            with pe.Fori(0, 4) as i:
                def free(j):
                    if j < 2:
                        pe.wait_ge(s["rel_act"], 2 * i + (REL_SC - 2 + j + 1))
                    else:
                        pe.wait_ge(s["sc_prod"], 2 * i + (j - 2 + 1))
                project(i + S_SC, xh, xl, KD, free, lambda k: PO.wait(pe, f"x1_{k}"))
            for i in range(2):
                def free(j):
                    if i:
                        DV.wait(pe, f"scp{j}")
                    elif j < 2:
                        pe.wait_ge(s["rel_act"], REL_SC + KD)
                    else:
                        pe.wait_ge(s["sc_prod"], KD + 2)
                project(S_SC + 4 + i, xh, xl, KD, free, nothing)
            tails("sc", KD, range(2))
            out_proj(S_SCO, hh, hl, lambda k: DV.wait(pe, f"schl{k}"), 2, lambda j: DV.wait(pe, f"scp{4 + j}"),
                     lambda: history("f1", KF))
            feed_forward(1, 3)
            for i in range(6):
                at, n = TILES[i // 2]
                for c in range(4):
                    m = 4 * (i % 2) + c
                    AC.wait(pe, f"ln3_{m}")
                    ins = pe.transpose(bank[i][0:n, P * c:P * c + P], xres[:, m, at:at + n], ident[:, :])
                PE.up(ins, f"yT{i}")



_INS = ["x_prompt", "x_sample", "cache_k", "cache_v", "state_dn", "state_dn_conv", "state_sc_conv", "state_ffn_conv",
        "page_table", "w_in_mix", "dn_conv_w", "dn_a_log", "dn_dt_bias", "dn_norm_w", "w_out_mix", "w_in_sc", "sc_conv_w",
        "w_out_sc", "ln_mix_g", "ln_mix_b", "w_up", "ffn_conv_w", "w_down", "ln_ffn_g", "ln_ffn_b"]
_OUTS = [("y_p", (1, SEQ, D)), ("y_s", (NB, NT, D)), ("k_p", (1, 1, SEQ, H, HD)), ("v_p", (1, 1, SEQ, H, HD)),
         ("k_s", (1, NB, NT, H, HD)), ("v_s", (1, NB, NT, H, HD)), ("dn_p", (1, 1, H, HD, HD)),
         ("dn_s", (1, NB, H, HD, HD)), ("dnc_p", (1, 1, 3, DNW)), ("dnc_s", (1, NB, 3, DNW)), ("scc_p", (1, 1, 2, D)),
         ("scc_s", (1, NB, 2, D)), ("ffc_p", (2, 1, 2, DFF)), ("ffc_s", (2, NB, 2, DFF))]


def kernel(**inputs):
    import numpy as np
    import concourse.bacc as bacc
    from concourse.bass_utils import run_bass_kernel_spmd as run

    nc = bacc.Bacc("TRN2", target_bir_lowering=False, num_devices=1)
    arrays = {n: np.ascontiguousarray(inputs[n]) for n in _INS}
    a = {n: nc.dram_tensor(n, x.shape, mybir.dt.from_np(x.dtype), kind="ExternalInput").ap() for n, x in arrays.items()}
    o = {n: nc.dram_tensor(n, shape, F32, kind="ExternalOutput").ap() for n, shape in _OUTS}
    trunk_program(nc, a, o)
    r = run(nc, [arrays], core_ids=[0])
    return tuple(r.results[0][n] for n, _ in _OUTS)
```
